# Optimizing a Trainium2 kernel written in Bass

```python
import jax
import jax.numpy as jnp
from jax import lax
import numpy as np

D_MODEL = 1024
BATCH = 1
SEQ = 512
DEPTH = 1
DEC_BATCH = 8
DEC_SEQ = 4
PAST_LEN = 1024
PAGE_SIZE = 128

HEAD_DIM = 64
NSA_WIDTH = 3 * D_MODEL // 4
NSA_HEADS = NSA_WIDTH // HEAD_DIM
NSA_GROUPS = 2
NSA_HPG = NSA_HEADS // NSA_GROUPS
CMP_LEN = 32
CMP_STRIDE = 16
CMP_HID = 64
SLC_BLOCK = 64
N_SELECT = 16
WINDOW = 512
Q_BLOCK = 64
FORCE_SCORE = 1e4
RWKV_WIDTH = 3 * D_MODEL // 4
RWKV_HEAD_DIM = 64
RWKV_HEADS = RWKV_WIDTH // RWKV_HEAD_DIM
DECAY_LORA = 64
ICL_LORA = 64
GATE_LORA = 128
RWKV_SPLITS = (RWKV_WIDTH, RWKV_WIDTH, RWKV_WIDTH, DECAY_LORA, ICL_LORA, GATE_LORA)
RWKV_PROJ = 3 * RWKV_WIDTH + DECAY_LORA + ICL_LORA + GATE_LORA
GN_EPS = 64e-5
MEM_TOKENS = 256
MEM_HEADS = 4
MEM_WIDTH = D_MODEL // 2
MEM_HEAD_DIM = MEM_WIDTH // MEM_HEADS
N_BRANCHES = 3
D_FF = ((-(-8 * D_MODEL // 3) + 255) // 256) * 256
NSA_KV_COLS = 3 * 2 * NSA_GROUPS * HEAD_DIM
IN_SPLITS = (NSA_WIDTH, NSA_KV_COLS, 3 * NSA_HEADS, RWKV_PROJ, MEM_WIDTH, N_BRANCHES * D_MODEL)
IN_COLS = NSA_WIDTH + NSA_KV_COLS + 3 * NSA_HEADS + RWKV_PROJ + MEM_WIDTH + N_BRANCHES * D_MODEL
RMS_EPS = 1e-6

kernel_name = 'nsa_rwkv7_memory_hybrid_step'

def rms_norm(x, g):
    xf = x.astype(jnp.float32)
    y = xf * lax.rsqrt(jnp.mean(xf * xf, axis=-1, keepdims=True) + RMS_EPS)
    return (y * g.astype(jnp.float32)).astype(x.dtype)

def split_cols(z, sizes):
    parts, start = [], 0
    for s in sizes:
        parts.append(z[..., start:start + s])
        start += s
    return parts

def masked_softmax(s, mask):
    s = jnp.where(mask, s.astype(jnp.float32), -1e30)
    return jnp.where(mask, jax.nn.softmax(s, axis=-1), 0.0)

def nsa_kv_rows(kv):
    b, t = kv.shape[:2]
    kv = kv.reshape(b, t, 3, 2, NSA_GROUPS, HEAD_DIM)
    return [kv[:, :, br, j] for br in range(3) for j in range(2)]

def compress_rows(rows, pe, w1, b1, w2):
    b, L, g, hd = rows.shape
    n_chunks = L // CMP_STRIDE
    r = CMP_LEN // CMP_STRIDE
    nc = n_chunks - r + 1
    ch = rows[:, :n_chunks * CMP_STRIDE].reshape(b, n_chunks, CMP_STRIDE, g, hd)
    w1r = w1.reshape(r, CMP_STRIDE, hd, CMP_HID)
    u = jnp.einsum('bncgd,icdh->ibngh', ch, w1r)
    pre = u[0][:, 0:nc]
    for i in range(1, r):
        pre = pre + u[i][:, i:i + nc]
    pre = pre + (pe.reshape(-1) @ w1 + b1)
    return jax.nn.gelu(pre) @ w2

def block_overlap(nc, ns):
    i = jnp.arange(nc, dtype=jnp.int32)[:, None] * CMP_STRIDE
    j = jnp.arange(ns, dtype=jnp.int32)[None, :] * SLC_BLOCK
    return ((i < j + SLC_BLOCK) & (i + CMP_LEN > j)).astype(jnp.float32)

def to_blocks(rows):
    b, L, g, hd = rows.shape
    ns = -(-L // SLC_BLOCK)
    rows = jnp.pad(rows, ((0, 0), (0, ns * SLC_BLOCK - L), (0, 0), (0, 0)))
    return rows.reshape(b, ns, SLC_BLOCK, g, hd).transpose(0, 3, 1, 2, 4)

def nsa_attend(q, t_q, kc, vc, ksb, vsb, kw, vw, t_w, gate):
    b, nq, g, r, hd = q.shape
    nc, ns = kc.shape[1], ksb.shape[2]
    scale = HEAD_DIM ** -0.5
    s_c = jnp.einsum('bqgrd,bngd->bqgrn', q, kc).astype(jnp.float32) * scale
    c_end = jnp.arange(nc, dtype=jnp.int32) * CMP_STRIDE + (CMP_LEN - 1)
    p_c = masked_softmax(s_c, (c_end[None, :] <= t_q[:, None])[None, :, None, None, :])
    o_c = jnp.einsum('bqgrn,bngd->bqgrd', p_c.astype(vc.dtype), vc)
    imp = jnp.einsum('bqgn,ns->bqgs', p_c.sum(axis=3), block_overlap(nc, ns))
    j = jnp.arange(ns, dtype=jnp.int32)[None, :]
    cur = (t_q // SLC_BLOCK)[:, None]
    forced = (j == 0) | (j == cur) | (j == cur - 1)
    score = jnp.where(forced[None, :, None, :], FORCE_SCORE, imp)
    score = jnp.where((j <= cur)[None, :, None, :], score, -jnp.inf)
    top_s, idx = lax.top_k(score, min(N_SELECT, ns))
    b_ix = jnp.arange(b)[:, None, None, None]
    g_ix = jnp.arange(g)[None, None, :, None]
    kb = ksb[b_ix, g_ix, idx]
    vb = vsb[b_ix, g_ix, idx]
    s_s = jnp.einsum('bqgrd,bqgkcd->bqgrkc', q, kb).astype(jnp.float32) * scale
    pos = idx[..., None] * SLC_BLOCK + jnp.arange(SLC_BLOCK, dtype=jnp.int32)
    m_s = (pos <= t_q[None, :, None, None, None]) & jnp.isfinite(top_s)[..., None]
    nk = idx.shape[-1] * SLC_BLOCK
    p_s = masked_softmax(s_s.reshape(b, nq, g, r, nk), m_s.reshape(b, nq, g, 1, nk)).reshape(s_s.shape)
    o_s = jnp.einsum('bqgrkc,bqgkcd->bqgrd', p_s.astype(vb.dtype), vb)
    s_w = jnp.einsum('bqgrd,bkgd->bqgrk', q, kw).astype(jnp.float32) * scale
    diff = t_q[:, None] - t_w[None, :]
    m_w = ((diff >= 0) & (diff <= WINDOW) & (t_w >= 0)[None, :])[None, :, None, None, :]
    p_w = masked_softmax(s_w, m_w)
    o_w = jnp.einsum('bqgrk,bkgd->bqgrd', p_w.astype(vw.dtype), vw)
    gate = gate.astype(q.dtype)
    return gate[..., 0:1] * o_c + gate[..., 1:2] * o_s + gate[..., 2:3] * o_w

def nsa_gates(gn):
    b, t = gn.shape[:2]
    return jax.nn.sigmoid(gn.astype(jnp.float32)).astype(gn.dtype).reshape(b, t, NSA_GROUPS, NSA_HPG, 3)

def nsa_prompt(q, gate, kc, vc, ks_r, vs_r, kw_r, vw_r):
    b, t = q.shape[:2]
    nb = t // Q_BLOCK
    qb = jnp.moveaxis(q.reshape(b, nb, Q_BLOCK, NSA_GROUPS, NSA_HPG, HEAD_DIM), 1, 0)
    gb = jnp.moveaxis(gate.reshape(b, nb, Q_BLOCK, NSA_GROUPS, NSA_HPG, 3), 1, 0)
    starts = jnp.arange(nb, dtype=jnp.int32) * Q_BLOCK
    ksb, vsb = to_blocks(ks_r), to_blocks(vs_r)
    pad = ((0, 0), (WINDOW, 0), (0, 0), (0, 0))
    kw_pad, vw_pad = jnp.pad(kw_r, pad), jnp.pad(vw_r, pad)
    span = Q_BLOCK + WINDOW

    def one_block(args):
        q_blk, g_blk, start = args
        t_q = start + jnp.arange(Q_BLOCK, dtype=jnp.int32)
        t_w = start - WINDOW + jnp.arange(span, dtype=jnp.int32)
        kw = lax.dynamic_slice_in_dim(kw_pad, start, span, axis=1)
        vw = lax.dynamic_slice_in_dim(vw_pad, start, span, axis=1)
        return nsa_attend(q_blk, t_q, kc, vc, ksb, vsb, kw, vw, t_w, g_blk)

    out = lax.map(one_block, (qb, gb, starts))
    return jnp.moveaxis(out, 0, 1).reshape(b, t, NSA_WIDTH)

def rwkv_prep(p, p_prev, mu, w0, w2, a0, a2, g2, k_k, k_a):
    b, t = p.shape[:2]
    prev = jnp.concatenate([p_prev[:, None].astype(p.dtype), p[:, :-1]], axis=1)
    xm = p + (prev - p) * mu
    r, k, v, wd, ad, gd = split_cols(xm, RWKV_SPLITS)
    w = (w0 + jnp.tanh(wd) @ w2).astype(jnp.float32)
    decay = jnp.exp(-jnp.exp(-jax.nn.softplus(-w) - 0.5))
    a = jax.nn.sigmoid(a0 + ad @ a2)
    g = jax.nn.sigmoid(gd) @ g2
    heads = lambda z: z.reshape(b, t, RWKV_HEADS, RWKV_HEAD_DIM)
    kk = heads((k * k_k).astype(jnp.float32))
    kk = kk / jnp.maximum(jnp.sqrt(jnp.sum(kk * kk, axis=-1, keepdims=True)), 1e-12)
    k = k * (1.0 + (a - 1.0) * k_a)
    return heads(r), heads(decay), heads(k), heads(v), kk, heads(a), g

def rwkv_scan(s0, r, decay, k, v, kk, a):
    def step(s, inp):
        r_t, w_t, k_t, v_t, kk_t, a_t = inp
        sa = jnp.einsum('bhij,bhj->bhi', s, -kk_t)
        s = s * w_t[:, :, None, :] + sa[..., None] * (kk_t * a_t)[:, :, None, :] + v_t[..., None] * k_t[:, :, None, :]
        return s, jnp.einsum('bhij,bhj->bhi', s, r_t)
    seq = tuple(jnp.moveaxis(z.astype(jnp.float32), 1, 0) for z in (r, decay, k, v, kk, a))
    s, y = lax.scan(step, s0.astype(jnp.float32), seq)
    return s, jnp.moveaxis(y, 0, 1)

def rwkv_out(y, r, k, v, g, ln_g, ln_b, r_k):
    b, t = y.shape[:2]
    mean = jnp.mean(y, axis=-1, keepdims=True)
    var = jnp.mean(jnp.square(y - mean), axis=-1, keepdims=True)
    yn = (y - mean) * lax.rsqrt(var + GN_EPS)
    bonus = jnp.sum((r * k * r_k).astype(jnp.float32), axis=-1, keepdims=True) * v.astype(jnp.float32)
    out = (yn.reshape(b, t, RWKV_WIDTH) * ln_g + ln_b + bonus.reshape(b, t, RWKV_WIDTH)) * g
    return out.astype(g.dtype)

def mem_kv(mem, g, w):
    b, m = mem.shape[:2]
    k, v = split_cols(rms_norm(mem, g) @ w, (MEM_WIDTH, MEM_WIDTH))
    return k.reshape(b, m, MEM_HEADS, MEM_HEAD_DIM), v.reshape(b, m, MEM_HEADS, MEM_HEAD_DIM)

def mem_attend(q, mk, mv):
    b, t = q.shape[:2]
    qh = q.reshape(b, t, MEM_HEADS, MEM_HEAD_DIM)
    s = jnp.einsum('bthd,bmhd->bthm', qh, mk).astype(jnp.float32) * MEM_HEAD_DIM ** -0.5
    p = jax.nn.softmax(s, axis=-1).astype(mv.dtype)
    return jnp.einsum('bthm,bmhd->bthd', p, mv).reshape(b, t, MEM_WIDTH)

def merge_ffn(x, o_nsa, o_rwkv, o_mem, mg, w_o_nsa, w_o_rwkv, w_o_mem, w_out, ffn_norm, w_gate, w_up, w_down):
    b, t = x.shape[:2]
    g = jax.nn.sigmoid(mg.astype(jnp.float32)).astype(x.dtype).reshape(b, t, N_BRANCHES, D_MODEL)
    m = g[:, :, 0] * (o_nsa @ w_o_nsa) + g[:, :, 1] * (o_rwkv @ w_o_rwkv) + g[:, :, 2] * (o_mem @ w_o_mem)
    x = x + m @ w_out
    hf = rms_norm(x, ffn_norm)
    return x + (jax.nn.silu(hf @ w_gate) * (hf @ w_up)) @ w_down

def gather_pages(pool, page_table):
    rows = pool[page_table]
    b, n, ps = rows.shape[:3]
    return rows.reshape(b, n * ps, rows.shape[3], rows.shape[4])

def setup_inputs(seed: int = 0) -> dict:
    key = jax.random.key(seed)
    ks = list(jax.random.split(key, 80))

    def nrm(shape, scale):
        return jax.random.normal(ks.pop(), shape, jnp.float32) * scale

    n_pages = PAST_LEN // PAGE_SIZE
    n_used = DEC_BATCH * n_pages
    n_phys = n_used + n_used // 4
    lw = min(WINDOW, PAST_LEN)
    paged = (DEPTH, n_phys, PAGE_SIZE, NSA_GROUPS, HEAD_DIM)
    win = (DEPTH, DEC_BATCH, lw, NSA_GROUPS, HEAD_DIM)
    memc = (DEPTH, DEC_BATCH, MEM_TOKENS, MEM_HEADS, MEM_HEAD_DIM)
    perm = jax.random.permutation(ks.pop(), n_phys)
    page_table = perm[:n_used].reshape(DEC_BATCH, n_pages).astype(jnp.int32)
    cl = CMP_LEN * HEAD_DIM
    inp = {
        'x_prompt': nrm((BATCH, SEQ, D_MODEL), 1.0),
        'x_sample': nrm((DEC_BATCH, DEC_SEQ, D_MODEL), 1.0),
        'cache_cmp_k': nrm(paged, 1.0),
        'cache_cmp_v': nrm(paged, 1.0),
        'cache_slc_k': nrm(paged, 1.0),
        'cache_slc_v': nrm(paged, 1.0),
        'cache_win_k': nrm(win, 1.0),
        'cache_win_v': nrm(win, 1.0),
        'state_rwkv_shift': nrm((DEPTH, DEC_BATCH, RWKV_PROJ), 1.0),
        'state_rwkv_wkv': nrm((DEPTH, DEC_BATCH, RWKV_HEADS, RWKV_HEAD_DIM, RWKV_HEAD_DIM), 0.3),
        'cache_mem_k': nrm(memc, 1.0),
        'cache_mem_v': nrm(memc, 1.0),
        'page_table': page_table,
        'mem_prompt': nrm((BATCH, MEM_TOKENS, D_MODEL), 1.0),
        'attn_norm': 1.0 + nrm((DEPTH, D_MODEL), 0.02),
        'w_in': nrm((DEPTH, D_MODEL, IN_COLS), D_MODEL ** -0.5),
        'cmp_pe_k': nrm((DEPTH, CMP_LEN, HEAD_DIM), 0.1),
        'cmp_w1_k': nrm((DEPTH, cl, CMP_HID), cl ** -0.5),
        'cmp_b1_k': nrm((DEPTH, CMP_HID), 0.02),
        'cmp_w2_k': nrm((DEPTH, CMP_HID, HEAD_DIM), 1.5 * CMP_HID ** -0.5),
        'cmp_pe_v': nrm((DEPTH, CMP_LEN, HEAD_DIM), 0.1),
        'cmp_w1_v': nrm((DEPTH, cl, CMP_HID), cl ** -0.5),
        'cmp_b1_v': nrm((DEPTH, CMP_HID), 0.02),
        'cmp_w2_v': nrm((DEPTH, CMP_HID, HEAD_DIM), 1.5 * CMP_HID ** -0.5),
        'rwkv_mu': jax.random.uniform(ks.pop(), (DEPTH, RWKV_PROJ), jnp.float32),
        'rwkv_w0': nrm((DEPTH, RWKV_WIDTH), 0.5),
        'rwkv_w2': nrm((DEPTH, DECAY_LORA, RWKV_WIDTH), 0.1),
        'rwkv_a0': nrm((DEPTH, RWKV_WIDTH), 0.1),
        'rwkv_a2': nrm((DEPTH, ICL_LORA, RWKV_WIDTH), 0.1),
        'rwkv_g2': nrm((DEPTH, GATE_LORA, RWKV_WIDTH), GATE_LORA ** -0.5),
        'rwkv_kk': 0.85 + nrm((DEPTH, RWKV_WIDTH), 0.02),
        'rwkv_ka': 1.0 + nrm((DEPTH, RWKV_WIDTH), 0.02),
        'rwkv_rk': nrm((DEPTH, RWKV_HEADS, RWKV_HEAD_DIM), 0.1),
        'rwkv_ln_g': 1.0 + nrm((DEPTH, RWKV_WIDTH), 0.02),
        'rwkv_ln_b': nrm((DEPTH, RWKV_WIDTH), 0.02),
        'mem_norm': 1.0 + nrm((DEPTH, D_MODEL), 0.02),
        'w_mem_kv': nrm((DEPTH, D_MODEL, 2 * MEM_WIDTH), D_MODEL ** -0.5),
        'w_o_nsa': nrm((DEPTH, NSA_WIDTH, D_MODEL), NSA_WIDTH ** -0.5),
        'w_o_rwkv': nrm((DEPTH, RWKV_WIDTH, D_MODEL), RWKV_WIDTH ** -0.5),
        'w_o_mem': nrm((DEPTH, MEM_WIDTH, D_MODEL), MEM_WIDTH ** -0.5),
        'w_out': nrm((DEPTH, D_MODEL, D_MODEL), D_MODEL ** -0.5),
        'ffn_norm': 1.0 + nrm((DEPTH, D_MODEL), 0.02),
        'w_gate': nrm((DEPTH, D_MODEL, D_FF), D_MODEL ** -0.5),
        'w_up': nrm((DEPTH, D_MODEL, D_FF), D_MODEL ** -0.5),
        'w_down': nrm((DEPTH, D_FF, D_MODEL), D_FF ** -0.5),
        'final_norm': 1.0 + nrm((D_MODEL,), 0.02),
    }
    return inp

def reference(x_prompt, x_sample, cache_cmp_k, cache_cmp_v, cache_slc_k, cache_slc_v, cache_win_k, cache_win_v,
              state_rwkv_shift, state_rwkv_wkv, cache_mem_k, cache_mem_v, page_table, mem_prompt,
              attn_norm, w_in, cmp_pe_k, cmp_w1_k, cmp_b1_k, cmp_w2_k, cmp_pe_v, cmp_w1_v, cmp_b1_v, cmp_w2_v,
              rwkv_mu, rwkv_w0, rwkv_w2, rwkv_a0, rwkv_a2, rwkv_g2, rwkv_kk, rwkv_ka, rwkv_rk, rwkv_ln_g, rwkv_ln_b,
              mem_norm, w_mem_kv, w_o_nsa, w_o_rwkv, w_o_mem, w_out, ffn_norm, w_gate, w_up, w_down, final_norm):
    xp, xs = x_prompt, x_sample
    bp, t = xp.shape[:2]
    bs, tn = xs.shape[:2]
    lw = cache_win_k.shape[2]
    t_new = PAST_LEN + jnp.arange(tn, dtype=jnp.int32)
    t_w_s = PAST_LEN - lw + jnp.arange(lw + tn, dtype=jnp.int32)
    wp0 = max(t - WINDOW, 0)
    P = {n: [] for n in ('ck', 'cv', 'sk', 'sv', 'wk', 'wv', 'sh', 'wkv', 'mk', 'mv')}
    S = {n: [] for n in ('ck', 'cv', 'sk', 'sv', 'wk', 'wv', 'sh', 'wkv')}
    for l in range(DEPTH):
        cmp_k = (cmp_pe_k[l], cmp_w1_k[l], cmp_b1_k[l], cmp_w2_k[l])
        cmp_v = (cmp_pe_v[l], cmp_w1_v[l], cmp_b1_v[l], cmp_w2_v[l])
        rw_p = (rwkv_mu[l], rwkv_w0[l], rwkv_w2[l], rwkv_a0[l], rwkv_a2[l], rwkv_g2[l], rwkv_kk[l], rwkv_ka[l])
        out_p = (w_o_nsa[l], w_o_rwkv[l], w_o_mem[l], w_out[l], ffn_norm[l], w_gate[l], w_up[l], w_down[l])

        hp = rms_norm(xp, attn_norm[l])
        q, kv, gn, pr, mq, mg = split_cols(hp @ w_in[l], IN_SPLITS)
        kc_r, vc_r, ks_r, vs_r, kw_r, vw_r = nsa_kv_rows(kv)
        kc = compress_rows(kc_r, *cmp_k)
        vc = compress_rows(vc_r, *cmp_v)
        o_nsa = nsa_prompt(q, nsa_gates(gn), kc, vc, ks_r, vs_r, kw_r, vw_r)
        r_, w_, k_, v_, kk_, a_, g_ = rwkv_prep(pr, jnp.zeros((bp, RWKV_PROJ), pr.dtype), *rw_p)
        s_p, y_ = rwkv_scan(jnp.zeros((bp, RWKV_HEADS, RWKV_HEAD_DIM, RWKV_HEAD_DIM), jnp.float32),
                            r_, w_, k_, v_, kk_, a_)
        o_rwkv = rwkv_out(y_, r_, k_, v_, g_, rwkv_ln_g[l], rwkv_ln_b[l], rwkv_rk[l])
        mk, mv = mem_kv(mem_prompt, mem_norm[l], w_mem_kv[l])
        o_mem = mem_attend(mq, mk, mv)
        xp = merge_ffn(xp, o_nsa, o_rwkv, o_mem, mg, *out_p)
        for n, a in (('ck', kc_r), ('cv', vc_r), ('sk', ks_r), ('sv', vs_r), ('wk', kw_r[:, wp0:]),
                     ('wv', vw_r[:, wp0:]), ('sh', pr[:, -1]), ('wkv', s_p.astype(xp.dtype)), ('mk', mk), ('mv', mv)):
            P[n].append(a)

        hs = rms_norm(xs, attn_norm[l])
        q, kv, gn, pr, mq, mg = split_cols(hs @ w_in[l], IN_SPLITS)
        kc_n, vc_n, ks_n, vs_n, kw_n, vw_n = nsa_kv_rows(kv)
        kc = compress_rows(jnp.concatenate([gather_pages(cache_cmp_k[l], page_table), kc_n], axis=1), *cmp_k)
        vc = compress_rows(jnp.concatenate([gather_pages(cache_cmp_v[l], page_table), vc_n], axis=1), *cmp_v)
        ksb = to_blocks(jnp.concatenate([gather_pages(cache_slc_k[l], page_table), ks_n], axis=1))
        vsb = to_blocks(jnp.concatenate([gather_pages(cache_slc_v[l], page_table), vs_n], axis=1))
        kw = jnp.concatenate([cache_win_k[l], kw_n], axis=1)
        vw = jnp.concatenate([cache_win_v[l], vw_n], axis=1)
        qh = q.reshape(bs, tn, NSA_GROUPS, NSA_HPG, HEAD_DIM)
        o_nsa = nsa_attend(qh, t_new, kc, vc, ksb, vsb, kw, vw, t_w_s, nsa_gates(gn)).reshape(bs, tn, NSA_WIDTH)
        r_, w_, k_, v_, kk_, a_, g_ = rwkv_prep(pr, state_rwkv_shift[l], *rw_p)
        s_s, y_ = rwkv_scan(state_rwkv_wkv[l], r_, w_, k_, v_, kk_, a_)
        o_rwkv = rwkv_out(y_, r_, k_, v_, g_, rwkv_ln_g[l], rwkv_ln_b[l], rwkv_rk[l])
        o_mem = mem_attend(mq, cache_mem_k[l], cache_mem_v[l])
        xs = merge_ffn(xs, o_nsa, o_rwkv, o_mem, mg, *out_p)
        for n, a in (('ck', kc_n), ('cv', vc_n), ('sk', ks_n), ('sv', vs_n), ('wk', kw[:, tn:]),
                     ('wv', vw[:, tn:]), ('sh', pr[:, -1]), ('wkv', s_s.astype(xs.dtype))):
            S[n].append(a)

    y_prompt = rms_norm(xp, final_norm)
    y_sample = rms_norm(xs, final_norm)
    p_ck, p_cv, p_sk, p_sv = jnp.stack(P['ck']), jnp.stack(P['cv']), jnp.stack(P['sk']), jnp.stack(P['sv'])
    p_wk, p_wv, p_sh, p_wkv = jnp.stack(P['wk']), jnp.stack(P['wv']), jnp.stack(P['sh']), jnp.stack(P['wkv'])
    p_mk, p_mv = jnp.stack(P['mk']), jnp.stack(P['mv'])
    s_ck, s_cv, s_sk, s_sv = jnp.stack(S['ck']), jnp.stack(S['cv']), jnp.stack(S['sk']), jnp.stack(S['sv'])
    s_wk, s_wv, s_sh, s_wkv = jnp.stack(S['wk']), jnp.stack(S['wv']), jnp.stack(S['sh']), jnp.stack(S['wkv'])
    return (y_prompt, y_sample,
            p_ck, p_cv, p_sk, p_sv, p_wk, p_wv, p_sh, p_wkv, p_mk, p_mv,
            s_ck, s_cv, s_sk, s_sv, s_wk, s_wv, s_sh, s_wkv)


_drawn_inputs = setup_inputs


def setup_inputs(seed=0):
    import zlib

    import numpy as np

    out = dict(_drawn_inputs(seed))
    spreads = {}
    factors = {'cache_slc_k': 4.097,
     'cache_slc_v': 3.302,
     'cmp_pe_k': 8.0,
     'cmp_b1_k': 8.0,
     'cmp_b1_v': 24.361,
     'rwkv_kk': 64.0,
     'rwkv_ka': 2.939,
     'rwkv_ln_g': 8.0,
     'rwkv_ln_b': 8.0,
     'mem_norm': 9.083,
     'ffn_norm': 4.042,
     'final_norm': 8.094,
     'cmp_pe_v': 4.511}
    for name, (base, spread) in spreads.items():
        noise = np.random.default_rng([zlib.crc32(name.encode()), seed]).standard_normal(out[name].shape)
        drawn = base * np.exp(spread * noise) if base else spread * noise
        out[name] = jnp.asarray(drawn.astype(out[name].dtype))
    for name, factor in factors.items():
        out[name] = (out[name] * factor).astype(out[name].dtype)
    return out
```

```python
import numpy as np
from contextlib import ExitStack
import concourse.bass as bass
from concourse import mybir

F32 = mybir.dt.float32
I32 = mybir.dt.int32
ALU = mybir.AluOpType
ACT = mybir.ActivationFunctionType
AX = mybir.AxisListType.X

P = 128
D = 1024
KT = D // P
TP, TS = 512, 32
T = TP + TS
HALF_T = T // 2
QT = TP // P
HD = 64
NG, HPG = 2, 6
NB, NQ = 8, 4
MEM_H, MEM_T = 4, 256
PAST, PAGE = 1024, 128
NPG = PAST // PAGE
N_PHYS = NB * NPG * 5 // 4
WIN = 512
CMP = 16
NC_P = TP // CMP - 1
NC_S = PAST // CMP - 1
PAIRS = 6
C = 64
NCH = TP // C
FF = 2816
FFT = FF // P
RMS_EPS = 1e-6
GN_EPS = 64e-5
NEG = -1e30

T_Q, T_KV, T_MQ, N_IN = 0, 6, 12, 16
R_R, R_K, R_V, R_LORA, R_GD, N_RW = 0, 6, 12, 18, 19, 20
T_CK, T_CV, T_SK, T_SV, T_WK, T_WV = range(T_KV, T_KV + 6)

RING = 5
S_IN = 0
S_MEM = S_IN + N_IN
S_RW = S_MEM + KT
S_MG = S_RW + N_RW
S_MERGE = S_MG + 3 * KT
MERGE_K = 6 + 6 + 4
S_OUT = S_MERGE + MERGE_K
S_GU = S_OUT + KT
S_DOWN = S_GU + 2 * FFT
N_SLOTS = S_DOWN + FFT

SEG = {}


def _segments():
    at = 0
    for name, n in (("ident", P), ("causal", P), ("cmpmask", QT * NC_P), ("cmp01", QT * NC_P),
                    ("newmask", 2 * TS), ("winfirst", NQ), ("winnew", 2 * TS), ("headsum", P), ("samequery", P),
                    ("blockno", 14), ("gram_p", 2 * C), ("tri_p", 5 * C), ("x2t_p", C),
                    ("gram_s", 2 * TS), ("tri_s", 1 * TS), ("x2t_s", TS), ("zmask", NB * TS), ("umask", NB),
                    ("reset", T)):
        SEG[name] = (at, at + n)
        at += n
    return at


N_CONST = _segments()


def constants():
    c = np.zeros((P, N_CONST), np.float32)

    def put(name, a):
        lo, hi = SEG[name]
        a = np.asarray(a, np.float32)
        a = a.reshape(a.shape[0], -1)
        assert a.shape[1] == hi - lo, (name, a.shape)
        c[:a.shape[0], lo:hi] = a

    p = np.arange(P)[:, None]
    put("ident", np.eye(P))
    put("causal", np.where(np.arange(P)[None] <= p, 0, NEG))
    ends = np.arange(NC_P) * CMP + 2 * CMP - 1
    seen = ends[None, None] <= (np.arange(QT)[None, :, None] * P + p[:, :, None])
    put("cmpmask", np.where(seen, 0, NEG))
    put("cmp01", seen)
    row_b, row_q, row_real = p // 32, p % 4, (p % 32) < HPG * NQ
    tok = np.arange(TS)[None]
    new = [(tok // NQ == row_b + 4 * half) & (tok % NQ <= row_q) for half in range(2)]
    put("newmask", np.concatenate([np.where(m, 0, NEG) for m in new], 1))
    put("winfirst", np.where(np.arange(NQ)[None] >= row_q, 0, NEG))
    put("winnew", np.concatenate([np.where(m, 0, NEG) for m in new], 1))
    put("headsum", (p // HD) == (np.arange(P)[None] // HD))
    same = (row_b == row_b.T) & (row_q == row_q.T) & row_real & row_real.T
    put("samequery", same)
    put("blockno", np.tile(np.arange(1, 15), (P, 1)))

    def gram(n, allowed):
        s, t = np.arange(n)[:, None], np.arange(n)[None]
        strict, incl = allowed(s, t) & (s < t), allowed(s, t) & (s <= t)
        return np.block([[strict, incl], [strict, incl]])

    def tri(n, allowed, levels):
        t, s = np.arange(n)[:, None], np.arange(n)[None]
        out = []
        for b in levels:
            off = (t // (2 * b) == s // (2 * b)) & ((t // b) % 2 == 1) & ((s // b) % 2 == 0)
            out.append(off & allowed(s, t) | (t == s))
        return np.concatenate(out, 1)

    every = lambda s, t: (s >= 0) & (t >= 0)
    mine = lambda s, t: s // NQ == t // NQ
    put("gram_p", gram(C, every))
    put("tri_p", tri(C, every, (2, 4, 8, 16, 32)))
    put("x2t_p", tri(C, every, (1,)).T)
    put("gram_s", gram(TS, mine))
    put("tri_s", tri(TS, mine, (2,)))
    put("x2t_s", tri(TS, mine, (1,)).T)
    put("zmask", np.tile((np.arange(TS)[None] // NQ == np.arange(NB)[:, None]).reshape(1, -1), (P, 1)))
    put("umask", ((np.arange(2 * TS)[:, None] % TS) // NQ) == np.arange(NB)[None])
    t = np.arange(T)
    put("reset", np.tile(np.where(t < TP, t % C != 0, (t - TP) % NQ != 0), (P, 1)))
    sel = np.zeros((36, HPG, 3, NG, HD), np.float32)
    for g in range(NG):
        for r in range(HPG):
            for br in range(3):
                sel[g * 18 + r * 3 + br, r, br, g] = 1
    return c, np.ascontiguousarray(sel.reshape(36, 18 * P))


def tiles(w, order=None):
    k, m = w.shape
    return w.reshape(k // P, P, m // P, P).transpose(2, 1, 0, 3).reshape(m // P, P, k)


def layout(i):
    f = lambda n: np.asarray(i[n])
    w = f("w_in")[0]
    at = np.cumsum([0, 768, 768, 36, 2560, 512, 3072])
    wq, wkv, wgn, wr, wmq, wmg = (w[:, a:b] for a, b in zip(at[:-1], at[1:]))
    pairs = lambda a: a.reshape(a.shape[0], NG, HPG, HD).transpose(0, 2, 1, 3).reshape(a.shape[0], -1)
    wq = pairs(wq)
    w_nsa = pairs(f("w_o_nsa")[0].T).T
    stream = np.empty((N_SLOTS, P, D), np.float32)
    stream[S_IN:S_MEM] = np.concatenate([tiles(np.ascontiguousarray(a)) for a in (wq, wkv, wmq)])
    stream[S_RW:S_MG] = tiles(np.ascontiguousarray(wr))
    stream[S_MEM:S_RW] = f("w_mem_kv")[0].reshape(KT, P, D)
    mg = tiles(wmg).reshape(3, KT, P, D)
    stream[S_MG:S_MERGE] = mg.transpose(1, 0, 2, 3).reshape(3 * KT, P, D)
    merge = np.concatenate([tiles(w_nsa), tiles(f("w_o_rwkv")[0]), tiles(f("w_o_mem")[0])], axis=2)
    stream[S_MERGE:S_OUT] = merge.reshape(KT, P, MERGE_K // KT, D).transpose(0, 2, 1, 3).reshape(-1, P, D)
    stream[S_OUT:S_GU] = tiles(f("w_out")[0])
    stream[S_GU:S_DOWN] = np.stack([tiles(f("w_gate")[0]), tiles(f("w_up")[0])], 1).reshape(-1, P, D)
    down = tiles(f("w_down")[0]).reshape(KT, P, FFT, P).transpose(0, 2, 1, 3)
    stream[S_DOWN:] = down.reshape(FFT, KT, P, P).transpose(0, 2, 1, 3).reshape(FFT, P, D)
    cols = [f(n).reshape(-1) for n in ("attn_norm", "mem_norm", "ffn_norm", "rwkv_mu", "rwkv_w0", "rwkv_a0",
                                          "rwkv_kk", "rwkv_ka", "rwkv_rk", "rwkv_ln_g", "rwkv_ln_b",
                                       "final_norm")]
    vec = np.concatenate([a.reshape(-1, P).T for a in cols], 1)
    pages = np.stack([f("cache_cmp_k")[0].reshape(N_PHYS, PAGE, P).transpose(0, 2, 1),
                      f("cache_cmp_v")[0].reshape(N_PHYS, PAGE, P).transpose(0, 2, 1),
                      f("cache_slc_k")[0].reshape(N_PHYS, PAGE, P).transpose(0, 2, 1),
                      f("cache_slc_v")[0].reshape(N_PHYS, PAGE, P)], 2)
    w1 = np.stack([f(f"cmp_w1_{n}")[0].reshape(2, CMP, HD, HD).transpose(2, 1, 0, 3) for n in "kv"], 1)
    x = np.concatenate([f("x_prompt")[0], f("x_sample").reshape(TS, D)])
    return {
        "x_all": x,
        "x_T": x.T.reshape(KT, P, T).transpose(1, 0, 2),
        "mem_x": f("mem_prompt")[0],
        "w_stream": stream,
        "w_gates": wgn.reshape(KT, P, 36).transpose(1, 0, 2),
        "vectors": vec,
        "consts": constants()[0],
        "gate_spread": constants()[1],
        "pages": pages,
        "page_table": f("page_table").reshape(1, NB * NPG),
        "win_kT": f("cache_win_k")[0].reshape(NB, WIN, P).transpose(0, 2, 1),
        "win_v": f("cache_win_v")[0].reshape(NB, WIN, P),
        "mem_kT": f("cache_mem_k")[0].transpose(0, 3, 2, 1),
        "mem_v": f("cache_mem_v")[0].reshape(NB, MEM_T, MEM_H * P),
        "shift_in": f("state_rwkv_shift")[0].reshape(NB, 20, P).transpose(2, 1, 0),
        "state_in": f("state_rwkv_wkv")[0].reshape(NB, PAIRS, 2, HD, HD).transpose(2, 4, 0, 1, 3),
        "cmp_w1": w1.reshape(HD, 2, CMP * P),
        "cmp_w1_rows": np.stack([f(f"cmp_w1_{n}")[0].reshape(16, P, HD).transpose(1, 0, 2) for n in "kv"], 1),
        "cmp_pe": np.stack([f(f"cmp_pe_{n}")[0].reshape(16, P).T for n in "kv"], 1),
        "cmp_b1": np.stack([f(f"cmp_b1_{n}")[0] for n in "kv"], 1),
        "cmp_w2": np.stack([f(f"cmp_w2_{n}")[0] for n in "kv"], 1),
        "lora_w": np.concatenate([f("rwkv_w2")[0], f("rwkv_a2")[0]]),
        "lora_g": f("rwkv_g2")[0],
    }


VEC = {}
N_VEC = 0
for _n, _k in (("attn", 8), ("mem", 8), ("ffn", 8), ("mu", 20), ("w0", 6), ("a0", 6), ("kk", 6), ("ka", 6), ("rk", 6),
               ("lng", 6), ("lnb", 6), ("final", 8)):
    VEC[_n] = N_VEC
    N_VEC += _k

OUTS = {
    "yT": (P, KT, T),
    "kvT": (6, P, T),
    "shift_out": (P, 20, 1 + NB),
    "wkv_p": (P, PAIRS, HD),
    "wkv_s": (P, PAIRS, NB, HD),
    "mem_kv": (MEM_T, D),
    "win_kT_out": (NB, P, WIN),
    "win_v_out": (NB, WIN, P),
}


def results(r):
    y = r["yT"].transpose(2, 1, 0).reshape(T, D)
    kv = r["kvT"].transpose(0, 2, 1)
    prompt = [kv[n, :TP].reshape(1, 1, TP, NG, HD) for n in range(6)]
    new = [kv[n, TP:].reshape(1, NB, NQ, NG, HD) for n in range(4)]
    sh = r["shift_out"].transpose(2, 1, 0).reshape(1 + NB, 2560)
    wkv_p = r["wkv_p"].reshape(2, HD, PAIRS, HD).transpose(2, 0, 3, 1).reshape(1, 1, 12, HD, HD)
    wkv_s = r["wkv_s"].reshape(2, HD, PAIRS, NB, HD).transpose(3, 2, 0, 4, 1).reshape(1, NB, 12, HD, HD)
    mkv = r["mem_kv"].reshape(1, 1, MEM_T, 2, MEM_H, P)
    wk = r["win_kT_out"].transpose(0, 2, 1).reshape(1, NB, WIN, NG, HD)
    wv = r["win_v_out"].reshape(1, NB, WIN, NG, HD)
    return (y[:TP].reshape(1, TP, D), y[TP:].reshape(NB, NQ, D), *prompt,
            sh[0].reshape(1, 1, 2560), wkv_p, mkv[:, :, :, 0], mkv[:, :, :, 1], *new,
            wk, wv, sh[1:].reshape(1, NB, 2560), wkv_s)


def bc(ap, axis, n):
    a = ap.unsqueeze(axis)
    shape = list(a.shape)
    shape[axis] = n
    return a.to_broadcast(shape)


class Steps:

    def __init__(self, engine, sem):
        self.engine, self.sem, self.base, self.n, self.it = engine, sem, 0, 0, None

    def loop(self, it, each):
        self.it, self.each, self.start = it, each, self.base + self.n
        self.base, self.n = self.start, 0

    def end(self, times):
        assert self.n == self.each, (self.n, self.each)
        self.base, self.n, self.it = self.start + times * self.each, 0, None

    def __call__(self, instruction):
        instruction.then_inc(self.sem, 1)
        self.n += 1
        at = self.base + self.n
        self.engine.wait_ge(self.sem, at if self.it is None else self.it * self.each + at)


def program(nc, A):
    with ExitStack() as ctx:
        def sb(name, shape, dt=F32):
            return ctx.enter_context(nc.sbuf_tensor("sb_" + name, shape, dt))

        def sem(name):
            return ctx.enter_context(nc.semaphore(name))

        acc = [ctx.enter_context(nc.psum_tensor(f"acc{n}", [P, 2, 512], F32)) for n in range(4)]
        cst = sb("cst", [P, N_CONST])
        vec = sb("vec", [P, N_VEC])
        wgn = sb("wgn", [P, KT, 36])
        ring = sb("ring", [P, RING, D])
        hT = sb("hT", [P, KT, T])
        onsaT = sb("onsaT", [P, HPG, T])
        omemT = sb("omemT", [P, MEM_H, T])
        gates_tm = sb("gates_tm", [P, QT + 1, 36])
        gates_s = sb("gates_s", [36, TS])
        stat = sb("stat", [P, 24])
        work = sb("work", [P, 35200])
        at = [0]

        def region(start, *shape):
            if start is None:
                start = at[0]
            n = int(np.prod(shape))
            at[0] = start + n
            assert at[0] <= 35200, at[0]
            ap = work[:, start:start + n]
            names = "abcd"[:len(shape)]
            if len(shape) == 1:
                return ap
            return ap.rearrange(f"p ({' '.join(names)}) -> p {' '.join(names)}",
                                **dict(zip(names[1:], shape[1:])))

        def const(name, rows=P):
            lo, hi = SEG[name]
            return cst[0:rows, lo:hi]

        def v(name, k, n=1):
            return vec[:, VEC[name] + k:VEC[name] + k + n]

        ident = const("ident")

        qT = region(0, 6, T)
        kvT = region(None, 6, T)
        mqT = region(None, 4, T)
        in_all = region(0, N_IN, T)
        att0 = at[0]
        x_tm = region(att0, 7, D)
        junk = region(None, D)
        memT = region(None, KT, MEM_T)
        mem_tm = region(at[0], 2, D)
        w1 = region(None, 2, CMP, P)
        w1_rows = region(None, 2, 16, HD)
        pe_cols = region(None, 2, 16)
        b1 = region(None, 2)
        w2 = region(None, 2, HD)
        att1 = at[0]
        v_tm = region(att0, 2, QT + 1, P)
        mkT = region(None, MEM_H, MEM_T)
        u_sb = region(None, NG, 2, TS)
        hid = region(None, 2, NG, TS)
        kcT = region(None, TS)
        vc = region(None, P)
        q_now = region(None, TP)
        c_shift = region(None, HPG, NC_P)
        c_prob = region(None, HPG, NC_P)
        c_probT = region(None, HPG, P)
        o_tm = region(None, QT, HPG, P)
        assert at[0] <= att0 + 8 * D
        probs = region(att1, 2, 2, TP)
        rw_now = region(att1, 2, T)
        probsT = region(att1 + 4 * TP, 2, TP)
        m_prob = region(None, MEM_H, MEM_T)
        m_probT = region(None, MEM_H * 2, P)
        small = sb("small", [P, 96])
        pre_bias = small[:, 94:96]
        k_pages = region(att0 + 2 * (QT + 1) * P, 2, NPG, 3, P)
        v_pages = region(None, 4, NPG, P)
        u_s = region(None, NG, 2, HD)
        hid_s = region(None, 2, NG, HD)
        kc_s = region(None, HD)
        assert at[0] <= att0 + 7 * D + D + KT * MEM_T + 2 * D
        win_v = region(att0 + 8 * D + KT * MEM_T + 2 * D + 2 * CMP * P, 4, WIN // P, P)
        win_k = region(att1, 2, WIN)
        W0, WN0, C0, N0, S0 = 0, WIN, WIN + TS, WIN + TS + NC_S, WIN + 2 * TS + NC_S
        scores = region(None, NG, S0 + PAST)
        assert att1 + 2 * WIN + NG * (S0 + PAST) + 15 * P + 4 * P + 18 * TS <= 34656
        sprobT = region(None, 15, P)
        vc_s = region(None, 4, P)
        grep = region(None, 3 * HPG, TS)
        spread = region(att0 + 2 * (QT + 1) * P + 2 * NPG * 3 * P, 3 * HPG, P)
        o_rows = region(34656, 6, HD)
        page_ids = region(None, NB * NPG)[0:1].bitcast(I32)
        q_half = region(att0 + 2 * (QT + 1) * P + 10816, 4, 32)
        imp = wgn[:].rearrange("p k c -> p (k c)")[:, 0:NG * 130].rearrange("p (g n) -> p g n", g=NG)
        o_gated = o_rows.rearrange("p a b -> p (a b)")[:, 0:288].rearrange("p (s x) -> p s x", s=3)
        mem_k = region(att0 + 2 * (QT + 1) * P, 2, MEM_H, MEM_T)
        mem_q = region(None, 4, MEM_H, 32)
        mem_v = region(att0 + 2 * (QT + 1) * P + 2 * NPG * 3 * P, 4, 2, MEM_H * P)
        mem_p = region(att1, MEM_T)
        mem_pT = region(None, 2, P)
        mem_o = region(None, MEM_H * P)

        rwT = region(0, N_RW, T)
        rT, kT, vT = rwT[:, R_R:R_R + PAIRS], rwT[:, R_K:R_K + PAIRS], rwT[:, R_V:R_V + PAIRS]
        zT = region(None, PAIRS, T)
        R_BT = at[0]
        bT = region(None, PAIRS, T)
        gT = region(None, PAIRS, T)
        bonusT = region(None, PAIRS, T)
        scan0 = at[0]
        kkT = region(scan0, PAIRS, T)
        tmp = region(None, 6, T)
        delta = region(None, T)
        gate_now = region(None, 2, T)
        lw_w = region(None, 6 * P)
        lw_g = region(None, 6 * P)
        shift9 = region(None, 20, 1 + NB)
        shift_now = region(None, 20, 1 + NB)
        pend = cst[:, SEG["cmpmask"][0]:SEG["cmpmask"][0] + PAIRS * (NCH + NB)]\
            .rearrange("p (a c) -> p a c", a=PAIRS)
        bk_now = region(scan0, 2, PAIRS, 2 * C)
        zr_now = region(None, 2, PAIRS, 2 * C)
        v_now = region(None, PAIRS, 2 * C)
        gram = region(None, 2, PAIRS, 2 * C)
        X = region(None, 2, PAIRS, C)
        XT = region(None, 2, PAIRS, C)
        Y = region(None, 2, PAIRS, C)
        bk_tm = region(None, PAIRS, P)
        zv = region(None, PAIRS, 2, C)
        uv = region(None, PAIRS, 2, C)
        S = region(None, PAIRS, 2, C)
        y_tm = Y.rearrange("p e a c -> p (e a c)").rearrange("p (a c) -> p a c", a=PAIRS)
        w_tm = y_tm
        S_s = region(0, NB, PAIRS, 2, C)
        S_out = region(None, PAIRS, NB, C)
        uv_b = region(None, 2, NB, C)
        z_b = region(None, 2, NB * TS)
        mT = region(0, KT, T)
        sig_a = region(None, KT // 2, 3, T)
        x1T = region(R_BT, KT, T)
        ffT = region(None, FFT, T)
        sig_b = region(R_BT + KT * T, KT // 2, 3, T)
        at[0] = R_BT + (KT + FFT) * T
        prod = region(None, T)
        sqT = region(None, 2, T)
        rms = region(None, T)
        ones = region(None, P)
        consts_in, x_in = sem("consts_in"), [sem("x_in"), sem("mem_x_in")]
        w_in_slot = [sem(f"w_in_slot{n}") for n in range(RING)]
        slot_used = sem("slot_used")
        dve_own, act_own = sem("dve_own"), sem("act_own")
        pe_passed = sem("pe_passed")
        squares, means, roots, scaled, turned, hT_ready = map(
            sem, ("squares", "means", "roots", "scaled", "turned", "hT_ready"))
        in_evicted = sem("in_evicted")
        gates_mm, gates_done = sem("gates_mm"), sem("gates_done")
        mem_mm, mem_done = sem("mem_mm"), sem("mem_done")
        stored = sem("stored")
        rw_in, rw_evicted, shift_in_sem, shift_taken, shift_stored, xm_done = map(
            sem, ("rw_in", "rw_evicted", "shift_in", "shift_taken", "shift_stored", "xm_done"))
        lo_act, lo_mm, lo_out, kn_sq, kn_mm, kn_max, kn_root, kn_done, ex_in, ex_out, bo_in, bo_mm, prep_done = map(
            sem, ("lo_act", "lo_mm", "lo_out", "kn_sq", "kn_mm", "kn_max", "kn_root", "kn_done", "ex_in", "ex_out",
                  "bo_in", "bo_mm", "prep_done"))
        staged, tb_mm, tv_mm, bk_rows, v_rows, uv_v, gram_mm, gram_out, x_mm, x_out, y_mm, y_out, xt_mm, xt_out = map(
            sem, ("staged", "tb_mm", "tv_mm", "bk_rows", "v_rows", "uv_v", "gram_mm", "gram_out", "x_mm", "x_out",
                  "y_mm", "y_out", "xt_mm", "xt_out"))
        w_mm, w_out, u_mm, u_out, o_mm, o_out, s_mm, s_out, yt_mm, yt_out, s_zero = map(
            sem, ("w_mm", "w_out", "u_mm", "u_out", "o_mm", "o_out", "s_mm", "s_out", "yt_mm", "yt_out", "s_zero"))
        states_in, z_masked, z_used, uvb_done, uvb_used, so_add, wkv_done = map(
            sem, ("states_in", "z_masked", "z_used", "uvb_done", "uvb_used", "so_add", "wkv_done"))
        wkv_stored = sem("wkv_stored")
        gn_mean, gn_diff, gn_max, gn_root, gn_var, gn_sq = kn_mm, kn_sq, kn_max, kn_root, lo_mm, lo_out
        gn_done = sem("gn_done")
        re_back = sem("re_back")
        spilled, sig_in = [sem("spilled0"), sem("spilled1")], [sem("sig_in0"), sem("sig_in1")]
        mg_sig, mg_mm, mg_part, xT_in, x1_added, sqT_made, sqT_summed, rms_in, rms_root, hf_done, gu_act, ff_done, dn_mm = map(
            sem, ("mg_sig", "mg_mm", "mg_part", "xT_in", "x1_added", "sqT_made", "sqT_summed", "rms_in", "rms_root",
                  "hf_done", "gu_act", "ff_done", "dn_mm"))
        ids_in = spread_in = sem("ids_in")
        k_in, v_in = [sem("k_in0"), sem("k_in1")], sem("v_in")
        (su_mm, su_done, sp_mm, sp_done, sk_mm, sk_done, sv_done, ss_a, ss_b, ss_act, ss_dve, sq_done, sg_mm, sg_done) = map(
            sem, ("su_mm", "su_done", "sp_mm", "sp_done", "sk_mm", "sk_done", "sv_done", "ss_a", "ss_b", "ss_act",
                  "ss_dve", "sq_done", "sg_mm", "sg_done"))
        sx_max, sx_exp, si_in, si_mm, st_mm, st_dve, st_act, so_mm, so_done, sf_mm, sf_done = map(
            sem, ("sx_max", "sx_exp", "si_in", "si_mm", "st_mm", "st_dve", "st_act", "so_mm", "so_done", "sf_mm",
                  "sf_done"))
        K_IN, V_IN = 4 * 16 * (NPG + 1), NB * 16 * (NPG + 1)
        ms_q, ms_norm, ms_ft = sem("ms_q"), sem("ms_norm"), sem("ms_ft")
        cmp_in = sem("cmp_in")
        rows_mm, rows_done = sem("rows_mm"), sem("rows_done")
        q_scaled = sem("q_scaled")
        cp_mm, cp_done = sem("cp_mm"), sem("cp_done")
        cs_mm, cs_shift, cs_exp, cs_prob, cs_turn, cs_copied, cs_out, cs_o = map(
            sem, ("cs_mm", "cs_shift", "cs_exp", "cs_prob", "cs_turn", "cs_copied", "cs_out", "cs_o"))
        at_q, at_s, at_max, at_exp, at_turn, at_cs, at_cw, at_pv, at_o = map(
            sem, ("at_q", "at_s", "at_max", "at_exp", "at_turn", "at_cs", "at_cw", "at_pv", "at_o"))
        ot_mm, ot_done = sem("ot_mm"), sem("ot_done")
        ma_s, ma_max, ma_exp, ma_prob, ma_turn, ma_copied, ma_pv, ma_done = (
            cs_mm, cs_shift, cs_exp, cs_prob, cs_turn, cs_copied, cs_out, cs_o)
        mk_in, mv_in = k_in, v_in
        ms_s, ms_max, ms_exp, ms_turn, ms_copied, ms_pv, ms_done = (
            cs_mm, cs_shift, cs_exp, cs_turn, cs_copied, cs_out, cs_o)
        MA, MS = NG * QT, NG * QT + QT
        n_stored = [0]
        rw_early = nc.dram_tensor("rwkv_features", (P, 12, T), F32, kind="Internal").ap()
        gates_out = nc.dram_tensor("branch_gates", (KT, P, 3, T), F32, kind="Internal").ap()

        kv_stored, mem_stored, win_stored = sem("kv_stored"), sem("mem_stored"), sem("win_stored")

        def store(instruction):
            instruction.then_inc(stored, 16)
            n_stored[0] += 16

        block = ctx.enter_context(nc.Block())

        RW_EARLY = 12
        GATES_FIRST = 9
        CMP_UNITS = [(g, t) for g in range(NG) for t in range(QT)]
        ATT_UNITS = [(g, t) for t in range(QT) for g in range(NG)]

        @block.sync
        def _(sp):
            def load(n, s, wait=None):
                if wait is not None:
                    sp.wait_ge(slot_used, wait)
                sp.dma_start(ring[:, s, :], A["w_stream"][n]).then_inc(w_in_slot[s], 16)

            def stream(first, last):
                n = first
                while n < last and n % RING:
                    load(n, n % RING, n - RING + 1 if n >= RING else None)
                    n += 1
                rounds = (last - n) // RING
                if n == 0 and rounds:
                    for s in range(RING):
                        load(s, s)
                    n, rounds = RING, rounds - 1
                if rounds > 0:
                    with sp.Fori(n // RING, n // RING + rounds) as i:
                        for s in range(RING):
                            sp.wait_ge(slot_used, (i - 1) * RING + s + 1)
                            sp.dma_start(ring[:, s, :], A["w_stream"][bass.ds(i * RING + s, 1)]
                                         .rearrange("a p c -> p (a c)")).then_inc(w_in_slot[s], 16)
                    n += rounds * RING
                for n in range(n, last):
                    load(n, n % RING, n - RING + 1)

            sp.dma_start(page_ids, A["page_table"]).then_inc(ids_in, 16)
            stream(0, min(N_SLOTS, S_RW + RW_EARLY + RING))
            sp.wait_ge(ids_in, 16)
            sp.wait_ge(mem_stored, 16)
            sp.wait_ge(ma_done, MA + QT)
            sp.dma_start(spread[0:36], A["gate_spread"].rearrange("p (a c) -> p a c", c=P)).then_inc(spread_in, 16)
            sp.wait_ge(sg_mm, 1)
            with sp.Fori(0, 2) as half:
                for b in range(4):
                    if b >= 2:
                        sp.wait_ge(ss_b, half * 4 + b - 1)
                    else:
                        sp.wait_ge(ss_b, half * 4)
                    sp.dma_start(win_k[:, b % 2, :], A["win_kT"][bass.ds(half * 4 + b, 1)]
                                 .rearrange("a p c -> p (a c)")).then_inc(k_in[b % 2], 16)
                    with sp.Fori(0, NPG) as n:
                        page = sp.value_load(page_ids[0:1, bass.ds((half * 4 + b) * NPG + n, 1)], min_val=0,
                                             max_val=N_PHYS - 1)
                        sp.dma_start(k_pages[:, b % 2, bass.ds(n, 1)].rearrange("p a k c -> p (a k) c"),
                                     A["pages"][bass.ds(page, 1), :, 0:3, :].rearrange("a p k c -> p (a k) c"))\
                          .then_inc(k_in[b % 2], 16)
                sp.wait_ge(so_mm, half * 2)
                for b in range(4):
                    sp.dma_start(win_v[:, b], A["win_v"][bass.ds(half * 4 + b, 1)]
                                 .rearrange("a (k p) c -> p (a k) c", p=P)).then_inc(v_in, 16)
                    with sp.Fori(0, NPG) as n:
                        page = sp.value_load(page_ids[0:1, bass.ds((half * 4 + b) * NPG + n, 1)], min_val=0,
                                             max_val=N_PHYS - 1)
                        sp.dma_start(v_pages[:, b, bass.ds(n, 1)].rearrange("p a c -> p (a c)"),
                                     A["pages"][bass.ds(page, 1), :, 3, :].rearrange("a p c -> p (a c)"))\
                          .then_inc(v_in, 16)
            with sp.Fori(0, 2) as half:
                sp.wait_ge(sf_done, 2)
                sp.wait_ge(ms_pv, MS + half)
                for b in range(4):
                    if b >= 2:
                        sp.wait_ge(ms_s, MS + half * 4 + b - 1)
                    else:
                        sp.wait_ge(ms_s, MS + half * 4)
                    sp.dma_start(mem_k[:, b % 2], A["mem_kT"][bass.ds(half * 4 + b, 1)]
                                 .rearrange("a p h c -> p (a h) c")).then_inc(mk_in[b % 2], 16)
                    sp.dma_start(mem_v[:, b], A["mem_v"][bass.ds(half * 4 + b, 1)]
                                 .rearrange("a (k p) c -> p (a k) c", p=P)).then_inc(mv_in, 16)
            stream(S_RW + RW_EARLY + RING, N_SLOTS)

        @block.gpsimd
        def _(pool):
            pool.dma_start(cst[:], A["consts"]).then_inc(consts_in, 16)
            pool.dma_start(vec[:], A["vectors"]).then_inc(consts_in, 16)
            pool.dma_start(wgn[:], A["w_gates"]).then_inc(consts_in, 16)
            for g in range(2):
                pool.dma_start(w1[g * HD:(g + 1) * HD].rearrange("p a c h -> p a (c h)"), A["cmp_w1"]).then_inc(cmp_in, 16)
            pool.dma_start(w1_rows, A["cmp_w1_rows"]).then_inc(cmp_in, 16)
            pool.dma_start(pe_cols, A["cmp_pe"]).then_inc(cmp_in, 16)
            pool.dma_start(b1[0:HD], A["cmp_b1"]).then_inc(cmp_in, 16)
            pool.dma_start(w2[0:HD], A["cmp_w2"]).then_inc(cmp_in, 16)
            pool.wait_ge(in_evicted, N_IN + 2)
            pool.dma_start(A["kvT"].rearrange("n p t -> p n t"), kvT).then_inc(kv_stored, 16)
            pool.wait_ge(mem_done, 2)
            pool.dma_start(A["mem_kv"].rearrange("(n p) d -> p n d", p=P), mem_tm).then_inc(mem_stored, 16)
            store(pool.dma_start(A["win_kT_out"][:, :, 0:WIN - NQ], A["win_kT"][:, :, NQ:WIN]))
            store(pool.dma_start(A["win_v_out"][:, 0:WIN - NQ, :], A["win_v"][:, NQ:WIN, :]))
            pool.wait_ge(rows_done, 2)
            pool.dma_start(A["win_kT_out"][:, :, WIN - NQ:WIN].rearrange("b p q -> p b q"),
                           in_all[:, T_WK, TP:T].rearrange("p (b q) -> p b q", q=NQ)).then_inc(win_stored, 16)
            for b in range(NB):
                pool.dma_start(A["win_v_out"][b, WIN - NQ:WIN, :], v_tm[b * NQ:(b + 1) * NQ, 1, QT, :])\
                    .then_inc(win_stored, 16)
            pool.wait_ge(win_stored, 16 * (NB + 1))
            pool.wait_ge(kv_stored, 16)
            pool.wait_ge(mem_stored, 16)
            for n in range(RW_EARLY):
                pool.wait_ge(rw_evicted, n + 1)
                pool.dma_start(rw_early[:, n, :], rw_now[:, n % 2, :]).then_inc(spilled[n % 2], 16)
            pool.wait_ge(sf_done, 2)
            pool.wait_ge(ms_done, MS + 2)
            pool.memset(shift9[:, :, 0], 0.0).then_inc(shift_in_sem, 1)
            for n in range(2):
                pool.wait_ge(spilled[n], 16 * RW_EARLY // 2)
            pool.dma_start(rwT[:, 0:RW_EARLY], rw_early).then_inc(re_back, 16)
            pool.dma_start(lw_w, A["lora_w"]).then_inc(rw_in, 16)
            pool.dma_start(lw_g, A["lora_g"]).then_inc(rw_in, 16)
            pool.dma_start(shift9[:, :, 1:], A["shift_in"]).then_inc(rw_in, 16)
            pool.wait_ge(shift_taken, 1)
            pool.dma_start(A["shift_out"], shift_now).then_inc(shift_stored, 16)
            pool.wait_ge(shift_stored, 16)
            for n in range(3 * KT):
                pool.wait_ge(mg_sig, n + 1)
                pool.dma_start(gates_out[n // 3, :, n % 3, :], gate_now[:, n % 2, :]).then_inc(spilled[n % 2], 16)
            for n in range(2):
                pool.wait_ge(spilled[n], 16 * (RW_EARLY + 3 * KT) // 2)
            pool.wait_ge(prep_done, PAIRS)
            pool.memset(v_now[:, :, 0:C], 0.0)

            def stage(c, par, t0, n):
                pool.wait_ge(o_mm, c)
                pool.wait_ge(tv_mm, c)
                d = lambda a: a.rearrange("p a (x n) -> p a x n", x=2)
                bk, zr = (d(x[:, par, :, 0:2 * n]) for x in (bk_now, zr_now))
                for dst, src in ((bk[:, :, 0, :], bT), (bk[:, :, 1, :], kT), (zr[:, :, 0, :], zT), (zr[:, :, 1, :], rT),
                                 (v_now[:, :, n:2 * n], vT)):
                    ins = pool.tensor_copy(dst, src[:, :, bass.ds(t0, n)])
                ins.then_inc(staged, 1)

            with pool.Fori(0, NCH // 2) as it:
                for par in range(2):
                    stage(it * 2 + par, par, (it * 2 + par) * C, C)
            pool.wait_ge(tv_mm, NCH)
            pool.memset(v_now[:, :, 0:TS], 0.0)
            stage(NCH, 0, TP, TS)
            pool.wait_ge(yt_out, NCH)
            pool.wait_ge(staged, NCH + 1)
            pool.memset(S_s, 0.0).then_inc(s_zero, 1)
            pool.wait_ge(s_zero, 2)
            for e in range(2):
                pool.dma_start(S_s[e * HD:(e + 1) * HD, :, :, e, :].rearrange("p b a c -> p (b a) c"),
                               A["state_in"][e].rearrange("p b a c -> p (b a) c")).then_inc(states_in, 16)
            pool.wait_ge(s_out, NCH)
            pool.dma_start(A["wkv_p"][0:HD], S[0:HD, :, 0, :]).then_inc(wkv_stored, 16)
            pool.dma_start(A["wkv_p"][HD:P], S[HD:P, :, 1, :]).then_inc(wkv_stored, 16)
            pool.wait_ge(wkv_done, 2 * PAIRS)
            pool.dma_start(A["wkv_s"], S_out).then_inc(wkv_stored, 16)
            pool.wait_ge(wkv_stored, 48)
            pool.wait_ge(wkv_stored, 48)
            pool.dma_start(sig_a, gates_out[0:KT // 2].rearrange("m p g t -> p m g t")).then_inc(sig_in[0], 16)
            pool.wait_ge(gn_done, PAIRS)
            pool.dma_start(sig_b, gates_out[KT // 2:].rearrange("m p g t -> p m g t")).then_inc(sig_in[1], 16)
            pool.dma_start(x1T, A["x_T"]).then_inc(xT_in, 16)
            for j in range(KT):
                pool.wait_ge(hf_done, KT + j + 1)
                store(pool.dma_start(A["yT"][:, j, :], x1T[:, j, :]))
            pool.wait_ge(stored, n_stored[0])

        NORM = [(P, n * P, hT, "attn") for n in range(QT)] + [(TS, TP, hT, "attn")] + \
               [(P, n * P, memT, "mem") for n in range(2)]

        @block.tensor
        def _(pe):
            def weights(slot, it=None, each=0):
                s, count = slot % RING, 16 * (slot // RING + 1)
                assert each % RING == 0
                pe.wait_ge(w_in_slot[s], count if it is None else it * (16 * each // RING) + count)
                return ring[:, s, :].rearrange("p (k c) -> p k c", k=KT)

            def settle():
                pe.sem_inc(pe_passed, 1)

            pe.wait_ge(consts_in, 48)
            for i, (rows, t0, dst, gain) in enumerate(NORM):
                pe.wait_ge(scaled, i + 1)
                if i >= 2:
                    pe.wait_ge(hT_ready, i - 1)
                o = acc[i % 2][:].rearrange("p a (k t) -> p (a k) t", t=P)
                for k in range(KT):
                    mm = pe.transpose(o[:, k, 0:rows], x_tm[0:rows, i, k * P:(k + 1) * P], ident[0:rows, 0:rows])
                mm.then_inc(turned, 1)

            pe.wait_ge(hT_ready, 7)
            for n in range(QT):
                for k in range(KT):
                    pe.matmul(acc[2][:, 0, 36 * n:36 * n + 36], hT[:, k, n * P:(n + 1) * P], wgn[:, k, :],
                              start=k == 0, stop=k == KT - 1)
            for k in range(KT):
                mm = pe.matmul(acc[2][0:36, 1, 0:TS], wgn[:, k, :], hT[:, k, TP:T], start=k == 0, stop=k == KT - 1)
            mm.then_inc(gates_mm, 1)

            def in_tile(n, it=None, each=0):
                w = weights(S_IN + n, it, each)
                pe.wait_ge(in_evicted, n + 1 if it is None else it * each + n + 1)
                o = acc[n % 2]
                for k in range(KT):
                    for b in range(2):
                        mm = pe.matmul(o[:, b, 0:HALF_T], w[:, k, :], hT[:, k, b * HALF_T:(b + 1) * HALF_T],
                                       start=k == 0, stop=k == KT - 1)
                mm.then_inc(slot_used, 1)

            for n in range(N_IN):
                in_tile(n)
            pe.wait_ge(in_evicted, N_IN + 2)
            pe.wait_ge(gates_done, 2)
            for k in range(KT):
                w = weights(S_MEM + k)
                for n in range(2):
                    for h in range(2):
                        mm = pe.matmul(acc[n][:, h, :], memT[:, k, n * P:(n + 1) * P],
                                       w[:, 4 * h:4 * h + 4, :].rearrange("p a c -> p (a c)"),
                                       start=k == 0, stop=k == KT - 1)
                mm.then_inc(slot_used, 1)

            pe.wait_ge(mem_done, 2)
            for n, tile in enumerate((T_SV, T_WV)):
                for t in range(QT + 1):
                    rows = P if t < QT else TS
                    mm = pe.transpose(acc[2 + n][0:rows, t // QT, t % QT * P:t % QT * P + P],
                                      in_all[:, tile, t * P:t * P + rows], ident)
            mm.then_inc(rows_mm, 1)
            for h in range(MEM_H):
                for n in range(2):
                    mm = pe.transpose(acc[0][:, h // 2, (h % 2 * 2 + n) * P:(h % 2 * 2 + n + 1) * P],
                                      mem_tm[:, n, h * P:(h + 1) * P], ident)
            mm.then_inc(rows_mm, 1)

            pe.wait_ge(cmp_in, 96)
            for kind in range(2):
                for n in range(16):
                    mm = pe.matmul(acc[1][0:HD, 0, kind:kind + 1], w1_rows[:, kind, n, :], pe_cols[:, kind, n:n + 1],
                                   start=n == 0, stop=n == 15)
            mm.then_inc(cp_mm, 1)
            pe.wait_ge(rows_done, 2)
            for g in range(NG):
                for kind, tile in enumerate((T_CK, T_CV)):
                    for c in range(CMP):
                        mm = pe.matmul(acc[2][:, g, kind * TS:(kind + 1) * TS], w1[g * HD:(g + 1) * HD, kind, c, :],
                                       in_all[g * HD:(g + 1) * HD, tile, c:TP:CMP], start=c == 0, stop=c == CMP - 1)
            mm.then_inc(cp_mm, 1)
            pe.wait_ge(cp_done, 2)
            for kind in range(2):
                for g in range(NG):
                    o = acc[3][0:HD, 0, (kind * 2 + g) * TS:(kind * 2 + g) * TS + NC_P]
                    pe.matmul(o, ident[:, 0:HD], u_sb[:, g, kind, 0:NC_P], start=True, stop=False)
                    mm = pe.matmul(o, ident[:, HD:P], u_sb[:, g, kind, 1:NC_P + 1], start=False, stop=True)
            mm.then_inc(cp_mm, 1)
            pe.wait_ge(cp_done, 4)
            for g in range(NG):
                mm = pe.matmul(acc[2][g * HD:(g + 1) * HD, 0, 0:NC_P], w2[0:HD, 0, :], hid[0:HD, 0, g, 0:NC_P],
                               start=True, stop=True)
            for g in range(NG):
                mm = pe.matmul(acc[2][0:NC_P, 1, g * HD:(g + 1) * HD], hid[0:HD, 1, g, 0:NC_P], w2[0:HD, 1, :],
                               start=True, stop=True)
            mm.then_inc(cp_mm, 1)

            early = [0]

            def rw_tile():
                n = early[0]
                early[0] += 1
                w = weights(S_RW + n)
                if n:
                    pe.wait_ge(rw_evicted, n)
                for k in range(KT):
                    for b in range(2):
                        mm = pe.matmul(acc[3][:, b, 0:HALF_T], w[:, k, :], hT[:, k, b * HALF_T:(b + 1) * HALF_T],
                                       start=k == 0, stop=k == KT - 1)
                mm.then_inc(slot_used, 1)

            pe.wait_ge(q_scaled, 1)
            pe.wait_ge(cp_done, 6)
            for u, (g, t) in enumerate(CMP_UNITS):
                gs = slice(g * HD, (g + 1) * HD)
                if u >= 1:
                    pe.wait_ge(cs_shift, u)
                o = acc[0][:, 0, 0:HPG * NC_P].rearrange("p (r n) -> p r n", r=HPG)
                pe.matmul(o, ident, bc(const("cmpmask")[:, t * NC_P:(t + 1) * NC_P], 1, HPG), start=True, stop=False)
                for r in range(HPG):
                    mm = pe.matmul(o[:, r, :], qT[gs, r, t * P:(t + 1) * P], kcT[gs, 0:NC_P],
                                   start=False, stop=r == HPG - 1)
                mm.then_inc(cs_mm, 1)
                rw_tile()
                pe.wait_ge(cs_prob, u + 1)
                if u >= 1:
                    pe.wait_ge(cs_copied, u)
                o = acc[1][0:NC_P].rearrange("p a (r t) -> p (a r) t", t=P)
                for r in range(HPG):
                    mm = pe.transpose(o[:, r, :], c_prob[:, r, :], ident)
                mm.then_inc(cs_turn, 1)
                if u % 2:
                    rw_tile()
                pe.wait_ge(cs_copied, u + 1)
                if u >= 1:
                    pe.wait_ge(cs_o, u)
                for r in range(HPG):
                    mm = pe.matmul(acc[2][:, 0, r * HD:(r + 1) * HD], c_probT[0:NC_P, r, :], vc[0:NC_P, gs],
                                   start=True, stop=True)
                mm.then_inc(cs_out, 1)

            def att_scores(it, u):
                g, t = ATT_UNITS[u]
                gs, w = slice(g * HD, (g + 1) * HD), (t + 1) * P
                pe.wait_ge(at_exp, it * 8 + u + 1)
                for b, tile in enumerate((T_SK, T_WK)):
                    o = acc[u % 2][:, b, :]
                    pe.matmul(o[:, 0:w], q_now[gs, t * P:(t + 1) * P], in_all[gs, tile, 0:w], start=True, stop=False)
                    mm = pe.matmul(o[:, t * P:w], ident, const("causal"), start=False, stop=True)
                mm.then_inc(at_s, 1)

            def att_turn(it, u):
                g, t = ATT_UNITS[u]
                pe.wait_ge(at_exp, it * 8 + u + 3)
                pe.wait_ge(at_cs, it * 8 + u + 1)
                pe.wait_ge(at_cw, it * 8 + u + 1)
                for b in range(2):
                    for k in range(t + 1):
                        mm = pe.transpose(acc[2][:, b, k * P:(k + 1) * P], probs[:, u % 2, b, k * P:(k + 1) * P], ident)
                mm.then_inc(at_turn, 1)

            def att_values(it, u):
                g, t = ATT_UNITS[u]
                pe.wait_ge(at_cs, it * 8 + u + 2)
                pe.wait_ge(at_cw, it * 8 + u + 2)
                pe.wait_ge(at_o, it * 8 + u + 1)
                for b in range(2):
                    for k in range(t + 1):
                        mm = pe.matmul(acc[3][:, u % 2, b * HD:(b + 1) * HD], probsT[:, b, k * P:(k + 1) * P],
                                       v_tm[:, b, k, g * HD:(g + 1) * HD], start=k == 0, stop=k == t)
                mm.then_inc(at_pv, 1)

            pe.wait_ge(cs_o, len(CMP_UNITS))
            pe.wait_ge(rw_evicted, RW_EARLY)
            with pe.Fori(0, HPG) as it:
                pe.wait_ge(at_q, it + 1)
                for u in range(8):
                    att_scores(it, u)
                    if u >= 2:
                        att_values(it, u - 2)
                    if u >= 1:
                        att_turn(it, u - 1)
                att_values(it, 6)
                att_turn(it, 7)
                att_values(it, 7)

            for r in range(HPG):
                if r == 0:
                    pe.wait_ge(at_o, 2 + 8 * HPG)
                else:
                    pe.wait_ge(ot_done, r)
                for t in range(QT):
                    mm = pe.transpose(acc[0][:, r % 2, t * P:(t + 1) * P], o_tm[:, t, r, :], ident)
                mm.then_inc(ot_mm, 1)
            pe.wait_ge(ot_done, HPG)
            for t in range(QT):
                if t >= 1:
                    pe.wait_ge(ma_exp, MA + t)
                for h in range(MEM_H):
                    mm = pe.matmul(acc[0][:, h // 2, h % 2 * MEM_T:(h % 2 + 1) * MEM_T],
                                   mqT[:, h, t * P:(t + 1) * P], mkT[:, h, :], start=True, stop=True)
                mm.then_inc(ma_s, 1)
                pe.wait_ge(ma_prob, MA + t + 1)
                if t >= 1:
                    pe.wait_ge(ma_copied, MA + t)
                for h in range(MEM_H):
                    for n in range(2):
                        mm = pe.transpose(acc[1][:, h // 2, (h % 2 * 2 + n) * P:(h % 2 * 2 + n + 1) * P],
                                          m_prob[:, h, n * P:(n + 1) * P], ident)
                mm.then_inc(ma_turn, 1)
                pe.wait_ge(ma_copied, MA + t + 1)
                if t >= 1:
                    pe.wait_ge(ma_done, MA + t)
                for h in range(MEM_H):
                    for n in range(2):
                        mm = pe.matmul(acc[2][:, 0, h * P:(h + 1) * P], mem_tm[:, n, TP + h * P:TP + (h + 1) * P],
                                       m_probT[:, h * 2 + n, :], start=n == 0, stop=n == 1)
                mm.then_inc(ma_pv, 1)

            pe.wait_ge(spread_in, 32)
            pe.wait_ge(ma_done, MA + QT)
            o = acc[0][:].rearrange("p a (n t) -> p (a n) t", t=TS)
            for n in range(3 * HPG):
                mm = pe.matmul(o[:, n, :], spread[0:36, n, :], gates_s[:], start=True, stop=True)
            mm.then_inc(sg_mm, 1)
            pe.wait_ge(sg_done, 1)
            with pe.Fori(0, 2) as half:
                pe.wait_ge(sq_done, half + 1)
                for b in range(4):
                    n = half * 4 + b
                    kp, rows = k_pages[:, b % 2], slice(b * 32, (b + 1) * 32)
                    pe.wait_ge(k_in[b % 2], half * (2 * 16 * 9) + (b // 2 + 1) * 16 * 9)
                    pe.wait_ge(so_done, half)
                    pe.wait_ge(ss_dve, n)
                    settle()
                    for g in range(NG):
                        for kind in range(2):
                            for c in range(CMP):
                                mm = pe.matmul(acc[2][:, g, kind * HD:(kind + 1) * HD], w1[g * HD:(g + 1) * HD, kind, c, :],
                                               kp[g * HD:(g + 1) * HD, :, kind, c:P:CMP], start=c == 0, stop=c == CMP - 1)
                    mm.then_inc(su_mm, 1)
                    pe.wait_ge(ss_act, n)
                    pe.wait_ge(st_act, half * 2)
                    pe.wait_ge(st_dve, half * 2)
                    settle()
                    for g in range(NG):
                        gs = slice(g * HD, (g + 1) * HD)
                        for j in range(2):
                            mm = pe.matmul(acc[g][rows, j, :], q_half[gs, b, :], kp[gs, 4 * j:4 * j + 4, 2, :],
                                           start=True, stop=True)
                    mm.then_inc(ss_a, 1)
                    pe.wait_ge(su_done, n + 1)
                    pe.wait_ge(sf_done, half)
                    for kind in range(2):
                        for g in range(NG):
                            o = acc[3][0:HD, 0, (kind * 2 + g) * HD:(kind * 2 + g) * HD + NC_S]
                            pe.matmul(o, ident[:, 0:HD], u_s[:, g, kind, 0:NC_S], start=True, stop=False)
                            mm = pe.matmul(o, ident[:, HD:P], u_s[:, g, kind, 1:NC_S + 1], start=False, stop=True)
                    mm.then_inc(sp_mm, 1)
                    for g in range(NG):
                        gs = slice(g * HD, (g + 1) * HD)
                        pe.matmul(acc[2][rows, g, :], q_half[gs, b, :], win_k[gs, b % 2, :], start=True, stop=True)
                    pe.wait_ge(sp_done, n + 1)
                    settle()
                    for g in range(NG):
                        mm = pe.matmul(acc[3][g * HD:(g + 1) * HD, 1, 0:NC_S], w2[0:HD, 0, :], hid_s[0:HD, 0, g, 0:NC_S],
                                       start=True, stop=True)
                    for g in range(NG):
                        mm = pe.matmul(acc[3][0:NC_S, 1, HD + g * HD:HD + (g + 1) * HD], hid_s[0:HD, 1, g, 0:NC_S],
                                       w2[0:HD, 1, :], start=True, stop=True)
                    mm.then_inc(sk_mm, 1)
                    pe.wait_ge(sk_done, n + 1)
                    pe.wait_ge(sv_done, n + 1)
                    settle()
                    for g in range(NG):
                        gs = slice(g * HD, (g + 1) * HD)
                        o = acc[3][rows, g, :]
                        pe.matmul(o[:, 0:TS], q_half[gs, b, :], in_all[gs, T_WK, TP:T], start=True, stop=True)
                        pe.matmul(o[:, TS:TS + NC_S], q_half[gs, b, :], kc_s[gs, 0:NC_S], start=True, stop=True)
                        mm = pe.matmul(o[:, TS + NC_S:2 * TS + NC_S], q_half[gs, b, :], in_all[gs, T_SK, TP:T],
                                       start=True, stop=True)
                    mm.then_inc(ss_b, 1)
                pe.wait_ge(si_in, half + 1)
                pe.wait_ge(ss_dve, half * 4 + 4)
                pe.wait_ge(sv_done, half * 4 + 4)
                pe.matmul(acc[3][:, 1, 0:NG * NC_S], const("samequery"), imp[:, :, 0:NC_S], start=True, stop=True)\
                  .then_inc(si_mm, 1)
                for g in range(NG):
                    pe.wait_ge(sx_exp, half * 3 + 3)
                    if g == 0:
                        pe.wait_ge(ss_act, half * 4 + 4)
                        pe.wait_ge(so_mm, half * 2)
                    else:
                        pe.wait_ge(st_act, half * 2 + 1)
                        pe.wait_ge(st_dve, half * 2 + 1)
                    for k in range(NPG):
                        pe.transpose(acc[0][:, k // 4, k % 4 * P:(k % 4 + 1) * P],
                                     scores[:, g, S0 + k * P:S0 + (k + 1) * P], ident)
                    for k in range(4):
                        pe.transpose(acc[1][:, 0, k * P:(k + 1) * P], scores[:, g, k * P:(k + 1) * P], ident)
                    for k, (c0, n) in enumerate(((WN0, TS), (N0, TS), (C0, NC_S))):
                        mm = pe.transpose(acc[1][0:n, 1, k * P:(k + 1) * P], scores[:, g, c0:c0 + n], ident)
                    mm.then_inc(st_mm, 1)
                    pe.wait_ge(st_act, half * 2 + g + 1)
                    pe.wait_ge(st_dve, half * 2 + g + 1)
                    pe.wait_ge(v_in, (half + 1) * (4 * 16 * 9))
                    settle()
                    for b in range(4):
                        rows = slice(b * 32, (b + 1) * 32)
                        hd = slice(g * HD, (g + 1) * HD)
                        parts = [[(14, NC_S, vc_s[0:NC_S, b, hd])],
                                 [(k, P, v_pages[:, b, k, hd]) for k in range(NPG)] + [(13, TS, v_tm[0:TS, 0, QT, hd])],
                                 [(NPG + k, P, win_v[:, b, k, hd]) for k in range(4)] + [(12, TS, v_tm[0:TS, 1, QT, hd])]]
                        for s_, part in enumerate(parts):
                            o = acc[2][rows, 0, (s_ * NG + g) * HD:(s_ * NG + g + 1) * HD]
                            for k, (slot, n, value) in enumerate(part):
                                mm = pe.matmul(o, sprobT[0:n, slot, rows], value, start=k == 0, stop=k == len(part) - 1)
                    mm.then_inc(so_mm, 1)
                pe.wait_ge(so_done, half + 1)
                for s_ in range(3):
                    mm = pe.transpose(acc[3][:, 0, s_ * P:(s_ + 1) * P],
                                      o_rows[:, 2 * s_:2 * s_ + 2, :].rearrange("p g d -> p (g d)"), ident)
                mm.then_inc(sf_mm, 1)
            with pe.Fori(0, 2) as half:
                pe.wait_ge(ms_q, half + 1)
                pe.wait_ge(sf_done, 2)
                for b in range(4):
                    rows = slice(b * 32, (b + 1) * 32)
                    pe.wait_ge(mk_in[b % 2], K_IN + half * 32 + (b // 2 + 1) * 16)
                    for h in range(MEM_H):
                        mm = pe.matmul(acc[0][rows, 0, 0:MEM_T], mem_q[:, b, h, :], mem_k[:, b % 2, h, :],
                                       start=h == 0, stop=h == MEM_H - 1)
                    mm.then_inc(ms_s, 1)
                pe.wait_ge(ms_exp, MS + half + 1)
                for n in range(2):
                    mm = pe.transpose(acc[1][:, 0, n * P:(n + 1) * P], mem_p[:, n * P:(n + 1) * P], ident)
                mm.then_inc(ms_turn, 1)
                pe.wait_ge(ms_copied, MS + half + 1)
                pe.wait_ge(mv_in, V_IN + (half + 1) * 64)
                for b in range(4):
                    rows = slice(b * 32, (b + 1) * 32)
                    for n in range(2):
                        mm = pe.matmul(acc[2][rows, 0, :], mem_pT[:, n, rows], mem_v[:, b, n, :], start=n == 0, stop=n == 1)
                mm.then_inc(ms_pv, 1)
                pe.wait_ge(ms_norm, half + 1)
                for h in range(MEM_H):
                    mm = pe.transpose(acc[3][:, 0, h * P:(h + 1) * P], mem_o[:, h * P:(h + 1) * P], ident)
                mm.then_inc(ms_ft, 1)

            pe.wait_ge(sf_done, 2)
            pe.wait_ge(ms_done, MS + 2)
            pe.wait_ge(kv_stored, 16)
            for n in range(RW_EARLY, N_RW):
                w = weights(S_RW + n)
                pe.wait_ge(rw_evicted, n + 1)
                for k in range(KT):
                    for b in range(2):
                        mm = pe.matmul(acc[n % 2][:, b, 0:HALF_T], w[:, k, :], hT[:, k, b * HALF_T:(b + 1) * HALF_T],
                                       start=k == 0, stop=k == KT - 1)
                mm.then_inc(slot_used, 1)

            def tokens(a, lhsT, rhs):
                for b in range(2):
                    mm = pe.matmul(acc[a][:, b, 0:HALF_T], lhsT, rhs[:, b * HALF_T:(b + 1) * HALF_T], start=True, stop=True)
                return mm

            def gate_tile(n):
                w = weights(S_MG + n)
                if n:
                    pe.wait_ge(mg_sig, n)
                for k in range(KT):
                    for b in range(2):
                        mm = pe.matmul(acc[2][:, b, 0:HALF_T], w[:, k, :], hT[:, k, b * HALF_T:(b + 1) * HALF_T],
                                       start=k == 0, stop=k == KT - 1)
                mm.then_inc(slot_used, 1)

            for n in range(GATES_FIRST):
                gate_tile(n)
            pe.wait_ge(lo_act, 2)
            pe.wait_ge(rw_evicted, N_RW + 2)
            for i in range(PAIRS):
                ps = slice(i * P, (i + 1) * P)
                for x, (w, rhs) in enumerate(((lw_w[0:HD, ps], tmp[0:HD, 0, :]), (lw_w[HD:P, ps], rwT[HD:P, R_LORA, :]),
                                              (lw_g[:, ps], tmp[:, 1, :]))):
                    if 3 * i + x >= 2:
                        pe.wait_ge(lo_out, 3 * i + x - 1)
                    tokens((3 * i + x) % 2, w, rhs).then_inc(lo_mm, 1)
                pe.wait_ge(kn_sq, i + 1)
                if i > 0:
                    pe.wait_ge(kn_max, i)
                tokens(3, const("headsum"), tmp[:, 2 + i % 2, :]).then_inc(kn_mm, 1)
                gate_tile(GATES_FIRST + i)
            for i in range(PAIRS):
                gate_tile(GATES_FIRST + PAIRS + i)
                pe.wait_ge(bo_in, i + 1)
                if i > 0:
                    pe.wait_ge(prep_done, i)
                else:
                    pe.wait_ge(kn_max, PAIRS)
                tokens(3, const("headsum"), tmp[:, 0, :]).then_inc(bo_mm, 1)
            for n in range(GATES_FIRST + 2 * PAIRS, 3 * KT):
                gate_tile(n)

            pe.sem_inc(o_mm, 1)
            both = lambda n: acc[n][:].rearrange("p a c -> p (a c)")

            def chunk_solve(c, par, n, levels):
                bk, zr = bk_now[:, par, :, 0:2 * n], zr_now[:, par, :, 0:2 * n]
                pe.wait_ge(staged, c + 1)
                pe.wait_ge(o_out, c)
                for i in range(PAIRS):
                    mm = pe.transpose(both(1)[0:2 * n, i * P:(i + 1) * P], bk[:, i, :], ident)
                mm.then_inc(tb_mm, 1)
                pe.wait_ge(s_out, c)
                pe.wait_ge(yt_out, c)
                for i in range(PAIRS):
                    mm = pe.transpose(both(3)[0:2 * n, i * P:(i + 1) * P], v_now[:, i, 0:2 * n], ident)
                mm.then_inc(tv_mm, 1)
                for e in range(2):
                    rows = slice(e * HD, (e + 1) * HD)
                    pe.wait_ge(u_out if e else w_out, c)
                    if e == 0:
                        settle()
                    for i in range(PAIRS):
                        mm = pe.matmul(both(2 * e)[0:2 * n, i * P:i * P + 2 * n], bk[rows, i, :], zr[rows, i, :],
                                       start=True, stop=True)
                    mm.then_inc(gram_mm, 1)
                for e in range(2):
                    pe.wait_ge(gram_out, c * 2 + e + 1)
                    pe.wait_ge(v_rows if e else bk_rows, c + 1)
                    settle()
                    for i in range(PAIRS):
                        mm = pe.transpose(acc[2 * e + 1][0:n, 0, i * C:i * C + n], XT[0:n, e, i, 0:n], ident[0:n, 0:n])
                    mm.then_inc(x_mm, 1)
                for l in range(levels):
                    for e in range(2):
                        pe.wait_ge(x_out, c * 10 + 2 * l + e + 1)
                        settle()
                        for i in range(PAIRS):
                            mm = pe.matmul(acc[2 * e][0:n, 0, i * C:i * C + n], gram[0:n, e, i, 0:n], X[0:n, e, i, 0:n],
                                           start=True, stop=True)
                        mm.then_inc(y_mm, 1)
                    for e in range(2):
                        pe.wait_ge(y_out, c * 10 + 2 * l + e + 1)
                        if l:
                            pe.wait_ge(xt_out, c * 10 + 2 * l - 1 + e)
                        settle()
                        if l < levels - 1:
                            for i in range(PAIRS):
                                mm = pe.matmul(acc[2 * e + 1][0:n, 0, i * C:i * C + n], XT[0:n, e, i, 0:n], Y[0:n, e, i, 0:n],
                                               start=True, stop=True)
                            mm.then_inc(x_mm, 1)
                        for i in range(PAIRS):
                            mm = pe.matmul(acc[2 * e + 1][0:n, 1, i * C:i * C + n], Y[0:n, e, i, 0:n], XT[0:n, e, i, 0:n],
                                           start=True, stop=True)
                        mm.then_inc(xt_mm, 1)

            def chunk_out(c, par, n, levels, state):
                bk, zr = bk_now[:, par, :, 0:2 * n], zr_now[:, par, :, 0:2 * n]
                pe.wait_ge(s_out, c)
                pe.wait_ge(y_out, c * 10 + 2 * levels)
                pe.wait_ge(uv_v, c + 1)
                settle()
                for i in range(PAIRS):
                    for e in range(2):
                        o = both(0)[0:n, i * P + e * C:i * P + e * C + C]
                        state(o, 0, i, e, zr)
                        mm = pe.matmul(o, gram[0:2 * n, e, i, 0:n],
                                       zv[0:2 * n, i, e, :], start=False, stop=True)
                mm.then_inc(w_mm, 1)
                pe.wait_ge(w_out, c + 1)
                pe.wait_ge(xt_out, c * 10 + 2 * levels)
                settle()
                for i in range(PAIRS):
                    for e in range(2):
                        mm = pe.matmul(both(2)[0:n, i * P + e * C:i * P + e * C + C], XT[0:n, e, i, 0:n],
                                       w_tm[0:n, i, e * C:(e + 1) * C], start=True, stop=True)
                mm.then_inc(u_mm, 1)
                pe.wait_ge(u_out, c + 1)
                settle()

            def chunk_y(c, par, n, state):
                bk, zr = bk_now[:, par, :, 0:2 * n], zr_now[:, par, :, 0:2 * n]
                for i in range(PAIRS):
                    for e in range(2):
                        o = both(1)[0:n, i * P + e * C:i * P + e * C + C]
                        state(o, 1, i, e, zr)
                        mm = pe.matmul(o, gram[0:2 * n, e, i, n:2 * n],
                                       uv[0:2 * n, i, e, :], start=False, stop=True)
                mm.then_inc(o_mm, 1)

            def chunk_turn(c, n):
                pe.wait_ge(o_out, c + 1)
                settle()
                for i in range(PAIRS):
                    mm = pe.transpose(acc[3][:, 1, i * C:i * C + n], y_tm[0:n, i, :], ident[0:n, 0:n])
                mm.then_inc(yt_mm, 1)

            def state_product(o, x, i, e, zr):
                pe.matmul(o, zr[:, i, x * C:(x + 1) * C], S[:, i, e, :], start=True, stop=False)

            with pe.Fori(0, NCH // 2) as it:
                for par in range(2):
                    c = it * 2 + par
                    chunk_solve(c, par, C, 5)
                    chunk_out(c, par, C, 5, state_product)
                    for e in range(2):
                        for i in range(PAIRS):
                            mm = pe.matmul(acc[3][e * HD:(e + 1) * HD, 0, i * C:(i + 1) * C], bk_tm[:, i, e * HD:(e + 1) * HD],
                                           uv[:, i, e, :], start=True, stop=True)
                    mm.then_inc(s_mm, 1)
                    chunk_y(c, par, C, state_product)
                    chunk_turn(c, C)

            pe.wait_ge(states_in, 32)
            chunk_solve(NCH, 0, TS, 1)

            def state_sample(o, x, i, e, zr):
                turn = (x * PAIRS + i) + 1
                pe.wait_ge(z_masked, turn)
                zb = z_b[:, turn % 2, :].rearrange("p (b t) -> p b t", b=NB)
                for b in range(NB):
                    mm = pe.matmul(o, zb[:, b, :], S_s[:, b, i, e, :], start=b == 0, stop=False)
                if e:
                    mm.then_inc(z_used, 1)

            chunk_out(NCH, 0, TS, 1, state_sample)
            chunk_y(NCH, 0, TS, state_sample)
            chunk_turn(NCH, TS)
            for i in range(PAIRS):
                for e in range(2):
                    j = 2 * i + e
                    pe.wait_ge(uvb_done, j + 1)
                    if i >= 1:
                        pe.wait_ge(wkv_done, 2 * i)
                    else:
                        pe.wait_ge(o_out, NCH + 1)
                    mm = pe.matmul(acc[1][e * HD:(e + 1) * HD, 0, :], bk_tm[0:2 * TS, i, e * HD:(e + 1) * HD],
                                   uv_b[0:2 * TS, j % 2].rearrange("p b c -> p (b c)"), start=True, stop=True)
                    mm.then_inc(uvb_used, 1)

            def gn_tokens(a, rhs):
                for b in range(2):
                    mm = pe.matmul(acc[a][:, b, 0:HALF_T], const("headsum"), rhs[:, b * HALF_T:(b + 1) * HALF_T],
                                   start=True, stop=True)
                return mm

            pe.wait_ge(yt_out, NCH + 1)
            for i in range(PAIRS):
                pe.wait_ge(gn_diff, PAIRS + i) if i else pe.wait_ge(wkv_done, 2 * PAIRS)
                gn_tokens(0, zT[:, i, :]).then_inc(gn_mean, 1)
                pe.wait_ge(gn_sq, 3 * PAIRS + i + 1)
                if i:
                    pe.wait_ge(gn_max, PAIRS + i)
                gn_tokens(1, kkT[:, 2 + i % 2, :]).then_inc(gn_var, 1)

            pe.wait_ge(gn_done, PAIRS)
            block = 0
            for m in range(KT):
                sources = ([onsaT[:, r, :] for r in range(HPG)], [zT[:, i, :] for i in range(PAIRS)],
                           [omemT[:, h, :] for h in range(MEM_H)])
                for g, source in enumerate(sources):
                    n = 3 * m + g
                    if n >= 4:
                        pe.wait_ge(mg_part, n - 3)
                    for k, x in enumerate(source):
                        if block % KT == 0:
                            w = weights(S_MERGE + block // KT)
                        for b in range(2):
                            mm = pe.matmul(acc[n % 4][:, b, 0:HALF_T], w[:, block % KT, :],
                                           x[:, b * HALF_T:(b + 1) * HALF_T], start=k == 0, stop=k == len(source) - 1)
                        block += 1
                        if block % KT == 0:
                            mm.then_inc(slot_used, 1)
                        elif k == len(source) - 1:
                            mm.then_inc(mg_mm, 1)

            def square_sum(j, done):
                pe.wait_ge(sqT_made, done + j + 1)
                for b in range(2):
                    mm = pe.matmul(acc[3][:, b, 0:HALF_T], ones, sqT[:, j % 2, b * HALF_T:(b + 1) * HALF_T],
                                   start=j == 0, stop=j == KT - 1)
                mm.then_inc(sqT_summed, 1)

            pe.wait_ge(mg_part, 3 * KT + 1)
            for j in range(KT):
                w = weights(S_OUT + j)
                if j >= 2:
                    pe.wait_ge(x1_added, j - 1)
                for k in range(KT):
                    for b in range(2):
                        mm = pe.matmul(acc[j % 2][:, b, 0:HALF_T], w[:, k, :], mT[:, k, b * HALF_T:(b + 1) * HALF_T],
                                       start=k == 0, stop=k == KT - 1)
                mm.then_inc(slot_used, 1)
                if j:
                    square_sum(j - 1, 0)
            square_sum(KT - 1, 0)

            def ff_tile(n, it=None):
                t_done = n if it is None else it * 10 + n
                for x in range(2):
                    w = weights(S_GU + 2 * n + x, it, 20)
                    if it is not None or n >= 2:
                        pe.wait_ge(ff_done if x else gu_act, t_done + 1)
                    for k in range(KT):
                        for b in range(2):
                            mm = pe.matmul(acc[2 * x + n % 2][:, b, 0:HALF_T], w[:, k, :],
                                           hT[:, k, b * HALF_T:(b + 1) * HALF_T], start=k == 0, stop=k == KT - 1)
                    mm.then_inc(slot_used, 1)

            pe.wait_ge(hf_done, KT)
            with pe.Fori(0, FFT // 10) as it:
                for n in range(10):
                    ff_tile(n, it)
            for n in range(FFT // 10 * 10, FFT):
                ff_tile(n)

            pe.wait_ge(ff_done, FFT + 2)
            block = 0
            for j in range(KT):
                if j >= 2:
                    pe.wait_ge(x1_added, KT + j - 1)
                for k in range(FFT):
                    if block % KT == 0:
                        w = weights(S_DOWN + block // KT)
                    for b in range(2):
                        mm = pe.matmul(acc[j % 2][:, b, 0:HALF_T], w[:, block % KT, :],
                                       ffT[:, k, b * HALF_T:(b + 1) * HALF_T], start=k == 0, stop=k == FFT - 1)
                    block += 1
                    if block % KT == 0:
                        mm.then_inc(slot_used, 1)
                    elif k == FFT - 1:
                        mm.then_inc(dn_mm, 1)
                if j:
                    square_sum(j - 1, KT)
            square_sum(KT - 1, KT)

        @block.scalar
        def _(act):
            for i in range(QT):
                act.dma_start(x_tm[:, i, :], A["x_all"][i * P:(i + 1) * P]).then_inc(x_in[0], 16)
            act.dma_start(x_tm[0:TS, QT, :], A["x_all"][TP:T]).then_inc(x_in[0], 16)
            for i in range(2):
                act.dma_start(x_tm[:, 5 + i, :], A["mem_x"][i * P:(i + 1) * P]).then_inc(x_in[1], 16)
            own = Steps(act, act_own)
            act.wait_ge(means, 1)
            for i, (rows, *_) in enumerate(NORM):
                act.wait_ge(x_in[i > QT], 32 if i > QT else 16 * (QT + 1))
                own(act.activation(junk[0:rows], x_tm[0:rows, i, :], ACT.Square, accum_out=stat[0:rows, i:i + 1]))
            act.activation(stat[:, 16:17], stat[:, 0:1], ACT.Copy).then_inc(squares, 1)
            act.wait_ge(means, 2)
            act.activation(stat[:, 8:15], stat[:, 8:15], ACT.Sqrt).then_inc(roots, 1)
            act.wait_ge(gates_mm, 1)
            act.activation(gates_tm[:, 0:QT, :], acc[2][:, 0, 0:36 * QT].rearrange("p (n c) -> p n c", n=QT),
                           ACT.Sigmoid).then_inc(gates_done, 1)
            act.activation(gates_s[:], acc[2][0:36, 1, 0:TS], ACT.Sigmoid).then_inc(gates_done, 1)
            act.wait_ge(hT_ready, 7)
            act.sem_inc(in_evicted, 2)
            with act.Fori(0, N_IN // 2) as i:
                for k in range(2):
                    act.wait_ge(slot_used, i * 2 + k + 1)
                    act.activation(in_all[:, bass.ds(i * 2 + k, 1), :].rearrange("p a (b t) -> p (a b) t", b=2),
                                   acc[k][:, :, 0:HALF_T], ACT.Copy).then_inc(in_evicted, 1)
            act.wait_ge(slot_used, S_RW)
            for n in range(2):
                act.activation(mem_tm[:, n, :], acc[n][:].rearrange("p a c -> p (a c)"), ACT.Copy)\
                   .then_inc(mem_done, 1)

            act.wait_ge(cp_mm, 3)
            act.wait_ge(cp_done, 2)
            for kind in range(2):
                act.activation(hid[0:HD, kind, :, 0:NC_P],
                               acc[3][0:HD, 0, kind * 2 * TS:(kind + 1) * 2 * TS].rearrange("p (g n) -> p g n", g=NG)[:, :, 0:NC_P],
                               ACT.Gelu_apprx_tanh, bias=pre_bias[0:HD, kind:kind + 1]).then_inc(cp_done, 1)
            for u, (g, t) in enumerate(CMP_UNITS):
                act.wait_ge(cs_shift, u + 1)
                act.activation(c_prob, c_shift, ACT.Exp).then_inc(cs_exp, 1)
                for n in range(3 * u // 2, 3 * (u + 1) // 2):
                    act.wait_ge(slot_used, S_RW + n + 1)
                    if n >= 2:
                        act.wait_ge(spilled[n % 2], n // 2 * 16)
                    act.activation(rw_now[:, n % 2, :].rearrange("p (b t) -> p b t", b=2), acc[3][:, :, 0:HALF_T],
                                   ACT.Copy).then_inc(rw_evicted, 1)
                act.wait_ge(cs_out, u + 1)
                act.activation(o_tm[:, t, :, g * HD:(g + 1) * HD],
                               acc[2][:, 0, 0:HPG * HD].rearrange("p (r d) -> p r d", r=HPG), ACT.Copy)\
                   .then_inc(cs_o, 1)
            act.wait_ge(cs_out, len(CMP_UNITS))
            for n in range(2):
                act.wait_ge(spilled[n], 16 * RW_EARLY // 2)
            act.sem_inc(at_exp, 2)
            act.sem_inc(at_cw, 1)

            def att_exp(it, u):
                g, t = ATT_UNITS[u]
                w = (t + 1) * P
                act.wait_ge(at_max, it * 8 + u + 1)
                act.wait_ge(at_turn, it * 8 + u - 1) if u >= 2 else None
                if u < 2:
                    act.wait_ge(at_turn, it * 8)
                for b in range(2):
                    ins = act.activation(probs[:, u % 2, b, 0:w], acc[u % 2][:, b, 0:w], ACT.Exp,
                                         bias=small[:, 2 * (u % 2) + b:2 * (u % 2) + b + 1],
                                         accum_out=small[:, 8 + 2 * (u % 2) + b:9 + 2 * (u % 2) + b])
                ins.then_inc(at_exp, 1)

            def att_copy(it, u):
                g, t = ATT_UNITS[u]
                w = (t + 1) * P
                act.wait_ge(at_turn, it * 8 + u + 1)
                act.wait_ge(at_pv, it * 8 + u)
                act.activation(probsT[:, 1, 0:w], acc[2][:, 1, 0:w], ACT.Copy).then_inc(at_cw, 1)

            with act.Fori(0, HPG) as it:
                act.wait_ge(at_s, it * 8)
                act.activation(q_now, qT[:, bass.ds(it, 1), 0:TP].rearrange("p a t -> p (a t)"), ACT.Copy)\
                   .then_inc(at_q, 1)
                for u in range(8):
                    att_exp(it, u)
                    if u >= 1:
                        att_copy(it, u - 1)
                att_copy(it, 7)
            for r in range(HPG):
                act.wait_ge(ot_mm, r + 1)
                act.activation(onsaT[:, r, 0:TP], acc[0][:, r % 2, :], ACT.Copy).then_inc(ot_done, 1)
            for t in range(QT):
                act.wait_ge(ma_max, MA + t + 1)
                if t >= 1:
                    act.wait_ge(ma_turn, MA + t)
                for h in range(MEM_H):
                    ins = act.activation(m_prob[:, h, :], acc[0][:, h // 2, h % 2 * MEM_T:(h % 2 + 1) * MEM_T],
                                         ACT.Exp, bias=small[:, 24 + h:25 + h], accum_out=small[:, 28 + h:29 + h])
                ins.then_inc(ma_exp, 1)
                act.wait_ge(ma_pv, MA + t + 1)
                act.activation(omemT[:, :, t * P:(t + 1) * P], acc[2][:, 0, :].rearrange("p (h t) -> p h t", h=MEM_H),
                               ACT.Copy).then_inc(ma_done, 1)

            with act.Fori(0, 2) as half:
                for b in range(4):
                    n, rows = half * 4 + b, slice(b * 32, (b + 1) * 32)
                    act.wait_ge(ss_a, n + 1)
                    for g in range(NG):
                        ins = act.activation(scores[rows, g, S0:S0 + PAST], acc[g][rows].rearrange("p a c -> p (a c)"),
                                             ACT.Copy)
                    ins.then_inc(ss_act, 1)
                    act.wait_ge(sp_mm, n + 1)
                    for kind in range(2):
                        ins = act.activation(hid_s[0:HD, kind, :, 0:NC_S],
                                             acc[3][0:HD, 0, kind * P:(kind + 1) * P]
                                             .rearrange("p (g n) -> p g n", g=NG)[:, :, 0:NC_S],
                                             ACT.Gelu_apprx_tanh, bias=pre_bias[0:HD, kind:kind + 1])
                    ins.then_inc(sp_done, 1)
                    act.wait_ge(sk_done, n + 1)
                    act.activation(vc_s[0:NC_S, b, :], acc[3][0:NC_S, 1, HD:HD + P], ACT.Copy).then_inc(sv_done, 1)
                for x, (c0, c1) in enumerate(((C0, N0), (W0, C0), (N0, S0 + PAST))):
                    act.wait_ge(sx_max, half * 3 + x + 1)
                    for g in range(NG):
                        ins = act.activation(scores[:, g, c0:c1], scores[:, g, c0:c1], ACT.Exp,
                                             bias=small[:, 2 * x + g:2 * x + g + 1],
                                             accum_out=small[:, 8 + 2 * x + g:9 + 2 * x + g])
                    ins.then_inc(sx_exp, 1)
                for g in range(NG):
                    act.wait_ge(st_mm, half * 2 + g + 1)
                    act.wait_ge(so_mm, half * 2 + g)
                    act.activation(sprobT[:, NPG:NPG + 4, :].rearrange("p a c -> p (a c)"), acc[1][:, 0, :], ACT.Copy)
                    act.activation(sprobT[0:TS, 12:14, :].rearrange("p a c -> p (a c)"), acc[1][0:TS, 1, 0:2 * P], ACT.Copy)
                    act.activation(sprobT[0:NC_S, 14, :], acc[1][0:NC_S, 1, 2 * P:3 * P], ACT.Copy).then_inc(st_act, 1)
            with act.Fori(0, 2) as half:
                act.wait_ge(ms_max, MS + half + 1)
                act.activation(mem_p, acc[0][:, 0, 0:MEM_T], ACT.Exp, bias=small[:, 0:1], accum_out=small[:, 1:2])\
                   .then_inc(ms_exp, 1)
                act.wait_ge(ms_turn, MS + half + 1)
                act.activation(mem_pT[:].rearrange("p a c -> p (a c)"), acc[1][:, 0, 0:2 * P], ACT.Copy).then_inc(ms_copied, 1)

            act.wait_ge(sf_done, 2)
            act.wait_ge(ms_done, MS + 2)
            act.wait_ge(kv_stored, 16)
            act.wait_ge(win_stored, 16 * (NB + 1))
            act.sem_inc(rw_evicted, 2)
            for n in range(RW_EARLY, N_RW):
                act.wait_ge(slot_used, S_RW + n + 1)
                act.activation(rwT[:, n, :].rearrange("p (b t) -> p b t", b=2), acc[n % 2][:, :, 0:HALF_T],
                               ACT.Copy).then_inc(rw_evicted, 1)
            h2 = lambda a: a.rearrange("p (b t) -> p b t", b=2)
            def gate_tile(n):
                act.wait_ge(slot_used, S_MG + n + 1)
                if n >= 2:
                    act.wait_ge(spilled[n % 2], (RW_EARLY + n) // 2 * 16)
                act.activation(h2(gate_now[:, n % 2, :]), acc[2][:, :, 0:HALF_T], ACT.Sigmoid).then_inc(mg_sig, 1)

            for n in range(GATES_FIRST):
                gate_tile(n)
            act.wait_ge(xm_done, N_RW)
            act.activation(tmp[:, 1, :], rwT[:, R_GD, :], ACT.Sigmoid).then_inc(lo_act, 1)
            act.activation(tmp[0:HD, 0, :], rwT[0:HD, R_LORA, :], ACT.Tanh).then_inc(lo_act, 1)
            for i in range(PAIRS):
                for x, (dst, f, bias) in enumerate(((zT, ACT.Sigmoid, "w0"), (bT, ACT.Sigmoid, "a0"), (gT, ACT.Copy, None))):
                    act.wait_ge(lo_mm, 3 * i + x + 1)
                    more = dict(bias=v(bias, i)) if bias else {}
                    act.activation(h2(dst[:, i, :]), acc[(3 * i + x) % 2][:, :, 0:HALF_T], f, **more).then_inc(lo_out, 1)
                gate_tile(GATES_FIRST + i)
                act.wait_ge(kn_max, i + 1)
                act.activation(tmp[:, 4 + i % 2, :], tmp[:, 4 + i % 2, :], ACT.Sqrt).then_inc(kn_root, 1)
            for i in range(PAIRS):
                gate_tile(GATES_FIRST + PAIRS + i)
                act.wait_ge(ex_in, i + 1)
                act.activation(tmp[:, 2, :], tmp[:, 1, :], ACT.Exp)
                act.activation(tmp[:, 3, :], tmp[:, 1, :], ACT.Exp, scale=-1.0)
                act.activation(tmp[:, 4, :], tmp[:, 5, :], ACT.Exp).then_inc(ex_out, 1)
            for n in range(GATES_FIRST + 2 * PAIRS, 3 * KT):
                gate_tile(n)
            both = lambda n: acc[n][:].rearrange("p a c -> p (a c)")
            flat = lambda a: a.rearrange("p a c -> p (a c)")

            def chunk(c, n, levels, t0):
                act.wait_ge(tb_mm, c + 1)
                act.activation(flat(bk_tm[0:2 * n]), both(1)[0:2 * n, 0:PAIRS * P], ACT.Copy).then_inc(bk_rows, 1)
                act.wait_ge(tv_mm, c + 1)
                act.activation(zv[0:2 * n].rearrange("p a e c -> p (a e c)"), both(3)[0:2 * n, 0:PAIRS * P], ACT.Copy)\
                   .then_inc(v_rows, 1)
                for l in range(levels):
                    for e in range(2):
                        act.wait_ge(x_mm, c * 10 + 2 * l + e + 1)
                        act.activation(X[0:n, e, :, 0:n],
                                       acc[2 * e + 1][0:n, 0, 0:PAIRS * C].rearrange("p (i s) -> p i s", i=PAIRS)[:, :, 0:n],
                                       ACT.Copy).then_inc(x_out, 1)
                act.wait_ge(w_mm, c + 1)
                act.activation(flat(w_tm[0:n]), both(0)[0:n, 0:PAIRS * P], ACT.Copy).then_inc(w_out, 1)
                act.wait_ge(o_mm, c + 2)
                act.activation(flat(y_tm[0:n]), both(1)[0:n, 0:PAIRS * P], ACT.Copy).then_inc(o_out, 1)
                act.wait_ge(yt_mm, c + 1)
                act.activation(zT[:, :, bass.ds(t0, n)],
                               acc[3][:, 1, 0:PAIRS * C].rearrange("p (i s) -> p i s", i=PAIRS)[:, :, 0:n],
                               ACT.Copy).then_inc(yt_out, 1)

            for n in range(2):
                act.wait_ge(spilled[n], 16 * (RW_EARLY + 3 * KT) // 2)
            with act.Fori(0, NCH) as it:
                chunk(it, C, 5, it * C)
            chunk(NCH, TS, 1, TP)
            for i in range(PAIRS):
                act.wait_ge(gn_diff, PAIRS + i + 1)
                act.activation(kkT[:, 2 + i % 2, :], kkT[:, i % 2, :], ACT.Square).then_inc(gn_sq, 1)
                act.wait_ge(gn_max, PAIRS + i + 1)
                act.activation(kkT[:, 4, :], kkT[:, 4, :], ACT.Sqrt).then_inc(gn_root, 1)

            def norm(done):
                for j in range(KT):
                    act.wait_ge(x1_added, done + j + 1)
                    if done + j >= 2:
                        act.wait_ge(sqT_summed, done + j - 1)
                    act.activation(sqT[:, j % 2, :], x1T[:, j, :], ACT.Square).then_inc(sqT_made, 1)
                act.wait_ge(rms_in, done // KT + 1)
                act.activation(rms, rms, ACT.Sqrt).then_inc(rms_root, 1)

            norm(0)
            act.sem_inc(gu_act, 2)

            def ff_tile(n, it=None):
                act.wait_ge(slot_used, S_GU + 2 * n + 1 if it is None else it * 20 + S_GU + 2 * n + 1)
                t = n if it is None else it * 10 + n
                act.activation(ffT[:, bass.ds(t, 1), :].rearrange("p a (b t) -> p (a b) t", b=2),
                               acc[n % 2][:, :, 0:HALF_T], ACT.Silu).then_inc(gu_act, 1)

            with act.Fori(0, FFT // 10) as it:
                for n in range(10):
                    ff_tile(n, it)
            for n in range(FFT // 10 * 10, FFT):
                ff_tile(n)
            norm(KT)

        @block.vector
        def _(dve):
            own = Steps(dve, dve_own)
            dve.memset(stat[:], 1.0).then_inc(means, 1)
            dve.wait_ge(squares, 1)
            dve.tensor_scalar(stat[:, 8:15], stat[:, 0:7], 1.0 / D, RMS_EPS, ALU.mult, ALU.add).then_inc(means, 1)
            dve.wait_ge(roots, 1)
            own(dve.reciprocal(stat[:, 8:15], stat[:, 8:15]))
            for i, (rows, *_) in enumerate(NORM):
                dve.tensor_scalar(x_tm[0:rows, i, :], x_tm[0:rows, i, :], stat[0:rows, 8 + i:9 + i], None, ALU.mult)\
                   .then_inc(scaled, 1)
            for i, (rows, t0, dst, gain) in enumerate(NORM):
                dve.wait_ge(turned, i + 1)
                o = acc[i % 2][:].rearrange("p a (k t) -> p (a k) t", t=P)
                dve.tensor_tensor(dst[:, :, t0:t0 + rows], o[:, :, 0:rows], bc(v(gain, 0, KT), 2, rows), ALU.mult)\
                   .then_inc(hT_ready, 1)

            dve.wait_ge(rows_mm, 1)
            for n in range(2):
                dve.tensor_copy(v_tm[:, n, 0:QT, :].rearrange("p t c -> p (t c)"), acc[2 + n][:, 0, :])
                ins = dve.tensor_copy(v_tm[0:TS, n, QT, :], acc[2 + n][0:TS, 1, 0:P])
            ins.then_inc(rows_done, 2)
            dve.wait_ge(rows_mm, 2)
            dve.tensor_copy(mkT[:].rearrange("p h t -> p (h t)"), acc[0][:].rearrange("p a c -> p (a c)"))\
               .then_inc(rows_done, 1)
            own(dve.tensor_scalar(in_all[:, T_Q:T_Q + 6, :], in_all[:, T_Q:T_Q + 6, :], HD ** -0.5, None, ALU.mult))
            dve.tensor_scalar(mqT, mqT, P ** -0.5, None, ALU.mult).then_inc(q_scaled, 1)
            dve.wait_ge(cp_mm, 1)
            dve.wait_ge(cmp_in, 96)
            dve.tensor_tensor(pre_bias[0:HD], acc[1][0:HD, 0, 0:2], b1[0:HD], ALU.add).then_inc(cp_done, 1)
            dve.wait_ge(cp_mm, 2)
            dve.tensor_copy(u_sb, acc[2][:, :, 0:2 * TS].rearrange("p g (k n) -> p g k n", k=2)).then_inc(cp_done, 1)
            dve.wait_ge(cp_mm, 4)
            dve.tensor_copy(kcT[:, 0:NC_P], acc[2][:, 0, 0:NC_P]).then_inc(cp_done, 1)
            dve.tensor_copy(vc[0:NC_P], acc[2][0:NC_P, 1, 0:P]).then_inc(cp_done, 1)
            for u, (g, t) in enumerate(CMP_UNITS):
                dve.wait_ge(cs_mm, u + 1)
                s3 = acc[0][:, 0, 0:HPG * NC_P].rearrange("p (r n) -> p r n", r=HPG)
                own(dve.tensor_reduce(small[:, 0:HPG], s3, AX, ALU.max, negate=True))
                dve.tensor_tensor(c_shift, s3, bc(small[:, 0:HPG], 2, NC_P), ALU.add).then_inc(cs_shift, 1)
                dve.wait_ge(cs_exp, u + 1)
                own(dve.tensor_reduce(small[:, 8:8 + HPG], c_prob, AX, ALU.add))
                own(dve.reciprocal(small[:, 8:8 + HPG], small[:, 8:8 + HPG]))
                own(dve.tensor_tensor(small[:, 16:16 + HPG], small[:, 8:8 + HPG],
                                      gates_tm[:, t, g * 18:g * 18 + 18].rearrange("p (r b) -> p r b", b=3)[:, :, 0],
                                      ALU.mult))
                own(dve.tensor_tensor(c_prob, c_prob, bc(const("cmp01")[:, t * NC_P:(t + 1) * NC_P], 1, HPG), ALU.mult))
                dve.tensor_tensor(c_prob, c_prob, bc(small[:, 16:16 + HPG], 2, NC_P), ALU.mult).then_inc(cs_prob, 1)
                dve.wait_ge(cs_turn, u + 1)
                dve.tensor_copy(c_probT[0:NC_P], acc[1][0:NC_P].rearrange("p a (r t) -> p (a r) t", t=P)[:, 0:HPG, :])\
                   .then_inc(cs_copied, 1)
            dve.wait_ge(cs_o, len(CMP_UNITS))
            dve.sem_inc(at_cs, 1)
            dve.sem_inc(at_o, 2)

            def att_max(it, u):
                g, t = ATT_UNITS[u]
                w = (t + 1) * P
                dve.wait_ge(at_s, it * 8 + u + 1)
                dve.tensor_reduce(small[:, 2 * (u % 2):2 * (u % 2) + 2], acc[u % 2][:, :, 0:w], AX, ALU.max, negate=True)\
                   .then_inc(at_max, 1)

            def att_copy(it, u):
                g, t = ATT_UNITS[u]
                w = (t + 1) * P
                d = 8 + 2 * (u % 2)
                dve.wait_ge(at_turn, it * 8 + u + 1)
                dve.wait_ge(at_pv, it * 8 + u)
                dve.tensor_copy(probsT[:, 0, 0:w], acc[2][:, 0, 0:w]).then_inc(at_cs, 1)
                dve.wait_ge(at_o, it * 8 + u + 1)
                own(dve.reciprocal(small[:, d + 4:d + 6], small[:, d:d + 2]))
                gate = gates_tm[:, t, g * 18:g * 18 + 18].rearrange("p (r b) -> p r b", b=3)[:, bass.ds(it, 1), 1:3]
                own(dve.tensor_tensor(small[:, d + 4:d + 6], small[:, d + 4:d + 6], gate.rearrange("p a b -> p (a b)"),
                                      ALU.mult))

            def att_out(it, u):
                g, t = ATT_UNITS[u]
                d = 8 + 2 * (u % 2)
                o = o_tm[:, t, bass.ds(it, 1), g * HD:(g + 1) * HD].rearrange("p a d -> p (a d)")
                dve.wait_ge(at_pv, it * 8 + u + 1)
                own(dve.scalar_tensor_tensor(o, acc[3][:, u % 2, 0:HD], small[:, d + 4:d + 5], o, ALU.mult, ALU.add))
                dve.scalar_tensor_tensor(o, acc[3][:, u % 2, HD:2 * HD], small[:, d + 5:d + 6], o, ALU.mult, ALU.add)\
                   .then_inc(at_o, 1)

            with dve.Fori(0, HPG) as it:
                own.loop(it, 8 * 3)
                for u in range(8):
                    att_max(it, u)
                    if u >= 1:
                        att_copy(it, u - 1)
                    if u >= 2:
                        att_out(it, u - 2)
                att_out(it, 6)
                att_copy(it, 7)
                att_out(it, 7)
            own.end(HPG)
            for t in range(QT):
                dve.wait_ge(ma_s, MA + t + 1)
                if t >= 1:
                    dve.wait_ge(ma_exp, MA + t)
                dve.tensor_reduce(small[:, 24:28], acc[0][:].rearrange("p a (h t) -> p (a h) t", h=2), AX, ALU.max,
                                  negate=True).then_inc(ma_max, 1)
                dve.wait_ge(ma_exp, MA + t + 1)
                own(dve.reciprocal(small[:, 32:36], small[:, 28:32]))
                dve.tensor_tensor(m_prob, m_prob, bc(small[:, 32:36], 2, MEM_T), ALU.mult).then_inc(ma_prob, 1)
                dve.wait_ge(ma_turn, MA + t + 1)
                if t >= 1:
                    dve.wait_ge(ma_pv, MA + t)
                dve.tensor_copy(m_probT[:].rearrange("p a c -> p (a c)"), acc[1][:].rearrange("p a c -> p (a c)"))\
                   .then_inc(ma_copied, 1)

            dve.wait_ge(sg_mm, 1)
            dve.tensor_copy(grep[:].rearrange("p a c -> p (a c)"), acc[0][:].rearrange("p a c -> p (a c)")[:, 0:18 * TS])\
               .then_inc(sg_done, 1)
            dve.wait_ge(mem_stored, 16)
            dve.memset(q_half, 0.0)
            own(dve.memset(imp, 0.0))
            with dve.Fori(0, 2) as half:
                own.loop(half, 15)
                dve.wait_ge(ss_b, half * 4)
                dve.tensor_copy(q_half[:, :, 0:HPG * NQ].rearrange("p b (r q) -> p b r q", q=NQ),
                                qT[:, :, bass.ds(TP + half * 16, 16)].rearrange("p r (b q) -> p b r q", q=NQ))\
                   .then_inc(sq_done, 1)
                for b in range(4):
                    n, rows = half * 4 + b, slice(b * 32, (b + 1) * 32)
                    dve.wait_ge(su_mm, n + 1)
                    dve.tensor_copy(u_s, acc[2][:, :, 0:P].rearrange("p g (k n) -> p g k n", k=2)).then_inc(su_done, 1)
                    dve.wait_ge(sk_mm, n + 1)
                    dve.tensor_copy(kc_s[:, 0:NC_S], acc[3][:, 1, 0:NC_S]).then_inc(sk_done, 1)
                    dve.wait_ge(ss_b, n + 1)
                    dve.tensor_copy(scores[rows, :, W0:WIN], acc[2][rows])
                    dve.tensor_copy(scores[rows, :, WN0:S0], acc[3][rows, :, 0:S0 - WN0]).then_inc(ss_dve, 1)
                dve.wait_ge(ss_dve, half * 4 + 4)
                dve.tensor_reduce(small[:, 0:2], scores[:, :, C0:N0], AX, ALU.max, negate=True).then_inc(sx_max, 1)
                lo = SEG["winnew"][0]
                dve.tensor_tensor(scores[:, :, WN0:C0], scores[:, :, WN0:C0],
                                  bc(cst[:, bass.ds(half * TS + lo, TS)], 1, NG), ALU.add)
                dve.tensor_tensor(scores[:, :, W0:W0 + NQ], scores[:, :, W0:W0 + NQ], bc(const("winfirst"), 1, NG), ALU.add)
                lo = SEG["newmask"][0]
                own(dve.tensor_tensor(scores[:, :, N0:S0], scores[:, :, N0:S0],
                                      bc(cst[:, bass.ds(half * TS + lo, TS)], 1, NG), ALU.add))
                dve.tensor_reduce(small[:, 2:4], scores[:, :, W0:C0], AX, ALU.max, negate=True).then_inc(sx_max, 1)
                dve.wait_ge(sx_exp, half * 3 + 1)
                own(dve.reciprocal(small[:, 16:18], small[:, 8:10]))
                dve.tensor_tensor(imp[:, :, 0:NC_S], scores[:, :, C0:N0], bc(small[:, 16:18], 2, NC_S), ALU.mult)\
                   .then_inc(si_in, 1)
                dve.wait_ge(si_mm, half + 1)
                own(dve.tensor_copy(imp[:, :, 65:65 + NC_S], acc[3][:, 1, 0:NG * NC_S].rearrange("p (g n) -> p g n", g=NG)))
                own(dve.tensor_reduce(small[:, 24:56].rearrange("p (g s) -> p g s", g=NG),
                                      imp[:, :, 64:128].rearrange("p g (s n) -> p g s n", n=4), AX, ALU.add))
                blocks = small[:, 24:56].rearrange("p (g s) -> p g s", g=NG)
                own(dve.tensor_tensor(blocks, blocks, imp[:, :, 68:129:4], ALU.add))
                inner = blocks[:, :, 1:15]
                own(dve.tensor_reduce(small[:, 16:18], inner, AX, ALU.min))
                own(dve.tensor_tensor(inner, inner, bc(small[:, 16:18], 2, 14), ALU.is_equal))
                own(dve.tensor_tensor(inner, inner, bc(const("blockno"), 1, NG), ALU.mult))
                own(dve.tensor_reduce(small[:, 16:18], inner, AX, ALU.max))
                own(dve.tensor_tensor(inner, inner, bc(small[:, 16:18], 2, 14), ALU.is_equal))
                own(dve.tensor_scalar(inner, inner, NEG, None, ALU.mult))
                dve.wait_ge(ss_act, half * 4 + 4)
                part = scores[:, :, S0 + HD:S0 + 15 * HD].rearrange("p g (s c) -> p g s c", c=HD)
                own(dve.tensor_tensor(part, part, bc(inner, 3, HD), ALU.add))
                dve.tensor_reduce(small[:, 4:6], scores[:, :, N0:S0 + PAST], AX, ALU.max, negate=True).then_inc(sx_max, 1)
                for g in range(NG):
                    dve.wait_ge(st_mm, half * 2 + g + 1)
                    dve.wait_ge(so_mm, half * 2 + g)
                    dve.tensor_copy(sprobT[:, 0:NPG, :].rearrange("p a c -> p (a c)"),
                                    acc[0][:].rearrange("p a c -> p (a c)")).then_inc(st_dve, 1)
                dve.wait_ge(sx_exp, half * 3 + 3)
                dve.reciprocal(small[:, 56:58], small[:, 8:10])
                dve.reciprocal(small[:, 58:60], small[:, 12:14])
                own(dve.reciprocal(small[:, 60:62], small[:, 10:12]))
                dve.wait_ge(so_mm, half * 2 + 2)
                dve.tensor_tensor(o_rows, acc[2][:, 0, 0:6 * HD].rearrange("p (s d) -> p s d", d=HD),
                                  bc(small[:, 56:62], 2, HD), ALU.mult).then_inc(so_done, 1)
                dve.wait_ge(sf_mm, half + 1)
                g4 = grep.rearrange("p (r s) t -> p r s t", s=3)
                for s_ in range(3):
                    ins = dve.tensor_tensor(
                        o_gated[:, s_, :].rearrange("p (b r q) -> p b r q", r=HPG, q=NQ),
                        acc[3][:, 0, s_ * P:(s_ + 1) * P].rearrange("p (b c) -> p b c", b=4)[:, :, 0:24]
                        .rearrange("p b (r q) -> p b r q", q=NQ),
                        g4[:, :, s_, bass.ds(half * 16, 16)].rearrange("p r (b q) -> p b r q", q=NQ), ALU.mult)
                own(ins)
                own(dve.tensor_tensor(o_gated[:, 0, :], o_gated[:, 0, :], o_gated[:, 1, :], ALU.add))
                f3 = lambda n: o_gated[:, n, :].rearrange("p (b r q) -> p b r q", r=HPG, q=NQ)
                dve.tensor_tensor(onsaT[:, :, bass.ds(TP + half * 16, 16)].rearrange("p r (b q) -> p b r q", q=NQ),
                                  f3(0), f3(2), ALU.add).then_inc(sf_done, 1)
            own.end(2)
            dve.wait_ge(sf_done, 2)
            own(dve.memset(mem_q, 0.0))
            with dve.Fori(0, 2) as half:
                own.loop(half, 1)
                dve.wait_ge(ms_s, MS + half * 4)
                for h in range(MEM_H):
                    ins = dve.tensor_copy(mem_q[:, :, h, h * NQ:(h + 1) * NQ],
                                          mqT[:, h, bass.ds(TP + half * 16, 16)].rearrange("p (b q) -> p b q", q=NQ))
                ins.then_inc(ms_q, 1)
                dve.wait_ge(ms_s, MS + half * 4 + 4)
                dve.tensor_reduce(small[:, 0:1], acc[0][:, 0, 0:MEM_T], AX, ALU.max, negate=True).then_inc(ms_max, 1)
                dve.wait_ge(ms_exp, MS + half + 1)
                own(dve.reciprocal(small[:, 2:3], small[:, 1:2]))
                dve.wait_ge(ms_pv, MS + half + 1)
                dve.tensor_scalar(mem_o, acc[2][:, 0, :], small[:, 2:3], None, ALU.mult).then_inc(ms_norm, 1)
                dve.wait_ge(ms_ft, half + 1)
                for h in range(MEM_H):
                    ins = dve.tensor_copy(omemT[:, h, bass.ds(TP + half * 16, 16)].rearrange("p (b q) -> p b q", q=NQ),
                                          acc[3][:, 0, h * P:(h + 1) * P].rearrange("p (b c) -> p b c", b=4)[:, :, h * NQ:(h + 1) * NQ])
                ins.then_inc(ms_done, 1)
            own.end(2)

            dve.wait_ge(rw_evicted, N_RW + 2)
            dve.wait_ge(re_back, 16)
            dve.tensor_copy(shift_now[:, :, 0], rwT[:, :, TP - 1])
            own(dve.tensor_copy(shift_now[:, :, 1:], rwT[:, :, TP + NQ - 1:T:NQ]))
            dve.sem_inc(shift_taken, 1)
            dve.wait_ge(rw_in, 48)
            dve.wait_ge(shift_in_sem, 1)
            with dve.Fori(0, N_RW) as n:
                own.loop(n, 4)
                x = rwT[:, bass.ds(n, 1), :].rearrange("p a t -> p (a t)")
                s9 = shift9[:, bass.ds(n, 1), :].rearrange("p a t -> p (a t)")
                own(dve.tensor_tensor(delta[:, 1:T], x[:, 0:T - 1], x[:, 1:T], ALU.subtract))
                own(dve.tensor_tensor(delta[:, 0:1], s9[:, 0:1], x[:, 0:1], ALU.subtract))
                own(dve.tensor_tensor(delta[:, TP:T:NQ], s9[:, 1:], x[:, TP:T:NQ], ALU.subtract))
                own(dve.scalar_tensor_tensor(x, delta, vec[:, bass.ds(n + VEC["mu"], 1)], x, ALU.mult, ALU.add))
            own.end(N_RW)
            dve.sem_inc(xm_done, N_RW)
            h2 = lambda a: a.rearrange("p (b t) -> p b t", b=2)
            for i in range(PAIRS):
                own(dve.tensor_scalar(kkT[:, i, :], kT[:, i, :], v("kk", i), None, ALU.mult))
                if i >= 2:
                    dve.wait_ge(kn_mm, i - 1)
                dve.tensor_tensor(tmp[:, 2 + i % 2, :], kkT[:, i, :], kkT[:, i, :], ALU.mult).then_inc(kn_sq, 1)
                dve.wait_ge(kn_mm, i + 1)
                dve.tensor_scalar(h2(tmp[:, 4 + i % 2, :]), acc[3][:, :, 0:HALF_T], 1e-24, None, ALU.max).then_inc(kn_max, 1)
                dve.wait_ge(kn_root, i + 1)
                own(dve.reciprocal(tmp[:, 4 + i % 2, :], tmp[:, 4 + i % 2, :]))
                own(dve.tensor_tensor(kkT[:, i, :], kkT[:, i, :], tmp[:, 4 + i % 2, :], ALU.mult))
            dve.wait_ge(lo_out, 3 * PAIRS)
            for i in range(PAIRS):
                own(dve.tensor_scalar(zT[:, i, :], zT[:, i, :], -float(np.exp(-0.5)), None, ALU.mult))
                own(dve.tensor_tensor_scan(tmp[:, 1, :], const("reset"), zT[:, i, :], 0.0, ALU.mult, ALU.add))
                dve.tensor_tensor(tmp[:, 5, :], tmp[:, 1, :], zT[:, i, :], ALU.subtract).then_inc(ex_in, 1)
                own(dve.tensor_scalar(delta, bT[:, i, :], -1.0, v("ka", i), ALU.add, ALU.mult))
                own(dve.scalar_tensor_tensor(kT[:, i, :], delta, 1.0, kT[:, i, :], ALU.add, ALU.mult))
                dve.scalar_tensor_tensor(tmp[:, 0, :], rT[:, i, :], v("rk", i), kT[:, i, :], ALU.mult, ALU.mult)\
                   .then_inc(bo_in, 1)
                own(dve.tensor_tensor(bT[:, i, :], bT[:, i, :], kkT[:, i, :], ALU.mult))
                dve.wait_ge(bo_in, i + 1)
                dve.wait_ge(ex_out, i + 1)
                dve.tensor_tensor(bT[:, i, :], bT[:, i, :], tmp[:, 3, :], ALU.mult)
                dve.tensor_tensor(kT[:, i, :], kT[:, i, :], tmp[:, 3, :], ALU.mult)
                dve.tensor_tensor(rT[:, i, :], rT[:, i, :], tmp[:, 2, :], ALU.mult)
                dve.tensor_copy(pend[:, i, 0:NCH], tmp[:, 2, C - 1:TP:C])
                dve.tensor_copy(pend[:, i, NCH:], tmp[:, 2, TP + NQ - 1:T:NQ])
                own(dve.scalar_tensor_tensor(zT[:, i, :], kkT[:, i, :], -1.0, tmp[:, 4, :], ALU.mult, ALU.mult))
                dve.wait_ge(bo_mm, i + 1)
                dve.tensor_tensor(h2(bonusT[:, i, :]), acc[3][:, :, 0:HALF_T], h2(vT[:, i, :]), ALU.mult).then_inc(prep_done, 1)
            both = lambda n: acc[n][:].rearrange("p a c -> p (a c)")
            dve.wait_ge(prep_done, PAIRS)
            dve.memset(S, 0.0).then_inc(s_zero, 1)
            dve.wait_ge(s_zero, 1)

            def chunk(c, n, levels, kind, upto_state):
                sg, st, sx = (SEG[x + kind][0] for x in ("gram_", "tri_", "x2t_"))
                for e in range(2):
                    dve.wait_ge(gram_mm, c * 2 + e + 1)
                    own(dve.tensor_tensor(gram[0:2 * n, e, :, 0:2 * n],
                                          both(2 * e)[0:2 * n, 0:PAIRS * P].rearrange("p (i s) -> p i s", i=PAIRS)[:, :, 0:2 * n],
                                          bc(cst[0:2 * n, sg:sg + 2 * n], 1, PAIRS), ALU.mult))
                    own(dve.tensor_tensor(gram[0:n, e, :, 0:n], gram[0:n, e, :, 0:n], bc(ident[0:n, 0:n], 1, PAIRS), ALU.add))
                    dve.tensor_tensor(XT[0:n, e, :, 0:n], gram[0:n, e, :, 0:n], bc(cst[0:n, sx:sx + n], 1, PAIRS), ALU.mult)\
                       .then_inc(gram_out, 1)
                dve.wait_ge(v_rows, c + 1)
                dve.tensor_copy(uv[n:2 * n], zv[n:2 * n]).then_inc(uv_v, 1)
                for l in range(levels):
                    for e in range(2):
                        dve.wait_ge(y_mm, c * 10 + 2 * l + e + 1)
                        dve.tensor_tensor(Y[0:n, e, :, 0:n],
                                          acc[2 * e][0:n, 0, 0:PAIRS * C].rearrange("p (i s) -> p i s", i=PAIRS)[:, :, 0:n],
                                          bc(cst[0:n, st + l * n:st + (l + 1) * n], 1, PAIRS), ALU.mult).then_inc(y_out, 1)
                    for e in range(2):
                        dve.wait_ge(xt_mm, c * 10 + 2 * l + e + 1)
                        dve.tensor_copy(XT[0:n, e, :, 0:n],
                                        acc[2 * e + 1][0:n, 1, 0:PAIRS * C].rearrange("p (i s) -> p i s", i=PAIRS)[:, :, 0:n])\
                           .then_inc(xt_out, 1)
                upto_state()
                dve.wait_ge(u_mm, c + 1)
                dve.tensor_copy(uv[0:n].rearrange("p a e c -> p (a e c)"), both(2)[0:n, 0:PAIRS * P]).then_inc(u_out, 1)

            with dve.Fori(0, NCH) as it:
                own.loop(it, 6)
                chunk(it, C, 5, "p", lambda: None)
                dve.wait_ge(s_mm, it + 1)
                dve.wait_ge(o_mm, it + 2)
                for e in range(2):
                    rows = slice(e * HD, (e + 1) * HD)
                    ins = dve.tensor_tensor(S[rows, :, e, :], acc[3][rows, 0, 0:PAIRS * C].rearrange("p (i c) -> p i c", i=PAIRS),
                                            S[rows, :, e, :], ALU.add)
                    own(ins)
                for e in range(2):
                    rows = slice(e * HD, (e + 1) * HD)
                    ins = dve.tensor_tensor(S[rows, :, e, :], S[rows, :, e, :],
                                            bc(pend[rows, :, bass.ds(it, 1)].rearrange("p i a -> p (i a)"), 2, C), ALU.mult)
                ins.then_inc(s_out, 1)
            own.end(NCH)
            turn = [0]

            def masked(x):
                for i in range(PAIRS):
                    turn[0] += 1
                    if turn[0] > 2:
                        dve.wait_ge(z_used, turn[0] - 2)
                    dve.tensor_tensor(z_b[:, turn[0] % 2, :].rearrange("p (b t) -> p b t", b=NB),
                                      bc(zr_now[:, 0, i, x * TS:(x + 1) * TS], 1, NB),
                                      const("zmask").rearrange("p (b t) -> p b t", b=NB), ALU.mult).then_inc(z_masked, 1)

            dve.wait_ge(staged, NCH + 1)
            chunk(NCH, TS, 1, "s", lambda: masked(0))
            masked(1)
            dve.wait_ge(o_mm, NCH + 2)
            dve.wait_ge(s_zero, 2)
            for i in range(PAIRS):
                for e in range(2):
                    j = 2 * i + e
                    if j >= 2:
                        dve.wait_ge(uvb_used, j - 1)
                    dve.wait_ge(u_out, NCH + 1)
                    dve.tensor_tensor(uv_b[0:2 * TS, j % 2], bc(uv[0:2 * TS, i, e, :], 1, NB),
                                      bc(const("umask", 2 * TS), 2, C), ALU.mult).then_inc(uvb_done, 1)
                dve.wait_ge(uvb_used, 2 * i + 2)
                for e in range(2):
                    rows = slice(e * HD, (e + 1) * HD)
                    own(dve.tensor_tensor(S_out[rows, i], acc[1][rows, 0, :].rearrange("p (b c) -> p b c", b=NB),
                                          S_s[rows, :, i, e, :], ALU.add))
                    dve.tensor_tensor(S_out[rows, i], S_out[rows, i], bc(pend[rows, i, NCH:], 2, C), ALU.mult)\
                       .then_inc(wkv_done, 1)
            for i in range(PAIRS):
                y, d = zT[:, i, :], kkT[:, i % 2, :]
                dve.wait_ge(gn_mean, PAIRS + i + 1)
                dve.scalar_tensor_tensor(h2(d), acc[0][:, :, 0:HALF_T], -1.0 / HD, h2(y), ALU.mult, ALU.add).then_inc(gn_diff, 1)
                dve.wait_ge(gn_var, 3 * PAIRS + i + 1)
                dve.tensor_scalar(h2(kkT[:, 4, :]), acc[1][:, :, 0:HALF_T], 1.0 / HD, GN_EPS, ALU.mult, ALU.add).then_inc(gn_max, 1)
                dve.wait_ge(gn_root, PAIRS + i + 1)
                own(dve.reciprocal(kkT[:, 4, :], kkT[:, 4, :]))
                own(dve.tensor_tensor(y, d, kkT[:, 4, :], ALU.mult))
                own(dve.tensor_scalar(y, y, v("lng", i), v("lnb", i), ALU.mult, ALU.add))
                own(dve.tensor_tensor(y, y, bonusT[:, i, :], ALU.add))
                dve.tensor_tensor(y, y, gT[:, i, :], ALU.mult).then_inc(gn_done, 1)

            dve.wait_ge(wkv_stored, 48)
            own(dve.memset(ones, 1.0))
            for m in range(KT):
                half, n = divmod(m, KT // 2)
                dve.wait_ge(sig_in[half], 16)
                for g in range(3):
                    if g < 2:
                        dve.wait_ge(mg_mm, 2 * m + g + 1)
                    else:
                        dve.wait_ge(slot_used, S_MERGE + 2 * m + 2)
                    dst = prod if g else mT[:, m, :]
                    dve.tensor_tensor(h2(dst), acc[(3 * m + g) % 4][:, :, 0:HALF_T],
                                      h2((sig_b if half else sig_a)[:, n, g, :]), ALU.mult).then_inc(mg_part, 1)
                    if g:
                        dve.wait_ge(mg_part, 3 * m + g + 1)
                        own(dve.tensor_tensor(mT[:, m, :], mT[:, m, :], prod, ALU.add))
            dve.sem_inc(mg_part, 1)

            def norm(done, gain, dst, count):
                for j in range(KT):
                    count(j)
                    dve.tensor_tensor(h2(x1T[:, j, :]), acc[j % 2][:, :, 0:HALF_T], h2(x1T[:, j, :]), ALU.add)\
                       .then_inc(x1_added, 1)
                dve.wait_ge(sqT_summed, done + KT)
                dve.tensor_scalar(h2(rms), acc[3][:, :, 0:HALF_T], 1.0 / D, RMS_EPS, ALU.mult, ALU.add)\
                   .then_inc(rms_in, 1)
                dve.wait_ge(rms_root, done // KT + 1)
                own(dve.reciprocal(rms, rms))
                for j in range(KT):
                    dve.scalar_tensor_tensor(dst[:, j, :], x1T[:, j, :], v(gain, j), rms, ALU.mult, ALU.mult)\
                       .then_inc(hf_done, 1)

            dve.wait_ge(xT_in, 16)
            norm(0, "ffn", hT, lambda j: dve.wait_ge(slot_used, S_OUT + j + 1))
            dve.sem_inc(ff_done, 2)

            def ff_tile(n, it=None):
                dve.wait_ge(slot_used, S_GU + 2 * n + 2 if it is None else it * 20 + S_GU + 2 * n + 2)
                dve.wait_ge(gu_act, n + 3 if it is None else it * 10 + n + 3)
                t = n if it is None else it * 10 + n
                f = ffT[:, bass.ds(t, 1), :].rearrange("p a (b t) -> p (a b) t", b=2)
                dve.tensor_tensor(f, acc[2 + n % 2][:, :, 0:HALF_T], f, ALU.mult).then_inc(ff_done, 1)

            with dve.Fori(0, FFT // 10) as it:
                for n in range(10):
                    ff_tile(n, it)
            for n in range(FFT // 10 * 10, FFT):
                ff_tile(n)

            def down(j):
                if j % 4 == 3:
                    dve.wait_ge(slot_used, S_DOWN + FFT * (j + 1) // KT)
                else:
                    dve.wait_ge(dn_mm, j + 1 - (j + 1) // 4)

            norm(KT, "final", x1T, down)


def kernel(**inputs):
    import concourse.bacc as bacc
    from concourse.bass_utils import run_bass_kernel_spmd as run

    nc = bacc.Bacc("TRN2", target_bir_lowering=False, num_devices=1)
    arrays = {name: np.ascontiguousarray(a) for name, a in layout(inputs).items()}
    aps = {name: nc.dram_tensor(name, a.shape, mybir.dt.from_np(a.dtype), kind="ExternalInput").ap()
           for name, a in arrays.items()}
    for name, shape in OUTS.items():
        aps[name] = nc.dram_tensor(name, shape, F32, kind="ExternalOutput").ap()
    program(nc, aps)
    r = run(nc, [arrays], core_ids=[0])
    return results({name: r.results[0][name] for name in OUTS})
```

```python
import numpy as np
from contextlib import ExitStack
import concourse.bass as bass
from concourse import mybir

F32 = mybir.dt.float32
I32 = mybir.dt.int32
ALU = mybir.AluOpType
ACT = mybir.ActivationFunctionType
AX = mybir.AxisListType.X

P = 128
D = 1024
KT = D // P
TP, TS = 512, 32
T = TP + TS
HALF_T = T // 2
QT = TP // P
HD = 64
NG, HPG = 2, 6
NB, NQ = 8, 4
MEM_H, MEM_T = 4, 256
PAST, PAGE = 1024, 128
NPG = PAST // PAGE
N_PHYS = NB * NPG * 5 // 4
WIN = 512
CMP = 16
NC_P = TP // CMP - 1
NC_S = PAST // CMP - 1
PAIRS = 6
C = 64
NCH = TP // C
FF = 2816
FFT = FF // P
RMS_EPS = 1e-6
GN_EPS = 64e-5
NEG = -1e30

T_Q, T_KV, T_MQ, N_IN = 0, 6, 12, 16
R_R, R_K, R_V, R_LORA, R_GD, N_RW = 0, 6, 12, 18, 19, 20
T_CK, T_CV, T_SK, T_SV, T_WK, T_WV = range(T_KV, T_KV + 6)

RING = 5
S_IN = 0
S_MEM = S_IN + N_IN
S_RW = S_MEM + KT
S_MG = S_RW + N_RW
S_MERGE = S_MG + 3 * KT
MERGE_K = 6 + 6 + 4
S_OUT = S_MERGE + MERGE_K
S_GU = S_OUT + KT
S_DOWN = S_GU + 2 * FFT
N_SLOTS = S_DOWN + FFT

SEG = {}


def _segments():
    at = 0
    for name, n in (("ident", P), ("causal", P), ("cmpmask", QT * NC_P), ("cmp01", QT * NC_P),
                    ("newmask", 2 * TS), ("winfirst", NQ), ("winnew", 2 * TS), ("headsum", P), ("samequery", P),
                    ("blockno", 14), ("gram_p", 2 * C), ("tri_p", 5 * C), ("x2t_p", C),
                    ("gram_s", 2 * TS), ("tri_s", 1 * TS), ("x2t_s", TS), ("zmask", NB * TS), ("umask", NB),
                    ("reset", T)):
        SEG[name] = (at, at + n)
        at += n
    return at


N_CONST = _segments()


def constants():
    c = np.zeros((P, N_CONST), np.float32)

    def put(name, a):
        lo, hi = SEG[name]
        a = np.asarray(a, np.float32)
        a = a.reshape(a.shape[0], -1)
        assert a.shape[1] == hi - lo, (name, a.shape)
        c[:a.shape[0], lo:hi] = a

    p = np.arange(P)[:, None]
    put("ident", np.eye(P))
    put("causal", np.where(np.arange(P)[None] <= p, 0, NEG))
    ends = np.arange(NC_P) * CMP + 2 * CMP - 1
    seen = ends[None, None] <= (np.arange(QT)[None, :, None] * P + p[:, :, None])
    put("cmpmask", np.where(seen, 0, NEG))
    put("cmp01", seen)
    row_b, row_q, row_real = p // 32, p % 4, (p % 32) < HPG * NQ
    tok = np.arange(TS)[None]
    new = [(tok // NQ == row_b + 4 * half) & (tok % NQ <= row_q) for half in range(2)]
    put("newmask", np.concatenate([np.where(m, 0, NEG) for m in new], 1))
    put("winfirst", np.where(np.arange(NQ)[None] >= row_q, 0, NEG))
    put("winnew", np.concatenate([np.where(m, 0, NEG) for m in new], 1))
    put("headsum", (p // HD) == (np.arange(P)[None] // HD))
    same = (row_b == row_b.T) & (row_q == row_q.T) & row_real & row_real.T
    put("samequery", same)
    put("blockno", np.tile(np.arange(1, 15), (P, 1)))

    def gram(n, allowed):
        s, t = np.arange(n)[:, None], np.arange(n)[None]
        strict, incl = allowed(s, t) & (s < t), allowed(s, t) & (s <= t)
        return np.block([[strict, incl], [strict, incl]])

    def tri(n, allowed, levels):
        t, s = np.arange(n)[:, None], np.arange(n)[None]
        out = []
        for b in levels:
            off = (t // (2 * b) == s // (2 * b)) & ((t // b) % 2 == 1) & ((s // b) % 2 == 0)
            out.append(off & allowed(s, t) | (t == s))
        out = np.concatenate(out, 1)
        return np.concatenate([out, out])

    every = lambda s, t: (s >= 0) & (t >= 0)
    mine = lambda s, t: s // NQ == t // NQ
    put("gram_p", gram(C, every))
    put("tri_p", tri(C, every, (2, 4, 8, 16, 32)))
    put("x2t_p", np.tile(tri(C, every, (1,))[:C].T, (2, 1)))
    put("gram_s", gram(TS, mine))
    put("tri_s", tri(TS, mine, (2,)))
    put("x2t_s", np.tile(tri(TS, mine, (1,))[:TS].T, (2, 1)))
    put("zmask", np.tile((np.arange(TS)[None] // NQ == np.arange(NB)[:, None]).reshape(1, -1), (P, 1)))
    put("umask", ((np.arange(2 * TS)[:, None] % TS) // NQ) == np.arange(NB)[None])
    t = np.arange(T)
    put("reset", np.tile(np.where(t < TP, t % C != 0, (t - TP) % NQ != 0), (P, 1)))
    sel = np.zeros((36, HPG, 3, NG, HD), np.float32)
    for g in range(NG):
        for r in range(HPG):
            for br in range(3):
                sel[g * 18 + r * 3 + br, r, br, g] = 1
    return c, np.ascontiguousarray(sel.reshape(36, 18 * P))


def tiles(w):
    k, m = w.shape
    return w.reshape(k // P, P, m // P, P).transpose(2, 1, 0, 3).reshape(m // P, P, k)


def layout(i):
    f = lambda n: np.asarray(i[n])
    w = f("w_in")[0]
    at = np.cumsum([0, 768, 768, 36, 2560, 512, 3072])
    wq, wkv, wgn, wr, wmq, wmg = (w[:, a:b] for a, b in zip(at[:-1], at[1:]))
    pairs = lambda a: a.reshape(a.shape[0], NG, HPG, HD).transpose(0, 2, 1, 3).reshape(a.shape[0], -1)
    wq = pairs(wq)
    w_nsa = pairs(f("w_o_nsa")[0].T).T
    stream = np.empty((N_SLOTS, P, D), np.float32)
    stream[S_IN:S_MEM] = np.concatenate([tiles(np.ascontiguousarray(a)) for a in (wq, wkv, wmq)])
    stream[S_RW:S_MG] = tiles(np.ascontiguousarray(wr))
    stream[S_MEM:S_RW] = f("w_mem_kv")[0].reshape(KT, P, D)
    mg = tiles(wmg).reshape(3, KT, P, D)
    stream[S_MG:S_MERGE] = mg.transpose(1, 0, 2, 3).reshape(3 * KT, P, D)
    merge = np.concatenate([tiles(w_nsa), tiles(f("w_o_rwkv")[0]), tiles(f("w_o_mem")[0])], axis=2)
    stream[S_MERGE:S_OUT] = merge.reshape(KT, P, MERGE_K // KT, D).transpose(0, 2, 1, 3).reshape(-1, P, D)
    stream[S_OUT:S_GU] = tiles(f("w_out")[0])
    stream[S_GU:S_DOWN] = np.stack([tiles(f("w_gate")[0]), tiles(f("w_up")[0])], 1).reshape(-1, P, D)
    down = tiles(f("w_down")[0]).reshape(KT, P, FFT, P).transpose(0, 2, 1, 3)
    stream[S_DOWN:] = down.reshape(FFT, KT, P, P).transpose(0, 2, 1, 3).reshape(FFT, P, D)
    cols = [f(n).reshape(-1) for n in ("attn_norm", "mem_norm", "ffn_norm", "rwkv_mu", "rwkv_w0", "rwkv_a0",
                                          "rwkv_kk", "rwkv_ka", "rwkv_rk", "rwkv_ln_g", "rwkv_ln_b",
                                       "final_norm")]
    vec = np.concatenate([a.reshape(-1, P).T for a in cols], 1)
    chunks = lambda n: f(n)[0].reshape(N_PHYS, PAGE // CMP, CMP, P).transpose(0, 3, 2, 1).reshape(N_PHYS, P, PAGE)
    pages = np.stack([chunks("cache_cmp_k"), chunks("cache_cmp_v"),
                      f("cache_slc_k")[0].reshape(N_PHYS, PAGE, P).transpose(0, 2, 1),
                      f("cache_slc_v")[0].reshape(N_PHYS, PAGE, P)], 2)
    w1 = np.stack([f(f"cmp_w1_{n}")[0].reshape(2, CMP, HD, HD).transpose(2, 1, 0, 3) for n in "kv"], 1)
    x = np.concatenate([f("x_prompt")[0], f("x_sample").reshape(TS, D)])
    return {
        "x_all": x,
        "x_T": x.T.reshape(KT, P, T).transpose(1, 0, 2),
        "mem_x": f("mem_prompt")[0],
        "w_stream": stream,
        "w_gates": wgn.reshape(KT, P, 36).transpose(1, 0, 2),
        "vectors": vec,
        "consts": constants()[0],
        "gate_spread": constants()[1],
        "pages": pages,
        "page_table": f("page_table").reshape(1, NB * NPG),
        "win_kT": f("cache_win_k")[0].reshape(NB, WIN, P).transpose(0, 2, 1),
        "win_v": f("cache_win_v")[0].reshape(NB, WIN, P),
        "mem_kT": f("cache_mem_k")[0].transpose(0, 3, 2, 1),
        "mem_v": f("cache_mem_v")[0].reshape(NB, MEM_T, MEM_H * P),
        "shift_in": f("state_rwkv_shift")[0].reshape(NB, 20, P).transpose(2, 1, 0),
        "state_in": f("state_rwkv_wkv")[0].reshape(NB, PAIRS, 2, HD, HD).transpose(2, 4, 0, 1, 3).reshape(P, NB, PAIRS, HD),
        "cmp_w1": w1.reshape(HD, 2, CMP * P),
        "cmp_w1_rows": np.stack([f(f"cmp_w1_{n}")[0].reshape(16, P, HD).transpose(1, 0, 2) for n in "kv"], 1),
        "cmp_pe": np.stack([f(f"cmp_pe_{n}")[0].reshape(16, P).T for n in "kv"], 1),
        "cmp_b1": np.stack([f(f"cmp_b1_{n}")[0] for n in "kv"], 1),
        "cmp_w2": np.stack([f(f"cmp_w2_{n}")[0] for n in "kv"], 1),
        "lora_w": np.concatenate([f("rwkv_w2")[0], f("rwkv_a2")[0]]),
        "lora_g": f("rwkv_g2")[0],
    }


VEC = {}
N_VEC = 0
for _n, _k in (("attn", 8), ("mem", 8), ("ffn", 8), ("mu", 20), ("w0", 6), ("a0", 6), ("kk", 6), ("ka", 6), ("rk", 6),
               ("lng", 6), ("lnb", 6), ("final", 8)):
    VEC[_n] = N_VEC
    N_VEC += _k

OUTS = {
    "yT": (P, KT, T),
    "kvT": (6, P, T),
    "shift_out": (P, 20, 1 + NB),
    "wkv_p": (P, PAIRS, HD),
    "wkv_s": (P, PAIRS, NB, HD),
    "mem_kv": (MEM_T, D),
    "win_kT_out": (NB, P, WIN),
    "win_v_out": (NB, WIN, P),
}


def results(r):
    y = r["yT"].transpose(2, 1, 0).reshape(T, D)
    kv = r["kvT"].transpose(0, 2, 1)
    prompt = [kv[n, :TP].reshape(1, 1, TP, NG, HD) for n in range(6)]
    new = [kv[n, TP:].reshape(1, NB, NQ, NG, HD) for n in range(4)]
    sh = r["shift_out"].transpose(2, 1, 0).reshape(1 + NB, 2560)
    wkv_p = r["wkv_p"].reshape(2, HD, PAIRS, HD).transpose(2, 0, 3, 1).reshape(1, 1, 12, HD, HD)
    wkv_s = r["wkv_s"].reshape(2, HD, PAIRS, NB, HD).transpose(3, 2, 0, 4, 1).reshape(1, NB, 12, HD, HD)
    mkv = r["mem_kv"].reshape(1, 1, MEM_T, 2, MEM_H, P)
    wk = r["win_kT_out"].transpose(0, 2, 1).reshape(1, NB, WIN, NG, HD)
    wv = r["win_v_out"].reshape(1, NB, WIN, NG, HD)
    return (y[:TP].reshape(1, TP, D), y[TP:].reshape(NB, NQ, D), *prompt,
            sh[0].reshape(1, 1, 2560), wkv_p, mkv[:, :, :, 0], mkv[:, :, :, 1], *new,
            wk, wv, sh[1:].reshape(1, NB, 2560), wkv_s)


def bc(ap, axis, n):
    a = ap.unsqueeze(axis)
    shape = list(a.shape)
    shape[axis] = n
    return a.to_broadcast(shape)


class Steps:

    def __init__(self, engine, sem):
        self.engine, self.sem, self.base, self.n, self.it = engine, sem, 0, 0, None

    def loop(self, it, each):
        self.it, self.each, self.start = it, each, self.base + self.n
        self.base, self.n = self.start, 0

    def end(self, times):
        assert self.n == self.each, (self.n, self.each)
        self.base, self.n, self.it = self.start + times * self.each, 0, None

    def __call__(self, instruction):
        instruction.then_inc(self.sem, 1)
        self.n += 1
        at = self.base + self.n
        self.engine.wait_ge(self.sem, at if self.it is None else self.it * self.each + at)


def program(nc, A):
    with ExitStack() as ctx:
        def sb(name, shape, dt=F32):
            return ctx.enter_context(nc.sbuf_tensor("sb_" + name, shape, dt))

        def sem(name):
            return ctx.enter_context(nc.semaphore(name))

        acc = [ctx.enter_context(nc.psum_tensor(f"acc{n}", [P, 2, 512], F32)) for n in range(4)]
        cst = sb("cst", [P, N_CONST])
        vec = sb("vec", [P, N_VEC])
        wgn = sb("wgn", [P, KT, 36])
        ring = sb("ring", [P, RING, D])
        hT = sb("hT", [P, KT, T])
        onsaT = sb("onsaT", [P, HPG, T])
        omemT = sb("omemT", [P, MEM_H, T])
        gates_tm = sb("gates_tm", [P, QT + 1, 36])
        gates_s = sb("gates_s", [36, TS])
        stat = sb("stat", [P, 24])
        work = sb("work", [P, 35200])
        at = [0]

        def region(start, *shape):
            if start is None:
                start = at[0]
            n = int(np.prod(shape))
            at[0] = start + n
            assert at[0] <= 35200, at[0]
            ap = work[:, start:start + n]
            names = "abcd"[:len(shape)]
            if len(shape) == 1:
                return ap
            return ap.rearrange(f"p ({' '.join(names)}) -> p {' '.join(names)}",
                                **dict(zip(names[1:], shape[1:])))

        def const(name, rows=P):
            lo, hi = SEG[name]
            return cst[0:rows, lo:hi]

        def v(name, k, n=1):
            return vec[:, VEC[name] + k:VEC[name] + k + n]

        ident = const("ident")

        qT = region(0, 6, T)
        kvT = region(None, 6, T)
        mqT = region(None, 4, T)
        in_all = region(0, N_IN, T)
        att0 = at[0]
        x_tm = region(att0, 7, D)
        junk = region(None, D)
        memT = region(None, KT, MEM_T)
        mem_tm = region(at[0], 2, D)
        w1 = region(None, 2, CMP, P)
        w1_rows = region(None, 2, 16, HD)
        pe_cols = region(None, 2, 16)
        b1 = region(None, 2)
        w2 = region(None, 2, HD)
        att1 = at[0]
        v_tm = region(att0, 2, QT + 1, P)
        mkT = region(None, MEM_H, MEM_T)
        u_sb = region(None, NG, 2, TS)
        hid = region(None, 2, NG, TS)
        kcT = region(None, TS)
        vc = region(None, P)
        q_now = region(None, TP)
        c_shift = region(None, HPG, NC_P)
        c_prob = region(None, HPG, NC_P)
        c_probT = region(None, HPG, P)
        q_pad = [q_now, c_probT.rearrange("p a c -> p (a c)")[:, 0:TP]]
        o_tm = region(None, QT, HPG, P)
        assert at[0] <= att0 + 8 * D
        probs = region(att1, 2, 2, TP)
        rw_now = region(att1, 2, T)
        probsT = region(att1 + 4 * TP, 2, TP)
        m_prob = region(None, MEM_H, MEM_T)
        m_probs = [m_prob, probs.rearrange("p a b c -> p (a b c)")[:, 0:MEM_H * MEM_T].rearrange("p (h t) -> p h t", h=MEM_H)]
        m_probT = region(None, MEM_H * 2, P)
        small = sb("small", [P, 96])
        pre_bias = small[:, 94:96]
        k_pages = region(att0 + 2 * (QT + 1) * P, 2, NPG, 3, P)
        v_pages = region(None, 4, NPG, P)
        u_s = region(None, NG, 2, HD)
        hid_s = region(None, 2, NG, HD)
        kc_s = region(None, HD)
        assert at[0] <= att0 + 7 * D + D + KT * MEM_T + 2 * D
        win_v = region(att0 + 8 * D + KT * MEM_T + 2 * D + 2 * CMP * P, 4, WIN // P, P)
        win_k = region(att1, 2, WIN)
        W0, WN0, C0, N0, S0 = 0, WIN, WIN + TS, WIN + TS + NC_S, WIN + 2 * TS + NC_S
        scores = region(None, NG, S0 + PAST)
        assert att1 + 2 * WIN + NG * (S0 + PAST) + 15 * P + 4 * P + 18 * TS <= 34656
        sprobT = region(None, 15, P)
        vc_s = region(None, 4, P)
        grep = region(None, 3 * HPG, TS)
        spread = region(att0 + 2 * (QT + 1) * P + 2 * NPG * 3 * P, 3 * HPG, P)
        o_rows = region(34656, 6, HD)
        page_ids = region(None, NB * NPG)[0:1].bitcast(I32)
        q_half = cst[:, SEG["causal"][0]:SEG["causal"][0] + NG * 4 * 32].rearrange("p (g b n) -> p g b n", g=NG, b=4)
        imp = wgn[:].rearrange("p k c -> p (k c)")[:, 0:NG * 130].rearrange("p (g n) -> p g n", g=NG)
        o_gated = o_rows.rearrange("p a b -> p (a b)")[:, 0:288].rearrange("p (s x) -> p s x", s=3)
        mem_k = region(att0 + 2 * (QT + 1) * P, 2, MEM_H, MEM_T)
        mem_q = region(None, 4, MEM_H, 32)
        mem_v = region(att0 + 2 * (QT + 1) * P + 2 * NPG * 3 * P, 4, 2, MEM_H * P)
        mem_p = region(att1, MEM_T)
        mem_pT = region(None, 2, P)
        mem_o = region(None, MEM_H * P)

        rwT = region(0, N_RW, T)
        rT, kT, vT = rwT[:, R_R:R_R + PAIRS], rwT[:, R_K:R_K + PAIRS], rwT[:, R_V:R_V + PAIRS]
        zT = region(None, PAIRS, T)
        R_BT = at[0]
        bT = region(None, PAIRS, T)
        gT = region(None, PAIRS, T)
        bonusT = region(None, PAIRS, T)
        scan0 = at[0]
        kkT = region(scan0, PAIRS, T)
        tmp = region(None, 6, T)
        delta = region(None, T)
        gate_now = region(None, 2, T)
        lw_w = region(None, 6 * P)
        lw_g = region(None, 6 * P)
        shift9 = region(None, 20, 1 + NB)
        shift_now = region(None, 20, 1 + NB)
        pend = cst[:, SEG["cmpmask"][0]:SEG["cmpmask"][0] + PAIRS * (NCH + NB)]\
            .rearrange("p (a c) -> p a c", a=PAIRS)
        bk_now = region(scan0, 2, PAIRS, 2 * C)
        zr_now = region(None, 2, PAIRS, 2 * C)
        v_now = region(None, PAIRS, 2 * C)
        gram = region(None, 2, PAIRS, 2 * C)
        XX = region(None, 2, 2, 3 * C).rearrange("p s x (k c) -> p s x k c", c=C)
        X = lambda i: XX[:, i // 3, 0, i % 3, :]
        XT = lambda i: XX[:, i // 3, 1, i % 3, :]
        Y = region(None, PAIRS, C)
        w_tm = region(None, PAIRS, C)
        bk_tm = region(None, PAIRS, P)
        uv = region(None, PAIRS, 2, C)
        S = region(None, PAIRS, C)
        S_s = region(0, NB, PAIRS, C)
        S_out = region(6144, PAIRS, NB, C)
        uv_b = region(None, 2, NB, C)
        z_b = region(None, 2, NB * TS)
        mT = region(0, KT, T)
        sig_a = region(None, KT // 2, 3, T)
        x1T = region(R_BT, KT, T)
        ffT = region(None, FFT, T)
        sig_b = region(R_BT + KT * T, KT // 2, 3, T)
        at[0] = R_BT + (KT + FFT) * T
        prod = region(None, T)
        sqT = region(None, 2, T)
        rms = region(None, T)
        ones = region(None, P)
        consts_in, x_in = sem("consts_in"), [sem("x_in"), sem("mem_x_in")]
        w_in_slot = [sem(f"w_in_slot{n}") for n in range(RING)]
        slot_used = sem("slot_used")
        dve_own, act_own, pool_own = sem("dve_own"), sem("act_own"), sem("pool_own")
        pe_passed = sem("pe_passed")
        squares, means, roots, scaled, turned, hT_ready = map(
            sem, ("squares", "means", "roots", "scaled", "turned", "hT_ready"))
        in_evicted = sem("in_evicted")
        gates_mm, gates_done = sem("gates_mm"), sem("gates_done")
        mem_done = sem("mem_done")
        stored = sem("stored")
        rw_in, rw_evicted, shift_in_sem, shift_taken, shift_stored, xm_done = map(
            sem, ("rw_in", "rw_evicted", "shift_in", "shift_taken", "shift_stored", "xm_done"))
        lo_act, lo_mm, lo_out, kn_sq, kn_mm, kn_max, kn_root, ex_in, ex_out, bo_in, bo_mm, prep_done = map(
            sem, ("lo_act", "lo_mm", "lo_out", "kn_sq", "kn_mm", "kn_max", "kn_root", "ex_in", "ex_out",
                  "bo_in", "bo_mm", "prep_done"))
        staged, tb_mm, tv_mm, bk_rows, v_rows, gram_mm, gram_out, x_mm, x_out, y_mm, y_out = map(
            sem, ("staged", "tb_mm", "tv_mm", "bk_rows", "v_rows", "gram_mm", "gram_out", "x_mm", "x_out",
                  "y_mm", "y_out"))
        w_mm, w_out, w_out_odd, u_mm, u_out, u_out_odd, o_mm, s_mm, s_out, yt_out, s_zero = map(
            sem, ("w_mm", "w_out", "w_out_odd", "u_mm", "u_out", "u_out_odd", "o_mm", "s_mm", "s_out", "yt_out", "s_zero"))
        states_in, z_masked, z_used, uvb_done, uvb_used, wkv_done = map(
            sem, ("states_in", "z_masked", "z_used", "uvb_done", "uvb_used", "wkv_done"))
        wkv_stored = sem("wkv_stored")
        gn_mean, gn_diff, gn_max, gn_root, gn_var, gn_sq = kn_mm, kn_sq, kn_max, kn_root, lo_mm, lo_out
        gn_done = sem("gn_done")
        re_back = sem("re_back")
        spilled, sig_in = [sem("spilled0"), sem("spilled1")], [sem("sig_in0"), sem("sig_in1")]
        mg_sig, mg_mm, mg_part, xT_in, x1_added, sqT_made, sqT_summed, rms_in, rms_root, hf_done, gu_act, ff_done, dn_mm = map(
            sem, ("mg_sig", "mg_mm", "mg_part", "xT_in", "x1_added", "sqT_made", "sqT_summed", "rms_in", "rms_root",
                  "hf_done", "gu_act", "ff_done", "dn_mm"))
        ids_in = spread_in = sem("ids_in")
        k_in, v_in = [sem("k_in0"), sem("k_in1")], sem("v_in")
        (su_mm, su_done, sp_mm, sp_done, sk_mm, sk_done, sv_done, ss_a, ss_b, ss_act, ss_dve, sq_done, sg_mm, sg_done) = map(
            sem, ("su_mm", "su_done", "sp_mm", "sp_done", "sk_mm", "sk_done", "sv_done", "ss_a", "ss_b", "ss_act",
                  "ss_dve", "sq_done", "sg_mm", "sg_done"))
        sx_max, sx_exp, si_in, si_mm, st_mm, st_dve, st_act, so_mm, so_done, sf_mm, sf_done = map(
            sem, ("sx_max", "sx_exp", "si_in", "si_mm", "st_mm", "st_dve", "st_act", "so_mm", "so_done", "sf_mm",
                  "sf_done"))
        K_IN, V_IN = 4 * 16 * (NPG + 1), NB * 16 * (NPG + 1)
        ms_q, ms_norm, ms_ft = sem("ms_q"), sem("ms_norm"), sem("ms_ft")
        cmp_in = sem("cmp_in")
        rows_mm, rows_done = sem("rows_mm"), sem("rows_done")
        q_scaled = sem("q_scaled")
        cp_mm, cp_done = sem("cp_mm"), sem("cp_done")
        cs_mm, cs_shift, cs_exp, cs_prob, cs_turn, cs_copied, cs_out, cs_o = map(
            sem, ("cs_mm", "cs_shift", "cs_exp", "cs_prob", "cs_turn", "cs_copied", "cs_out", "cs_o"))
        at_q, at_s, at_max, at_exp, at_turn, at_cs, at_cw, at_pv, at_o = map(
            sem, ("at_q", "at_s", "at_max", "at_exp", "at_turn", "at_cs", "at_cw", "at_pv", "at_o"))
        ot_mm, ot_done = sem("ot_mm"), sem("ot_done")
        ma_s, ma_max, ma_exp, ma_prob, ma_turn, ma_copied, ma_pv, ma_done = (
            cs_mm, cs_shift, cs_exp, cs_prob, cs_turn, cs_copied, cs_out, cs_o)
        mk_in, mv_in = k_in, v_in
        ms_s, ms_max, ms_exp, ms_turn, ms_copied, ms_pv, ms_done = (
            cs_mm, cs_shift, cs_exp, cs_turn, cs_copied, cs_out, cs_o)
        MA, MS = NG * QT, NG * QT + QT
        n_stored = [0]
        RW_EARLY = 12
        GATES_FIRST = 9
        rw_early = nc.dram_tensor("rwkv_features", (P, RW_EARLY, T), F32, kind="Internal").ap()
        gates_out = nc.dram_tensor("branch_gates", (KT, P, 3, T), F32, kind="Internal").ap()

        kv_stored, mem_stored, win_stored = sem("kv_stored"), sem("mem_stored"), sem("win_stored")

        def store(instruction):
            instruction.then_inc(stored, 16)
            n_stored[0] += 16

        block = ctx.enter_context(nc.Block())

        QUARTERS = ((0, 0), (1, 1), (0, 1), (1, 0))
        NPC = PAGE // CMP
        CMP_UNITS = [(g, t) for g in range(NG) for t in range(QT)]
        ATT_UNITS = [(g, t) for t in range(QT) for g in range(NG)]

        @block.sync
        def _(sp):
            def load(n, s, wait=None):
                if wait is not None:
                    sp.wait_ge(slot_used, wait)
                sp.dma_start(ring[:, s, :], A["w_stream"][n]).then_inc(w_in_slot[s], 16)

            def stream(first, last):
                n = first
                while n < last and n % RING:
                    load(n, n % RING, n - RING + 1 if n >= RING else None)
                    n += 1
                rounds = (last - n) // RING
                if n == 0 and rounds:
                    for s in range(RING):
                        load(s, s)
                    n, rounds = RING, rounds - 1
                if rounds > 0:
                    with sp.Fori(n // RING, n // RING + rounds) as i:
                        for s in range(RING):
                            sp.wait_ge(slot_used, (i - 1) * RING + s + 1)
                            sp.dma_start(ring[:, s, :], A["w_stream"][bass.ds(i * RING + s, 1)]
                                         .rearrange("a p c -> p (a c)")).then_inc(w_in_slot[s], 16)
                    n += rounds * RING
                for n in range(n, last):
                    load(n, n % RING, n - RING + 1)

            sp.wait_ge(x_in[0], 16 * (QT + 1))
            sp.dma_start(page_ids, A["page_table"]).then_inc(ids_in, 16)
            stream(0, S_RW + RW_EARLY + RING)
            sp.wait_ge(ids_in, 16)
            sp.wait_ge(mem_stored, 16)
            sp.wait_ge(ma_done, MA + QT)
            sp.dma_start(spread[0:36], A["gate_spread"].rearrange("p (a c) -> p a c", c=P)).then_inc(spread_in, 16)
            sp.wait_ge(sg_mm, 1)
            with sp.Fori(0, 2) as half:
                for b in range(4):
                    if b >= 2:
                        sp.wait_ge(ss_b, half * 4 + b - 1)
                    else:
                        sp.wait_ge(ss_b, half * 4)
                    sp.dma_start(win_k[:, b % 2, :], A["win_kT"][bass.ds(half * 4 + b, 1)]
                                 .rearrange("a p c -> p (a c)")).then_inc(k_in[b % 2], 16)
                    with sp.Fori(0, NPG) as n:
                        page = sp.value_load(page_ids[0:1, bass.ds((half * 4 + b) * NPG + n, 1)], min_val=0,
                                             max_val=N_PHYS - 1)
                        sp.dma_start(k_pages[:, b % 2, bass.ds(n, 1)].rearrange("p a k c -> p (a k) c"),
                                     A["pages"][bass.ds(page, 1), :, 0:3, :].rearrange("a p k c -> p (a k) c"))\
                          .then_inc(k_in[b % 2], 16)
                sp.wait_ge(so_mm, half * 2)
                for b in range(4):
                    sp.dma_start(win_v[:, b], A["win_v"][bass.ds(half * 4 + b, 1)]
                                 .rearrange("a (k p) c -> p (a k) c", p=P)).then_inc(v_in, 16)
                    with sp.Fori(0, NPG) as n:
                        page = sp.value_load(page_ids[0:1, bass.ds((half * 4 + b) * NPG + n, 1)], min_val=0,
                                             max_val=N_PHYS - 1)
                        sp.dma_start(v_pages[:, b, bass.ds(n, 1)].rearrange("p a c -> p (a c)"),
                                     A["pages"][bass.ds(page, 1), :, 3, :].rearrange("a p c -> p (a c)"))\
                          .then_inc(v_in, 16)
            with sp.Fori(0, 2) as half:
                sp.wait_ge(sf_done, 2)
                sp.wait_ge(ms_pv, MS + half)
                for b in range(4):
                    if b >= 2:
                        sp.wait_ge(ms_s, MS + half * 4 + b - 1)
                    else:
                        sp.wait_ge(ms_s, MS + half * 4)
                    sp.dma_start(mem_k[:, b % 2], A["mem_kT"][bass.ds(half * 4 + b, 1)]
                                 .rearrange("a p h c -> p (a h) c")).then_inc(mk_in[b % 2], 16)
                    sp.dma_start(mem_v[:, b], A["mem_v"][bass.ds(half * 4 + b, 1)]
                                 .rearrange("a (k p) c -> p (a k) c", p=P)).then_inc(mv_in, 16)
            stream(S_RW + RW_EARLY + RING, N_SLOTS)

        @block.gpsimd
        def _(pool):
            pool.dma_start(cst[:], A["consts"]).then_inc(consts_in, 16)
            pool.dma_start(vec[:], A["vectors"]).then_inc(consts_in, 16)
            pool.dma_start(wgn[:], A["w_gates"]).then_inc(consts_in, 16)
            for g in range(2):
                pool.dma_start(w1[g * HD:(g + 1) * HD].rearrange("p a c h -> p a (c h)"), A["cmp_w1"]).then_inc(cmp_in, 16)
            pool.dma_start(w1_rows, A["cmp_w1_rows"]).then_inc(cmp_in, 16)
            pool.dma_start(pe_cols, A["cmp_pe"]).then_inc(cmp_in, 16)
            pool.dma_start(b1[0:HD], A["cmp_b1"]).then_inc(cmp_in, 16)
            pool.dma_start(w2[0:HD], A["cmp_w2"]).then_inc(cmp_in, 16)
            pool.wait_ge(in_evicted, N_IN + 2)
            pool.dma_start(A["kvT"].rearrange("n p t -> p n t"), kvT).then_inc(kv_stored, 16)
            pool.wait_ge(mem_done, 2)
            pool.dma_start(A["mem_kv"].rearrange("(n p) d -> p n d", p=P), mem_tm).then_inc(mem_stored, 16)
            store(pool.dma_start(A["win_kT_out"][:, :, 0:WIN - NQ], A["win_kT"][:, :, NQ:WIN]))
            store(pool.dma_start(A["win_v_out"][:, 0:WIN - NQ, :], A["win_v"][:, NQ:WIN, :]))
            pool.wait_ge(rows_done, 2)
            pool.dma_start(A["win_kT_out"][:, :, WIN - NQ:WIN].rearrange("b p q -> p b q"),
                           in_all[:, T_WK, TP:T].rearrange("p (b q) -> p b q", q=NQ)).then_inc(win_stored, 16)
            for b in range(NB):
                pool.dma_start(A["win_v_out"][b, WIN - NQ:WIN, :], v_tm[b * NQ:(b + 1) * NQ, 1, QT, :])\
                    .then_inc(win_stored, 16)
            pool.wait_ge(win_stored, 16 * (NB + 1))
            pool.wait_ge(kv_stored, 16)
            pool.wait_ge(mem_stored, 16)
            for n in range(RW_EARLY):
                pool.wait_ge(rw_evicted, n + 1)
                pool.dma_start(rw_early[:, n, :], rw_now[:, n % 2, :]).then_inc(spilled[n % 2], 16)
            pool.wait_ge(sf_done, 2)
            pool.wait_ge(ms_done, MS + 2)
            pool.memset(shift9[:, :, 0], 0.0).then_inc(shift_in_sem, 1)
            for n in range(2):
                pool.wait_ge(spilled[n], 16 * RW_EARLY // 2)
            pool.dma_start(rwT[:, 0:RW_EARLY], rw_early).then_inc(re_back, 16)
            pool.dma_start(lw_w, A["lora_w"]).then_inc(rw_in, 16)
            pool.dma_start(lw_g, A["lora_g"]).then_inc(rw_in, 16)
            pool.dma_start(shift9[:, :, 1:], A["shift_in"]).then_inc(rw_in, 16)
            pool.wait_ge(shift_taken, 1)
            pool.dma_start(A["shift_out"], shift_now).then_inc(shift_stored, 16)
            pool.wait_ge(shift_stored, 16)
            for n in range(3 * KT):
                pool.wait_ge(mg_sig, n + 1)
                pool.dma_start(gates_out[n // 3, :, n % 3, :], gate_now[:, n % 2, :]).then_inc(spilled[n % 2], 16)
            for n in range(2):
                pool.wait_ge(spilled[n], 16 * (RW_EARLY + 3 * KT) // 2)
            pool.wait_ge(prep_done, PAIRS)
            even, odd = slice(0, HD), slice(HD, P)
            own = Steps(pool, pool_own)
            own(pool.memset(v_now[even, :, 0:C], 0.0))
            own(pool.memset(v_now[odd, :, C:2 * C], 0.0))

            def stage(c, par, t0, n):
                pool.wait_ge(o_mm, c)
                pool.wait_ge(tv_mm, c)
                src = lambda a, r: a[r, :, bass.ds(t0, n)]
                pool.tensor_copy(zr_now[:, par, :, 0:n], zT[:, :, bass.ds(t0, n)])
                own(pool.tensor_copy(zr_now[:, par, :, n:2 * n], rT[:, :, bass.ds(t0, n)]))
                for r, b0, k0 in ((odd, n, 0), (even, 0, n)):
                    pool.tensor_copy(bk_now[r, par, :, b0:b0 + n], src(bT, r))
                    pool.tensor_copy(bk_now[r, par, :, k0:k0 + n], src(kT, r))
                    ins = pool.tensor_copy(v_now[r, :, k0:k0 + n], src(vT, r))
                    if r is odd:
                        own(ins)
                ins.then_inc(staged, 1)

            with pool.Fori(0, NCH // 2) as it:
                own.loop(it, 4)
                for par in range(2):
                    stage(it * 2 + par, par, (it * 2 + par) * C, C)
            own.end(NCH // 2)
            pool.wait_ge(tv_mm, NCH)
            own(pool.memset(v_now[even, :, 0:TS], 0.0))
            own(pool.memset(v_now[odd, :, TS:2 * TS], 0.0))
            stage(NCH, 0, TP, TS)
            pool.wait_ge(yt_out, NCH)
            pool.wait_ge(staged, NCH + 1)
            pool.dma_start(S_s, A["state_in"]).then_inc(states_in, 16)
            pool.wait_ge(s_out, NCH)
            pool.dma_start(A["wkv_p"], S).then_inc(wkv_stored, 16)
            pool.wait_ge(wkv_done, 2 * PAIRS)
            pool.dma_start(A["wkv_s"], S_out).then_inc(wkv_stored, 16)
            pool.wait_ge(wkv_stored, 32)
            pool.wait_ge(wkv_stored, 32)
            pool.dma_start(sig_a, gates_out[0:KT // 2].rearrange("m p g t -> p m g t")).then_inc(sig_in[0], 16)
            pool.wait_ge(gn_done, PAIRS)
            pool.dma_start(sig_b, gates_out[KT // 2:].rearrange("m p g t -> p m g t")).then_inc(sig_in[1], 16)
            pool.dma_start(x1T, A["x_T"]).then_inc(xT_in, 16)
            for j in range(KT):
                pool.wait_ge(hf_done, KT + j + 1)
                store(pool.dma_start(A["yT"][:, j, :], x1T[:, j, :]))
            pool.wait_ge(stored, n_stored[0])

        NORM = [(P, n * P, hT, "attn") for n in range(QT)] + [(TS, TP, hT, "attn")] + \
               [(P, n * P, memT, "mem") for n in range(2)]

        @block.tensor
        def _(pe):
            def weights(slot, it=None, each=0):
                s, count = slot % RING, 16 * (slot // RING + 1)
                assert each % RING == 0
                pe.wait_ge(w_in_slot[s], count if it is None else it * (16 * each // RING) + count)
                return ring[:, s, :].rearrange("p (k c) -> p k c", k=KT)

            def settle():
                pe.sem_inc(pe_passed, 1)

            pe.wait_ge(consts_in, 48)
            for i, (rows, t0, dst, gain) in enumerate(NORM):
                pe.wait_ge(scaled, i + 1)
                if i >= 2:
                    pe.wait_ge(hT_ready, i - 1)
                o = acc[i % 2][:].rearrange("p a (k t) -> p (a k) t", t=P)
                for k in range(KT):
                    mm = pe.transpose(o[:, k, 0:rows], x_tm[0:rows, i, k * P:(k + 1) * P], ident[0:rows, 0:rows])
                mm.then_inc(turned, 1)

            pe.wait_ge(hT_ready, 7)
            for n in range(QT):
                for k in range(KT):
                    pe.matmul(acc[2][:, 0, 36 * n:36 * n + 36], hT[:, k, n * P:(n + 1) * P], wgn[:, k, :],
                              start=k == 0, stop=k == KT - 1)
            for k in range(KT):
                mm = pe.matmul(acc[2][0:36, 1, 0:TS], wgn[:, k, :], hT[:, k, TP:T], start=k == 0, stop=k == KT - 1)
            mm.then_inc(gates_mm, 1)

            def in_tile(n, it=None, each=0):
                w = weights(S_IN + n, it, each)
                pe.wait_ge(in_evicted, n + 1 if it is None else it * each + n + 1)
                o = acc[n % 2]
                for k in range(KT):
                    for b in range(2):
                        mm = pe.matmul(o[:, b, 0:HALF_T], w[:, k, :], hT[:, k, b * HALF_T:(b + 1) * HALF_T],
                                       start=k == 0, stop=k == KT - 1)
                mm.then_inc(slot_used, 1)

            for n in range(N_IN):
                in_tile(n)
            pe.wait_ge(in_evicted, N_IN + 2)
            pe.wait_ge(gates_done, 2)
            for k in range(KT):
                w = weights(S_MEM + k)
                for n in range(2):
                    for h in range(2):
                        mm = pe.matmul(acc[n][:, h, :], memT[:, k, n * P:(n + 1) * P],
                                       w[:, 4 * h:4 * h + 4, :].rearrange("p a c -> p (a c)"),
                                       start=k == 0, stop=k == KT - 1)
                mm.then_inc(slot_used, 1)

            pe.wait_ge(mem_done, 2)
            for n, tile in enumerate((T_SV, T_WV)):
                for t in range(QT + 1):
                    rows = P if t < QT else TS
                    mm = pe.transpose(acc[2 + n][0:rows, t // QT, t % QT * P:t % QT * P + P],
                                      in_all[:, tile, t * P:t * P + rows], ident)
            mm.then_inc(rows_mm, 1)
            for h in range(MEM_H):
                for n in range(2):
                    mm = pe.transpose(acc[0][:, h // 2, (h % 2 * 2 + n) * P:(h % 2 * 2 + n + 1) * P],
                                      mem_tm[:, n, h * P:(h + 1) * P], ident)
            mm.then_inc(rows_mm, 1)

            pe.wait_ge(cmp_in, 96)
            for kind in range(2):
                for n in range(16):
                    mm = pe.matmul(acc[1][0:HD, 0, kind:kind + 1], w1_rows[:, kind, n, :], pe_cols[:, kind, n:n + 1],
                                   start=n == 0, stop=n == 15)
            mm.then_inc(cp_mm, 1)
            pe.wait_ge(rows_done, 2)
            for kind, tile in enumerate((T_CK, T_CV)):
                for c in range(CMP):
                    for g, h in QUARTERS:
                        hs = slice(h * HD, (h + 1) * HD)
                        mm = pe.matmul(acc[2][hs, g, kind * TS:(kind + 1) * TS], w1[g * HD:(g + 1) * HD, kind, c, hs],
                                       in_all[g * HD:(g + 1) * HD, tile, c:TP:CMP], start=c == 0, stop=c == CMP - 1)
            mm.then_inc(cp_mm, 1)
            pe.wait_ge(cp_done, 2)
            for kind in range(2):
                for g in range(NG):
                    o = acc[3][0:HD, 0, (kind * 2 + g) * TS:(kind * 2 + g) * TS + NC_P]
                    pe.matmul(o, ident[:, 0:HD], u_sb[:, g, kind, 0:NC_P], start=True, stop=False)
                    mm = pe.matmul(o, ident[:, HD:P], u_sb[:, g, kind, 1:NC_P + 1], start=False, stop=True)
            mm.then_inc(cp_mm, 1)
            pe.wait_ge(cp_done, 4)
            for g in range(NG):
                mm = pe.matmul(acc[2][g * HD:(g + 1) * HD, 0, 0:NC_P], w2[0:HD, 0, :], hid[0:HD, 0, g, 0:NC_P],
                               start=True, stop=True)
            for g in range(NG):
                mm = pe.matmul(acc[2][0:NC_P, 1, g * HD:(g + 1) * HD], hid[0:HD, 1, g, 0:NC_P], w2[0:HD, 1, :],
                               start=True, stop=True)
            mm.then_inc(cp_mm, 1)

            early = [0]

            def rw_tile():
                n = early[0]
                early[0] += 1
                w = weights(S_RW + n)
                if n:
                    pe.wait_ge(rw_evicted, n)
                for k in range(KT):
                    for b in range(2):
                        mm = pe.matmul(acc[3][:, b, 0:HALF_T], w[:, k, :], hT[:, k, b * HALF_T:(b + 1) * HALF_T],
                                       start=k == 0, stop=k == KT - 1)
                mm.then_inc(slot_used, 1)

            pe.wait_ge(q_scaled, 1)
            pe.wait_ge(cp_done, 6)
            for u, (g, t) in enumerate(CMP_UNITS):
                gs = slice(g * HD, (g + 1) * HD)
                if u >= 1:
                    pe.wait_ge(cs_shift, u)
                o = acc[0][:, 0, 0:HPG * NC_P].rearrange("p (r n) -> p r n", r=HPG)
                pe.matmul(o, ident, bc(const("cmpmask")[:, t * NC_P:(t + 1) * NC_P], 1, HPG), start=True, stop=False)
                for r in range(HPG):
                    mm = pe.matmul(o[:, r, :], qT[gs, r, t * P:(t + 1) * P], kcT[gs, 0:NC_P],
                                   start=False, stop=r == HPG - 1)
                mm.then_inc(cs_mm, 1)
                rw_tile()
                pe.wait_ge(cs_prob, u + 1)
                if u >= 1:
                    pe.wait_ge(cs_copied, u)
                o = acc[1][0:NC_P].rearrange("p a (r t) -> p (a r) t", t=P)
                for r in range(HPG):
                    mm = pe.transpose(o[:, r, :], c_prob[:, r, :], ident)
                mm.then_inc(cs_turn, 1)
                if u % 2:
                    rw_tile()
                pe.wait_ge(cs_copied, u + 1)
                if u >= 1:
                    pe.wait_ge(cs_o, u)
                for r in range(HPG):
                    mm = pe.matmul(acc[2][:, 0, r * HD:(r + 1) * HD], c_probT[0:NC_P, r, :], vc[0:NC_P, gs],
                                   start=True, stop=True)
                mm.then_inc(cs_out, 1)

            def att_scores(it, u):
                g, t = ATT_UNITS[u]
                w = (t + 1) * P
                pe.wait_ge(at_exp, it * 8 + u + 1)
                for b, tile in enumerate((T_SK, T_WK)):
                    o = acc[u % 2][:, b, :]
                    pe.matmul(o[:, 0:w], q_pad[g][:, t * P:(t + 1) * P], in_all[:, tile, 0:w], start=True, stop=False)
                    mm = pe.matmul(o[:, t * P:w], ident, const("causal"), start=False, stop=True)
                mm.then_inc(at_s, 1)

            def att_turn(it, u):
                g, t = ATT_UNITS[u]
                pe.wait_ge(at_exp, it * 8 + u + 3)
                pe.wait_ge(at_cs, it * 8 + u + 1)
                pe.wait_ge(at_cw, it * 8 + u + 1)
                for b in range(2):
                    for k in range(t + 1):
                        mm = pe.transpose(acc[2][:, b, k * P:(k + 1) * P], probs[:, u % 2, b, k * P:(k + 1) * P], ident)
                mm.then_inc(at_turn, 1)

            def att_values(it, u):
                g, t = ATT_UNITS[u]
                pe.wait_ge(at_cs, it * 8 + u + 2)
                pe.wait_ge(at_cw, it * 8 + u + 2)
                pe.wait_ge(at_o, it * 8 + u + 1)
                for b in range(2):
                    for k in range(t + 1):
                        mm = pe.matmul(acc[3][:, u % 2, b * HD:(b + 1) * HD], probsT[:, b, k * P:(k + 1) * P],
                                       v_tm[:, b, k, g * HD:(g + 1) * HD], start=k == 0, stop=k == t)
                mm.then_inc(at_pv, 1)

            pe.wait_ge(cs_o, len(CMP_UNITS))
            pe.wait_ge(rw_evicted, RW_EARLY)
            pe.wait_ge(at_o, 2)
            with pe.Fori(0, HPG) as it:
                pe.wait_ge(at_q, it + 1)
                for u in range(8):
                    att_scores(it, u)
                    if u >= 2:
                        att_values(it, u - 2)
                    if u >= 1:
                        att_turn(it, u - 1)
                att_values(it, 6)
                att_turn(it, 7)
                att_values(it, 7)

            for r in range(HPG):
                if r == 0:
                    pe.wait_ge(at_o, 2 + 8 * HPG)
                else:
                    pe.wait_ge(ot_done, r)
                for t in range(QT):
                    mm = pe.transpose(acc[0][:, r % 2, t * P:(t + 1) * P], o_tm[:, t, r, :], ident)
                mm.then_inc(ot_mm, 1)
            pe.wait_ge(ot_done, HPG)
            def memory_scores(t):
                if t >= 2:
                    pe.wait_ge(ma_exp, MA + t - 1)
                for h in range(MEM_H):
                    mm = pe.matmul(acc[3 * (t % 2)][:, h // 2, h % 2 * MEM_T:(h % 2 + 1) * MEM_T],
                                   mqT[:, h, t * P:(t + 1) * P], mkT[:, h, :], start=True, stop=True)
                mm.then_inc(ma_s, 1)

            memory_scores(0)
            for t in range(QT):
                if t < QT - 1:
                    memory_scores(t + 1)
                pe.wait_ge(ma_prob, MA + t + 1)
                if t >= 1:
                    pe.wait_ge(ma_copied, MA + t)
                for h in range(MEM_H):
                    for n in range(2):
                        mm = pe.transpose(acc[1][:, h // 2, (h % 2 * 2 + n) * P:(h % 2 * 2 + n + 1) * P],
                                          m_probs[t % 2][:, h, n * P:(n + 1) * P], ident)
                mm.then_inc(ma_turn, 1)
                pe.wait_ge(ma_copied, MA + t + 1)
                if t >= 1:
                    pe.wait_ge(ma_done, MA + t)
                for h in range(MEM_H):
                    for n in range(2):
                        mm = pe.matmul(acc[2][:, 0, h * P:(h + 1) * P], mem_tm[:, n, TP + h * P:TP + (h + 1) * P],
                                       m_probT[:, h * 2 + n, :], start=n == 0, stop=n == 1)
                mm.then_inc(ma_pv, 1)

            pe.wait_ge(spread_in, 32)
            pe.wait_ge(ma_done, MA + QT)
            o = acc[0][:].rearrange("p a (n t) -> p (a n) t", t=TS)
            for n in range(3 * HPG):
                mm = pe.matmul(o[:, n, :], spread[0:36, n, :], gates_s[:], start=True, stop=True)
            mm.then_inc(sg_mm, 1)
            pe.wait_ge(sg_done, 1)
            with pe.Fori(0, 2) as half:
                pe.wait_ge(sq_done, half + 1)
                for b in range(4):
                    n = half * 4 + b
                    kp, rows = k_pages[:, b % 2], slice(b * 32, (b + 1) * 32)
                    pe.wait_ge(k_in[b % 2], half * (2 * 16 * 9) + (b // 2 + 1) * 16 * 9)
                    pe.wait_ge(so_done, half)
                    pe.wait_ge(ss_dve, n)
                    settle()
                    for kind in range(2):
                        for c in range(CMP):
                            for g, h in QUARTERS:
                                hs = slice(h * HD, (h + 1) * HD)
                                mm = pe.matmul(acc[2][hs, g, kind * HD:(kind + 1) * HD], w1[g * HD:(g + 1) * HD, kind, c, hs],
                                               kp[g * HD:(g + 1) * HD, :, kind, c * NPC:(c + 1) * NPC], start=c == 0, stop=c == CMP - 1)
                    mm.then_inc(su_mm, 1)
                    pe.wait_ge(ss_act, n)
                    pe.wait_ge(st_act, half * 2)
                    pe.wait_ge(st_dve, half * 2)
                    settle()
                    for j in range(2):
                        for g in range(NG):
                            mm = pe.matmul(acc[g][rows, j, :], q_half[:, g, b, :], kp[:, 4 * j:4 * j + 4, 2, :],
                                           start=True, stop=True)
                    mm.then_inc(ss_a, 1)
                    pe.wait_ge(su_done, n + 1)
                    pe.wait_ge(sf_done, half)
                    for kind in range(2):
                        for g in range(NG):
                            o = acc[3][0:HD, 0, (kind * 2 + g) * HD:(kind * 2 + g) * HD + NC_S]
                            pe.matmul(o, ident[:, 0:HD], u_s[:, g, kind, 0:NC_S], start=True, stop=False)
                            mm = pe.matmul(o, ident[:, HD:P], u_s[:, g, kind, 1:NC_S + 1], start=False, stop=True)
                    mm.then_inc(sp_mm, 1)
                    for g in range(NG):
                        pe.matmul(acc[2][rows, g, :], q_half[:, g, b, :], win_k[:, b % 2, :], start=True, stop=True)
                    pe.wait_ge(sp_done, n + 1)
                    settle()
                    for g in range(NG):
                        mm = pe.matmul(acc[3][g * HD:(g + 1) * HD, 1, 0:NC_S], w2[0:HD, 0, :], hid_s[0:HD, 0, g, 0:NC_S],
                                       start=True, stop=True)
                    for g in range(NG):
                        mm = pe.matmul(acc[3][0:NC_S, 1, HD + g * HD:HD + (g + 1) * HD], hid_s[0:HD, 1, g, 0:NC_S],
                                       w2[0:HD, 1, :], start=True, stop=True)
                    mm.then_inc(sk_mm, 1)
                    pe.wait_ge(sk_done, n + 1)
                    pe.wait_ge(sv_done, n + 1)
                    settle()
                    for c0, n_, keys in ((0, TS, in_all[:, T_WK, TP:T]), (TS, NC_S, kc_s[:, 0:NC_S]),
                                         (TS + NC_S, TS, in_all[:, T_SK, TP:T])):
                        for g in range(NG):
                            mm = pe.matmul(acc[3][rows, g, c0:c0 + n_], q_half[:, g, b, :], keys, start=True, stop=True)
                    mm.then_inc(ss_b, 1)
                pe.wait_ge(si_in, half + 1)
                pe.wait_ge(ss_dve, half * 4 + 4)
                pe.wait_ge(sv_done, half * 4 + 4)
                pe.matmul(acc[3][:, 1, 0:NG * NC_S], const("samequery"), imp[:, :, 0:NC_S], start=True, stop=True)\
                  .then_inc(si_mm, 1)
                for g in range(NG):
                    pe.wait_ge(sx_exp, half * 3 + 3)
                    if g == 0:
                        pe.wait_ge(ss_act, half * 4 + 4)
                        pe.wait_ge(so_mm, half * 2)
                    else:
                        pe.wait_ge(st_act, half * 2 + 1)
                        pe.wait_ge(st_dve, half * 2 + 1)
                    for k in range(NPG):
                        pe.transpose(acc[0][:, k // 4, k % 4 * P:(k % 4 + 1) * P],
                                     scores[:, g, S0 + k * P:S0 + (k + 1) * P], ident)
                    for k in range(4):
                        pe.transpose(acc[1][:, 0, k * P:(k + 1) * P], scores[:, g, k * P:(k + 1) * P], ident)
                    for k, (c0, n) in enumerate(((WN0, TS), (N0, TS), (C0, NC_S))):
                        mm = pe.transpose(acc[1][0:n, 1, k * P:(k + 1) * P], scores[:, g, c0:c0 + n], ident)
                    mm.then_inc(st_mm, 1)
                    pe.wait_ge(st_act, half * 2 + g + 1)
                    pe.wait_ge(st_dve, half * 2 + g + 1)
                    pe.wait_ge(v_in, (half + 1) * (4 * 16 * 9))
                    settle()
                    for b in range(4):
                        rows = slice(b * 32, (b + 1) * 32)
                        hd = slice(g * HD, (g + 1) * HD)
                        parts = [[(14, NC_S, vc_s[0:NC_S, b, hd])],
                                 [(k, P, v_pages[:, b, k, hd]) for k in range(NPG)] + [(13, TS, v_tm[0:TS, 0, QT, hd])],
                                 [(NPG + k, P, win_v[:, b, k, hd]) for k in range(4)] + [(12, TS, v_tm[0:TS, 1, QT, hd])]]
                        for s_, part in enumerate(parts):
                            o = acc[2][rows, 0, (s_ * NG + g) * HD:(s_ * NG + g + 1) * HD]
                            for k, (slot, n, value) in enumerate(part):
                                mm = pe.matmul(o, sprobT[0:n, slot, rows], value, start=k == 0, stop=k == len(part) - 1)
                    mm.then_inc(so_mm, 1)
                pe.wait_ge(so_done, half + 1)
                for s_ in range(3):
                    mm = pe.transpose(acc[3][:, 0, s_ * P:(s_ + 1) * P],
                                      o_rows[:, 2 * s_:2 * s_ + 2, :].rearrange("p g d -> p (g d)"), ident)
                mm.then_inc(sf_mm, 1)
            with pe.Fori(0, 2) as half:
                pe.wait_ge(ms_q, half + 1)
                pe.wait_ge(sf_done, 2)
                for b in range(4):
                    rows = slice(b * 32, (b + 1) * 32)
                    pe.wait_ge(mk_in[b % 2], K_IN + half * 32 + (b // 2 + 1) * 16)
                    for h in range(MEM_H):
                        mm = pe.matmul(acc[0][rows, 0, 0:MEM_T], mem_q[:, b, h, :], mem_k[:, b % 2, h, :],
                                       start=h == 0, stop=h == MEM_H - 1)
                    mm.then_inc(ms_s, 1)
                pe.wait_ge(ms_exp, MS + half + 1)
                for n in range(2):
                    mm = pe.transpose(acc[1][:, 0, n * P:(n + 1) * P], mem_p[:, n * P:(n + 1) * P], ident)
                mm.then_inc(ms_turn, 1)
                pe.wait_ge(ms_copied, MS + half + 1)
                pe.wait_ge(mv_in, V_IN + (half + 1) * 64)
                for b in range(4):
                    rows = slice(b * 32, (b + 1) * 32)
                    for n in range(2):
                        mm = pe.matmul(acc[2][rows, 0, :], mem_pT[:, n, rows], mem_v[:, b, n, :], start=n == 0, stop=n == 1)
                mm.then_inc(ms_pv, 1)
                pe.wait_ge(ms_norm, half + 1)
                for h in range(MEM_H):
                    mm = pe.transpose(acc[3][:, 0, h * P:(h + 1) * P], mem_o[:, h * P:(h + 1) * P], ident)
                mm.then_inc(ms_ft, 1)

            pe.wait_ge(sf_done, 2)
            pe.wait_ge(ms_done, MS + 2)
            pe.wait_ge(kv_stored, 16)
            for n in range(RW_EARLY, N_RW):
                w = weights(S_RW + n)
                pe.wait_ge(rw_evicted, n + 1)
                for k in range(KT):
                    for b in range(2):
                        mm = pe.matmul(acc[n % 2][:, b, 0:HALF_T], w[:, k, :], hT[:, k, b * HALF_T:(b + 1) * HALF_T],
                                       start=k == 0, stop=k == KT - 1)
                mm.then_inc(slot_used, 1)

            def tokens(a, lhsT, rhs):
                for b in range(2):
                    mm = pe.matmul(acc[a][:, b, 0:HALF_T], lhsT, rhs[:, b * HALF_T:(b + 1) * HALF_T], start=True, stop=True)
                return mm

            def gate_tile(n):
                w = weights(S_MG + n)
                if n:
                    pe.wait_ge(mg_sig, n)
                for k in range(KT):
                    for b in range(2):
                        mm = pe.matmul(acc[2][:, b, 0:HALF_T], w[:, k, :], hT[:, k, b * HALF_T:(b + 1) * HALF_T],
                                       start=k == 0, stop=k == KT - 1)
                mm.then_inc(slot_used, 1)

            for n in range(GATES_FIRST):
                gate_tile(n)
            pe.wait_ge(lo_act, 2)
            pe.wait_ge(rw_evicted, N_RW + 2)
            for i in range(PAIRS):
                ps = slice(i * P, (i + 1) * P)
                for x, (w, rhs) in enumerate(((lw_w[0:HD, ps], tmp[0:HD, 0, :]), (lw_w[HD:P, ps], rwT[HD:P, R_LORA, :]),
                                              (lw_g[:, ps], tmp[:, 1, :]))):
                    if 3 * i + x >= 2:
                        pe.wait_ge(lo_out, 3 * i + x - 1)
                    tokens((3 * i + x) % 2, w, rhs).then_inc(lo_mm, 1)
                pe.wait_ge(kn_sq, i + 1)
                if i > 0:
                    pe.wait_ge(kn_max, i)
                tokens(3, const("headsum"), tmp[:, 2 + i % 2, :]).then_inc(kn_mm, 1)
                gate_tile(GATES_FIRST + i)
            for i in range(PAIRS):
                gate_tile(GATES_FIRST + PAIRS + i)
                pe.wait_ge(bo_in, i + 1)
                if i > 0:
                    pe.wait_ge(prep_done, i)
                else:
                    pe.wait_ge(kn_max, PAIRS)
                tokens(3, const("headsum"), tmp[:, 0, :]).then_inc(bo_mm, 1)
            for n in range(GATES_FIRST + 2 * PAIRS, 3 * KT):
                gate_tile(n)

            pe.sem_inc(o_mm, 1)
            both = lambda n: acc[n][:].rearrange("p a c -> p (a c)")

            feats = (slice(0, HD), slice(HD, P))

            def heads(n):
                return slice(0, n), slice(n, 2 * n)

            def half_sets():
                for s_ in range(2):
                    yield s_, [(i, i - 3 * s_) for i in range(3 * s_, 3 * s_ + 3)]

            def chunk_solve(c, par, n, levels):
                bk, zr, rows = bk_now[:, par, :, 0:2 * n], zr_now[:, par, :, 0:2 * n], heads(n)
                pe.wait_ge(staged, c + 1)
                pe.wait_ge(w_out_odd, c)
                pe.wait_ge(u_out_odd, c)
                for i in range(PAIRS):
                    mm = pe.transpose(both(1)[0:2 * n, i * P:(i + 1) * P], bk[:, i, :], ident)
                mm.then_inc(tb_mm, 1)
                pe.wait_ge(s_out, c)
                pe.wait_ge(yt_out, c)
                pe.wait_ge(w_out, c)
                pe.wait_ge(u_out, c)
                settle()
                for e in range(2):
                    for i in range(PAIRS):
                        mm = pe.matmul(both(2 * e)[0:2 * n, i * P:i * P + 2 * n], bk[feats[e], i, :], zr[feats[e], i, :],
                                       start=True, stop=True)
                    mm.then_inc(gram_mm, 1)
                for i in range(PAIRS):
                    mm = pe.transpose(both(3)[0:2 * n, i * P:(i + 1) * P], v_now[:, i, 0:2 * n], ident)
                mm.then_inc(tv_mm, 1)
                pe.wait_ge(gram_out, c * 2 + 2)
                pe.wait_ge(v_rows, c + 1)
                pe.wait_ge(bk_rows, c + 1)
                settle()
                x_at, xt_at = (lambda k: slice(k * C, k * C + n)), (lambda k: slice((3 + k) * C, (3 + k) * C + n))
                for s_, pairs in half_sets():
                    for i, k in pairs:
                        for e in range(2):
                            mm = pe.matmul(acc[2 + e][rows[e], s_, x_at(k)], XT(i)[rows[e], 0:n],
                                           ident[rows[e], rows[e]], start=True, stop=True)
                    mm.then_inc(x_mm, 1)
                for l in range(levels):
                    for s_, pairs in half_sets():
                        pe.wait_ge(x_out, c * 12 + 2 * l + s_ + 1)
                        settle()
                        for i, k in pairs:
                            for e in range(2):
                                mm = pe.matmul(acc[e][rows[e], s_, x_at(k)], gram[rows[e], e, i, 0:n],
                                               X(i)[rows[e], 0:n], start=True, stop=True)
                        mm.then_inc(y_mm, 1)
                    for s_, pairs in half_sets():
                        pe.wait_ge(y_out, c * 10 + 2 * l + s_ + 1)
                        settle()
                        for i, k in pairs:
                            if l < levels - 1:
                                for e in range(2):
                                    pe.matmul(acc[2 + e][rows[e], s_, x_at(k)], XT(i)[rows[e], 0:n],
                                              Y[rows[e], i, 0:n], start=True, stop=True)
                            for e in range(2):
                                mm = pe.matmul(acc[2 + e][rows[e], s_, xt_at(k)], Y[rows[e], i, 0:n],
                                               XT(i)[rows[e], 0:n], start=True, stop=True)
                        mm.then_inc(x_mm, 1)

            def chunk_out(c, par, n, levels, state):
                zr, rows = zr_now[:, par, :, 0:2 * n], heads(n)
                pe.wait_ge(s_out, c)
                pe.wait_ge(y_out, c * 10 + 2 * levels)
                settle()
                for i in range(PAIRS):
                    out = [acc[e][rows[e], 0, i * C:(i + 1) * C] for e in range(2)]
                    for e in range(2):
                        state(out[e], i, e, zr)
                    if n < C:
                        pe.wait_ge(z_used, 2 * i + 1)
                    for e in range(2):
                        o = out[e]
                        mm = pe.matmul(o, gram[0:2 * n, e, i, 0:n], uv[0:2 * n, i, e, :], start=False, stop=True)
                    if n < C and i < PAIRS - 1:
                        mm.then_inc(z_used, 1)
                mm.then_inc(w_mm, 1)
                pe.wait_ge(w_out, c + 1)
                pe.wait_ge(w_out_odd, c + 1)
                pe.wait_ge(x_out, c * 12 + 2 * levels + 2)
                settle()
                for i in range(PAIRS):
                    for e in range(2):
                        mm = pe.matmul(acc[e][rows[e], 1, i * C:(i + 1) * C], XT(i)[rows[e], 0:n], w_tm[rows[e], i, :],
                                       start=True, stop=True)
                mm.then_inc(u_mm, 1)
                pe.wait_ge(u_out, c + 1)
                pe.wait_ge(u_out_odd, c + 1)
                settle()

            def chunk_y(c, par, n, state):
                zr = zr_now[:, par, :, 0:2 * n]
                for i in range(PAIRS):
                    out = [acc[2 + e][feats[e], 0, i * C:i * C + n] for e in range(2)]
                    for e in range(2):
                        state(out[e], i, e, zr)
                    if n < C:
                        pe.wait_ge(z_used, 2 * PAIRS - 1 + 2 * i + 1)
                    for e in range(2):
                        o = out[e]
                        mm = pe.matmul(o, uv[0:2 * n, i, e, :], gram[0:2 * n, e, i, n:2 * n], start=False, stop=True)
                    if n < C and i < PAIRS - 1:
                        mm.then_inc(z_used, 1)
                mm.then_inc(o_mm, 1)

            with pe.Fori(0, NCH // 2) as it:
                for par in range(2):
                    c = it * 2 + par
                    chunk_solve(c, par, C, 5)
                    chunk_out(c, par, C, 5, lambda o, i, e, zr: pe.matmul(
                        o, zr[feats[e], i, 0:C], S[feats[e], i, :], start=True, stop=False))
                    for i in range(PAIRS):
                        for e in range(2):
                            mm = pe.matmul(acc[2][feats[e], 1, i * C:(i + 1) * C], bk_tm[:, i, e * HD:(e + 1) * HD],
                                           uv[:, i, e, :], start=True, stop=True)
                    mm.then_inc(s_mm, 1)
                    chunk_y(c, par, C, lambda o, i, e, zr: pe.matmul(
                        o, S[feats[e], i, :], zr[feats[e], i, C:2 * C], start=True, stop=False))

            pe.wait_ge(states_in, 16)
            chunk_solve(NCH, 0, TS, 1)

            def sample_state(x):
                def products(o, i, e, zr):
                    turn = x * PAIRS + i + 1
                    pe.wait_ge(z_masked, turn)
                    if i:
                        pe.wait_ge(z_used, x * (2 * PAIRS - 1) + 2 * i)
                    zb = z_b[feats[e], turn % 2, :].rearrange("p (b t) -> p b t", b=NB)
                    for b in range(NB):
                        z, s_ = zb[:, b, :], S_s[feats[e], b, i, :]
                        mm = pe.matmul(o, s_ if x else z, z if x else s_, start=b == 0, stop=False)
                    if e:
                        mm.then_inc(z_used, 1)
                return products

            chunk_out(NCH, 0, TS, 1, sample_state(0))
            chunk_y(NCH, 0, TS, sample_state(1))
            for i in range(PAIRS):
                for e in range(2):
                    j = 2 * i + e
                    pe.wait_ge(uvb_done, j + 1)
                    if i >= 1:
                        pe.wait_ge(wkv_done, 2 * i)
                    mm = pe.matmul(acc[1][e * HD:(e + 1) * HD, 0, :], bk_tm[0:2 * TS, i, e * HD:(e + 1) * HD],
                                   uv_b[0:2 * TS, j % 2].rearrange("p b c -> p (b c)"), start=True, stop=True)
                    mm.then_inc(uvb_used, 1)

            def gn_tokens(a, rhs):
                for b in range(2):
                    mm = pe.matmul(acc[a][:, b, 0:HALF_T], const("headsum"), rhs[:, b * HALF_T:(b + 1) * HALF_T],
                                   start=True, stop=True)
                return mm

            pe.wait_ge(yt_out, NCH + 1)
            pe.wait_ge(wkv_done, 2 * PAIRS)
            gn_tokens(0, zT[:, 0, :]).then_inc(gn_mean, 1)
            for i in range(PAIRS):
                if i < PAIRS - 1:
                    pe.wait_ge(gn_diff, PAIRS + i + 1)
                    gn_tokens(0, zT[:, i + 1, :]).then_inc(gn_mean, 1)
                pe.wait_ge(gn_sq, 3 * PAIRS + i + 1)
                if i:
                    pe.wait_ge(gn_max, PAIRS + i)
                gn_tokens(1, kkT[:, 2 + i % 2, :]).then_inc(gn_var, 1)

            pe.wait_ge(gn_done, PAIRS)
            block = 0
            for m in range(KT):
                sources = ([onsaT[:, r, :] for r in range(HPG)], [zT[:, i, :] for i in range(PAIRS)],
                           [omemT[:, h, :] for h in range(MEM_H)])
                for g, source in enumerate(sources):
                    n = 3 * m + g
                    if n >= 4:
                        pe.wait_ge(mg_part, n - 3)
                    for k, x in enumerate(source):
                        if block % KT == 0:
                            w = weights(S_MERGE + block // KT)
                        for b in range(2):
                            mm = pe.matmul(acc[n % 4][:, b, 0:HALF_T], w[:, block % KT, :],
                                           x[:, b * HALF_T:(b + 1) * HALF_T], start=k == 0, stop=k == len(source) - 1)
                        block += 1
                        if block % KT == 0:
                            mm.then_inc(slot_used, 1)
                        elif k == len(source) - 1:
                            mm.then_inc(mg_mm, 1)

            def square_sum(j, done):
                pe.wait_ge(sqT_made, done + j + 1)
                for b in range(2):
                    mm = pe.matmul(acc[3][:, b, 0:HALF_T], ones, sqT[:, j % 2, b * HALF_T:(b + 1) * HALF_T],
                                   start=j == 0, stop=j == KT - 1)
                mm.then_inc(sqT_summed, 1)

            pe.wait_ge(mg_part, 3 * KT + 1)
            for j in range(KT):
                w = weights(S_OUT + j)
                if j >= 2:
                    pe.wait_ge(x1_added, j - 1)
                for k in range(KT):
                    for b in range(2):
                        mm = pe.matmul(acc[j % 2][:, b, 0:HALF_T], w[:, k, :], mT[:, k, b * HALF_T:(b + 1) * HALF_T],
                                       start=k == 0, stop=k == KT - 1)
                mm.then_inc(slot_used, 1)
                if j:
                    square_sum(j - 1, 0)
            square_sum(KT - 1, 0)

            def ff_tile(n, it=None):
                t_done = n if it is None else it * 10 + n
                for x in range(2):
                    w = weights(S_GU + 2 * n + x, it, 20)
                    if it is not None or n >= 2:
                        pe.wait_ge(ff_done if x else gu_act, t_done + 1)
                    for k in range(KT):
                        for b in range(2):
                            mm = pe.matmul(acc[2 * x + n % 2][:, b, 0:HALF_T], w[:, k, :],
                                           hT[:, k, b * HALF_T:(b + 1) * HALF_T], start=k == 0, stop=k == KT - 1)
                    mm.then_inc(slot_used, 1)

            pe.wait_ge(hf_done, KT)
            with pe.Fori(0, FFT // 10) as it:
                for n in range(10):
                    ff_tile(n, it)
            for n in range(FFT // 10 * 10, FFT):
                ff_tile(n)

            pe.wait_ge(ff_done, FFT + 2)
            block = 0
            for j in range(KT):
                if j >= 2:
                    pe.wait_ge(x1_added, KT + j - 1)
                for k in range(FFT):
                    if block % KT == 0:
                        w = weights(S_DOWN + block // KT)
                    for b in range(2):
                        mm = pe.matmul(acc[j % 2][:, b, 0:HALF_T], w[:, block % KT, :],
                                       ffT[:, k, b * HALF_T:(b + 1) * HALF_T], start=k == 0, stop=k == FFT - 1)
                    block += 1
                    if block % KT == 0:
                        mm.then_inc(slot_used, 1)
                    elif k == FFT - 1:
                        mm.then_inc(dn_mm, 1)
                if j:
                    square_sum(j - 1, KT)
            square_sum(KT - 1, KT)

        @block.scalar
        def _(act):
            for i in range(QT):
                act.dma_start(x_tm[:, i, :], A["x_all"][i * P:(i + 1) * P]).then_inc(x_in[0], 16)
            act.dma_start(x_tm[0:TS, QT, :], A["x_all"][TP:T]).then_inc(x_in[0], 16)
            for i in range(2):
                act.dma_start(x_tm[:, 5 + i, :], A["mem_x"][i * P:(i + 1) * P]).then_inc(x_in[1], 16)
            own = Steps(act, act_own)
            act.wait_ge(means, 1)
            for i, (rows, *_) in enumerate(NORM):
                act.wait_ge(x_in[i > QT], 32 if i > QT else 16 * (QT + 1))
                own(act.activation(junk[0:rows], x_tm[0:rows, i, :], ACT.Square, accum_out=stat[0:rows, i:i + 1]))
            act.activation(stat[:, 16:17], stat[:, 0:1], ACT.Copy).then_inc(squares, 1)
            act.wait_ge(means, 2)
            act.activation(stat[:, 8:15], stat[:, 8:15], ACT.Sqrt).then_inc(roots, 1)
            act.wait_ge(gates_mm, 1)
            act.activation(gates_tm[:, 0:QT, :], acc[2][:, 0, 0:36 * QT].rearrange("p (n c) -> p n c", n=QT),
                           ACT.Sigmoid).then_inc(gates_done, 1)
            act.activation(gates_s[:], acc[2][0:36, 1, 0:TS], ACT.Sigmoid).then_inc(gates_done, 1)
            act.wait_ge(hT_ready, 7)
            act.sem_inc(in_evicted, 2)
            with act.Fori(0, N_IN // 2) as i:
                for k in range(2):
                    act.wait_ge(slot_used, i * 2 + k + 1)
                    act.activation(in_all[:, bass.ds(i * 2 + k, 1), :].rearrange("p a (b t) -> p (a b) t", b=2),
                                   acc[k][:, :, 0:HALF_T], ACT.Copy).then_inc(in_evicted, 1)
            act.wait_ge(slot_used, S_RW)
            for n in range(2):
                act.activation(mem_tm[:, n, :], acc[n][:].rearrange("p a c -> p (a c)"), ACT.Copy)\
                   .then_inc(mem_done, 1)

            act.wait_ge(cp_mm, 3)
            act.wait_ge(cp_done, 2)
            for kind in range(2):
                act.activation(hid[0:HD, kind, :, 0:NC_P],
                               acc[3][0:HD, 0, kind * 2 * TS:(kind + 1) * 2 * TS].rearrange("p (g n) -> p g n", g=NG)[:, :, 0:NC_P],
                               ACT.Gelu_apprx_tanh, bias=pre_bias[0:HD, kind:kind + 1]).then_inc(cp_done, 1)
            for u, (g, t) in enumerate(CMP_UNITS):
                act.wait_ge(cs_shift, u + 1)
                act.activation(c_prob, c_shift, ACT.Exp).then_inc(cs_exp, 1)
                for n in range(3 * u // 2, 3 * (u + 1) // 2):
                    act.wait_ge(slot_used, S_RW + n + 1)
                    if n >= 2:
                        act.wait_ge(spilled[n % 2], n // 2 * 16)
                    act.activation(rw_now[:, n % 2, :].rearrange("p (b t) -> p b t", b=2), acc[3][:, :, 0:HALF_T],
                                   ACT.Copy).then_inc(rw_evicted, 1)
                act.wait_ge(cs_out, u + 1)
                act.activation(o_tm[:, t, :, g * HD:(g + 1) * HD],
                               acc[2][:, 0, 0:HPG * HD].rearrange("p (r d) -> p r d", r=HPG), ACT.Copy)\
                   .then_inc(cs_o, 1)
            act.wait_ge(cs_out, len(CMP_UNITS))
            for n in range(2):
                act.wait_ge(spilled[n], 16 * RW_EARLY // 2)
            act.sem_inc(at_exp, 2)
            act.sem_inc(at_cw, 1)

            def att_exp(it, u):
                g, t = ATT_UNITS[u]
                w = (t + 1) * P
                act.wait_ge(at_max, it * 8 + u + 1)
                act.wait_ge(at_turn, it * 8 + u - 1) if u >= 2 else None
                if u < 2:
                    act.wait_ge(at_turn, it * 8)
                for b in range(2):
                    ins = act.activation(probs[:, u % 2, b, 0:w], acc[u % 2][:, b, 0:w], ACT.Exp,
                                         bias=small[:, 2 * (u % 2) + b:2 * (u % 2) + b + 1],
                                         accum_out=small[:, 8 + 2 * (u % 2) + b:9 + 2 * (u % 2) + b])
                ins.then_inc(at_exp, 1)

            def att_copy(it, u):
                g, t = ATT_UNITS[u]
                w = (t + 1) * P
                act.wait_ge(at_turn, it * 8 + u + 1)
                act.wait_ge(at_pv, it * 8 + u)
                act.activation(probsT[:, 1, 0:w], acc[2][:, 1, 0:w], ACT.Copy).then_inc(at_cw, 1)

            with act.Fori(0, HPG) as it:
                act.wait_ge(at_s, it * 8)
                for g in range(NG):
                    gs = slice(g * HD, (g + 1) * HD)
                    ins = act.activation(q_pad[g][gs], qT[gs, bass.ds(it, 1), 0:TP].rearrange("p a t -> p (a t)"), ACT.Copy)
                ins.then_inc(at_q, 1)
                for u in range(8):
                    att_exp(it, u)
                    if u >= 1:
                        att_copy(it, u - 1)
                att_copy(it, 7)
            for r in range(HPG):
                act.wait_ge(ot_mm, r + 1)
                act.activation(onsaT[:, r, 0:TP], acc[0][:, r % 2, :], ACT.Copy).then_inc(ot_done, 1)
            def memory_exp(t):
                act.wait_ge(ma_max, MA + t + 1)
                if t >= 2:
                    act.wait_ge(ma_turn, MA + t - 1)
                d = 24 + 12 * (t % 2)
                for h in range(MEM_H):
                    ins = act.activation(m_probs[t % 2][:, h, :],
                                         acc[3 * (t % 2)][:, h // 2, h % 2 * MEM_T:(h % 2 + 1) * MEM_T], ACT.Exp,
                                         bias=small[:, d + h:d + h + 1], accum_out=small[:, d + 4 + h:d + 5 + h])
                ins.then_inc(ma_exp, 1)

            memory_exp(0)
            for t in range(QT):
                if t < QT - 1:
                    memory_exp(t + 1)
                act.wait_ge(ma_pv, MA + t + 1)
                act.activation(omemT[:, :, t * P:(t + 1) * P], acc[2][:, 0, :].rearrange("p (h t) -> p h t", h=MEM_H),
                               ACT.Copy).then_inc(ma_done, 1)

            with act.Fori(0, 2) as half:
                for b in range(4):
                    n, rows = half * 4 + b, slice(b * 32, (b + 1) * 32)
                    act.wait_ge(ss_a, n + 1)
                    for g in range(NG):
                        ins = act.activation(scores[rows, g, S0:S0 + PAST], acc[g][rows].rearrange("p a c -> p (a c)"),
                                             ACT.Copy)
                    ins.then_inc(ss_act, 1)
                    act.wait_ge(sp_mm, n + 1)
                    for kind in range(2):
                        ins = act.activation(hid_s[0:HD, kind, :, 0:NC_S],
                                             acc[3][0:HD, 0, kind * P:(kind + 1) * P]
                                             .rearrange("p (g n) -> p g n", g=NG)[:, :, 0:NC_S],
                                             ACT.Gelu_apprx_tanh, bias=pre_bias[0:HD, kind:kind + 1])
                    ins.then_inc(sp_done, 1)
                    act.wait_ge(sk_done, n + 1)
                    act.activation(vc_s[0:NC_S, b, :], acc[3][0:NC_S, 1, HD:HD + P], ACT.Copy).then_inc(sv_done, 1)
                for x, (c0, c1) in enumerate(((C0, N0), (W0, C0), (N0, S0 + PAST))):
                    act.wait_ge(sx_max, half * 3 + x + 1)
                    for g in range(NG):
                        ins = act.activation(scores[:, g, c0:c1], scores[:, g, c0:c1], ACT.Exp,
                                             bias=small[:, 2 * x + g:2 * x + g + 1],
                                             accum_out=small[:, 8 + 2 * x + g:9 + 2 * x + g])
                    ins.then_inc(sx_exp, 1)
                for g in range(NG):
                    act.wait_ge(st_mm, half * 2 + g + 1)
                    act.wait_ge(so_mm, half * 2 + g)
                    act.activation(sprobT[:, NPG:NPG + 4, :].rearrange("p a c -> p (a c)"), acc[1][:, 0, :], ACT.Copy)
                    act.activation(sprobT[0:TS, 12:14, :].rearrange("p a c -> p (a c)"), acc[1][0:TS, 1, 0:2 * P], ACT.Copy)
                    act.activation(sprobT[0:NC_S, 14, :], acc[1][0:NC_S, 1, 2 * P:3 * P], ACT.Copy).then_inc(st_act, 1)
            with act.Fori(0, 2) as half:
                act.wait_ge(ms_max, MS + half + 1)
                act.activation(mem_p, acc[0][:, 0, 0:MEM_T], ACT.Exp, bias=small[:, 0:1], accum_out=small[:, 1:2])\
                   .then_inc(ms_exp, 1)
                act.wait_ge(ms_turn, MS + half + 1)
                act.activation(mem_pT[:].rearrange("p a c -> p (a c)"), acc[1][:, 0, 0:2 * P], ACT.Copy).then_inc(ms_copied, 1)

            act.wait_ge(sf_done, 2)
            act.wait_ge(ms_done, MS + 2)
            act.wait_ge(kv_stored, 16)
            act.wait_ge(win_stored, 16 * (NB + 1))
            act.sem_inc(rw_evicted, 2)
            for n in range(RW_EARLY, N_RW):
                act.wait_ge(slot_used, S_RW + n + 1)
                act.activation(rwT[:, n, :].rearrange("p (b t) -> p b t", b=2), acc[n % 2][:, :, 0:HALF_T],
                               ACT.Copy).then_inc(rw_evicted, 1)
            h2 = lambda a: a.rearrange("p (b t) -> p b t", b=2)
            def gate_tile(n):
                act.wait_ge(slot_used, S_MG + n + 1)
                if n >= 2:
                    act.wait_ge(spilled[n % 2], (RW_EARLY + n) // 2 * 16)
                act.activation(h2(gate_now[:, n % 2, :]), acc[2][:, :, 0:HALF_T], ACT.Sigmoid).then_inc(mg_sig, 1)

            for n in range(GATES_FIRST):
                gate_tile(n)
            act.wait_ge(xm_done, N_RW)
            act.activation(tmp[:, 1, :], rwT[:, R_GD, :], ACT.Sigmoid).then_inc(lo_act, 1)
            act.activation(tmp[0:HD, 0, :], rwT[0:HD, R_LORA, :], ACT.Tanh).then_inc(lo_act, 1)
            for i in range(PAIRS):
                for x, (dst, f, bias) in enumerate(((zT, ACT.Sigmoid, "w0"), (bT, ACT.Sigmoid, "a0"), (gT, ACT.Copy, None))):
                    act.wait_ge(lo_mm, 3 * i + x + 1)
                    more = dict(bias=v(bias, i)) if bias else {}
                    act.activation(h2(dst[:, i, :]), acc[(3 * i + x) % 2][:, :, 0:HALF_T], f, **more).then_inc(lo_out, 1)
                gate_tile(GATES_FIRST + i)
                act.wait_ge(kn_max, i + 1)
                act.activation(tmp[:, 4 + i % 2, :], tmp[:, 4 + i % 2, :], ACT.Sqrt).then_inc(kn_root, 1)
            for i in range(PAIRS):
                gate_tile(GATES_FIRST + PAIRS + i)
                act.wait_ge(ex_in, i + 1)
                act.activation(tmp[:, 2, :], tmp[:, 1, :], ACT.Exp)
                act.activation(tmp[:, 3, :], tmp[:, 1, :], ACT.Exp, scale=-1.0)
                act.activation(tmp[:, 4, :], tmp[:, 5, :], ACT.Exp).then_inc(ex_out, 1)
            for n in range(GATES_FIRST + 2 * PAIRS, 3 * KT):
                gate_tile(n)
            both = lambda n: acc[n][:].rearrange("p a c -> p (a c)")
            flat = lambda a: a.rearrange("p a c -> p (a c)")
            pairs6 = lambda a: a.rearrange("p (i s) -> p i s", s=C)

            def chunk(c, n, levels, t0):
                odd = slice(n, 2 * n)
                act.wait_ge(tb_mm, c + 1)
                act.activation(flat(bk_tm[0:2 * n]), both(1)[0:2 * n, 0:PAIRS * P], ACT.Copy).then_inc(bk_rows, 1)
                act.wait_ge(tv_mm, c + 1)
                act.activation(uv[0:2 * n].rearrange("p a e c -> p (a e c)"), both(3)[0:2 * n, 0:PAIRS * P], ACT.Copy)\
                   .then_inc(v_rows, 1)
                for l in range(levels + 1):
                    first, last = (0, 2) if 0 < l < levels else (0, 1) if l == 0 else (1, 2)
                    for s_ in range(2):
                        act.wait_ge(x_mm, c * 12 + 2 * l + s_ + 1)
                        for e in range(2):
                            rows = slice(e * n, (e + 1) * n)
                            src = acc[2 + e][rows, s_, first * 3 * C:last * 3 * C]
                            ins = act.activation(XX[rows, s_, first:last, :, 0:n].rearrange("p x k c -> p (x k) c"),
                                                 pairs6(src)[:, :, 0:n], ACT.Copy)
                        ins.then_inc(x_out, 1)
                act.wait_ge(w_mm, c + 1)
                act.activation(flat(w_tm[0:n]), acc[0][0:n, 0, 0:PAIRS * C], ACT.Copy).then_inc(w_out, 1)
                act.wait_ge(u_mm, c + 1)
                act.activation(uv[odd, :, 1, :], pairs6(acc[1][odd, 1, 0:PAIRS * C]), ACT.Copy).then_inc(u_out_odd, 1)
                act.wait_ge(o_mm, c + 2)
                for e in range(2):
                    feats = slice(e * HD, (e + 1) * HD)
                    ins = act.activation(zT[feats, :, bass.ds(t0, n)],
                                         pairs6(acc[2 + e][feats, 0, 0:PAIRS * C])[:, :, 0:n], ACT.Copy)
                ins.then_inc(yt_out, 1)

            for n in range(2):
                act.wait_ge(spilled[n], 16 * (RW_EARLY + 3 * KT) // 2)
            with act.Fori(0, NCH) as it:
                chunk(it, C, 5, it * C)
            chunk(NCH, TS, 1, TP)
            def gn_square(i):
                act.wait_ge(gn_diff, PAIRS + i + 1)
                act.activation(kkT[:, 2 + i % 2, :], kkT[:, i % 2, :], ACT.Square).then_inc(gn_sq, 1)

            gn_square(0)
            for i in range(PAIRS):
                act.wait_ge(gn_max, PAIRS + i + 1)
                act.activation(kkT[:, 4, :], kkT[:, 4, :], ACT.Sqrt).then_inc(gn_root, 1)
                if i < PAIRS - 1:
                    gn_square(i + 1)

            def norm(done):
                for j in range(KT):
                    act.wait_ge(x1_added, done + j + 1)
                    if done + j >= 2:
                        act.wait_ge(sqT_summed, done + j - 1)
                    act.activation(sqT[:, j % 2, :], x1T[:, j, :], ACT.Square).then_inc(sqT_made, 1)
                act.wait_ge(rms_in, done // KT + 1)
                act.activation(rms, rms, ACT.Sqrt).then_inc(rms_root, 1)

            norm(0)
            act.sem_inc(gu_act, 2)

            def ff_tile(n, it=None):
                act.wait_ge(slot_used, S_GU + 2 * n + 1 if it is None else it * 20 + S_GU + 2 * n + 1)
                t = n if it is None else it * 10 + n
                act.activation(ffT[:, bass.ds(t, 1), :].rearrange("p a (b t) -> p (a b) t", b=2),
                               acc[n % 2][:, :, 0:HALF_T], ACT.Silu).then_inc(gu_act, 1)

            with act.Fori(0, FFT // 10) as it:
                for n in range(10):
                    ff_tile(n, it)
            for n in range(FFT // 10 * 10, FFT):
                ff_tile(n)
            norm(KT)

        @block.vector
        def _(dve):
            own = Steps(dve, dve_own)
            dve.memset(stat[:], 1.0).then_inc(means, 1)
            dve.wait_ge(squares, 1)
            dve.tensor_scalar(stat[:, 8:15], stat[:, 0:7], 1.0 / D, RMS_EPS, ALU.mult, ALU.add).then_inc(means, 1)
            dve.wait_ge(roots, 1)
            own(dve.reciprocal(stat[:, 8:15], stat[:, 8:15]))
            for i, (rows, *_) in enumerate(NORM):
                dve.tensor_scalar(x_tm[0:rows, i, :], x_tm[0:rows, i, :], stat[0:rows, 8 + i:9 + i], None, ALU.mult)\
                   .then_inc(scaled, 1)
            for i, (rows, t0, dst, gain) in enumerate(NORM):
                dve.wait_ge(turned, i + 1)
                o = acc[i % 2][:].rearrange("p a (k t) -> p (a k) t", t=P)
                dve.tensor_tensor(dst[:, :, t0:t0 + rows], o[:, :, 0:rows], bc(v(gain, 0, KT), 2, rows), ALU.mult)\
                   .then_inc(hT_ready, 1)

            dve.wait_ge(rows_mm, 1)
            for n in range(2):
                dve.tensor_copy(v_tm[:, n, 0:QT, :].rearrange("p t c -> p (t c)"), acc[2 + n][:, 0, :])
                ins = dve.tensor_copy(v_tm[0:TS, n, QT, :], acc[2 + n][0:TS, 1, 0:P])
            ins.then_inc(rows_done, 2)
            dve.wait_ge(rows_mm, 2)
            dve.tensor_copy(mkT[:].rearrange("p h t -> p (h t)"), acc[0][:].rearrange("p a c -> p (a c)"))\
               .then_inc(rows_done, 1)
            own(dve.tensor_scalar(in_all[:, T_Q:T_Q + 6, :], in_all[:, T_Q:T_Q + 6, :], HD ** -0.5, None, ALU.mult))
            dve.tensor_scalar(mqT, mqT, P ** -0.5, None, ALU.mult).then_inc(q_scaled, 1)
            dve.wait_ge(cp_mm, 1)
            dve.wait_ge(cmp_in, 96)
            dve.tensor_tensor(pre_bias[0:HD], acc[1][0:HD, 0, 0:2], b1[0:HD], ALU.add).then_inc(cp_done, 1)
            dve.wait_ge(cp_mm, 2)
            dve.tensor_copy(u_sb, acc[2][:, :, 0:2 * TS].rearrange("p g (k n) -> p g k n", k=2)).then_inc(cp_done, 1)
            dve.wait_ge(cp_mm, 4)
            dve.tensor_copy(kcT[:, 0:NC_P], acc[2][:, 0, 0:NC_P]).then_inc(cp_done, 1)
            dve.tensor_copy(vc[0:NC_P], acc[2][0:NC_P, 1, 0:P]).then_inc(cp_done, 1)
            for u, (g, t) in enumerate(CMP_UNITS):
                dve.wait_ge(cs_mm, u + 1)
                s3 = acc[0][:, 0, 0:HPG * NC_P].rearrange("p (r n) -> p r n", r=HPG)
                own(dve.tensor_reduce(small[:, 0:HPG], s3, AX, ALU.max, negate=True))
                dve.tensor_tensor(c_shift, s3, bc(small[:, 0:HPG], 2, NC_P), ALU.add).then_inc(cs_shift, 1)
                dve.wait_ge(cs_exp, u + 1)
                own(dve.tensor_reduce(small[:, 8:8 + HPG], c_prob, AX, ALU.add))
                own(dve.reciprocal(small[:, 8:8 + HPG], small[:, 8:8 + HPG]))
                own(dve.tensor_tensor(small[:, 16:16 + HPG], small[:, 8:8 + HPG],
                                      gates_tm[:, t, g * 18:g * 18 + 18].rearrange("p (r b) -> p r b", b=3)[:, :, 0],
                                      ALU.mult))
                own(dve.tensor_tensor(c_prob, c_prob, bc(const("cmp01")[:, t * NC_P:(t + 1) * NC_P], 1, HPG), ALU.mult))
                dve.tensor_tensor(c_prob, c_prob, bc(small[:, 16:16 + HPG], 2, NC_P), ALU.mult).then_inc(cs_prob, 1)
                dve.wait_ge(cs_turn, u + 1)
                dve.tensor_copy(c_probT[0:NC_P], acc[1][0:NC_P].rearrange("p a (r t) -> p (a r) t", t=P)[:, 0:HPG, :])\
                   .then_inc(cs_copied, 1)
            dve.wait_ge(cs_o, len(CMP_UNITS))
            dve.sem_inc(at_cs, 1)
            own(dve.memset(q_pad[0][HD:P], 0.0))
            own(dve.memset(q_pad[1][0:HD], 0.0))
            dve.sem_inc(at_o, 2)

            def att_max(it, u):
                g, t = ATT_UNITS[u]
                w = (t + 1) * P
                dve.wait_ge(at_s, it * 8 + u + 1)
                dve.tensor_reduce(small[:, 2 * (u % 2):2 * (u % 2) + 2], acc[u % 2][:, :, 0:w], AX, ALU.max, negate=True)\
                   .then_inc(at_max, 1)

            def att_copy(it, u):
                g, t = ATT_UNITS[u]
                w = (t + 1) * P
                d = 8 + 2 * (u % 2)
                dve.wait_ge(at_turn, it * 8 + u + 1)
                dve.wait_ge(at_pv, it * 8 + u)
                dve.tensor_copy(probsT[:, 0, 0:w], acc[2][:, 0, 0:w]).then_inc(at_cs, 1)
                dve.wait_ge(at_o, it * 8 + u + 1)
                own(dve.reciprocal(small[:, d + 4:d + 6], small[:, d:d + 2]))
                gate = gates_tm[:, t, g * 18:g * 18 + 18].rearrange("p (r b) -> p r b", b=3)[:, bass.ds(it, 1), 1:3]
                own(dve.tensor_tensor(small[:, d + 4:d + 6], small[:, d + 4:d + 6], gate.rearrange("p a b -> p (a b)"),
                                      ALU.mult))

            def att_out(it, u):
                g, t = ATT_UNITS[u]
                d = 8 + 2 * (u % 2)
                o = o_tm[:, t, bass.ds(it, 1), g * HD:(g + 1) * HD].rearrange("p a d -> p (a d)")
                dve.wait_ge(at_pv, it * 8 + u + 1)
                own(dve.scalar_tensor_tensor(o, acc[3][:, u % 2, 0:HD], small[:, d + 4:d + 5], o, ALU.mult, ALU.add))
                dve.scalar_tensor_tensor(o, acc[3][:, u % 2, HD:2 * HD], small[:, d + 5:d + 6], o, ALU.mult, ALU.add)\
                   .then_inc(at_o, 1)

            with dve.Fori(0, HPG) as it:
                own.loop(it, 8 * 3)
                for u in range(8):
                    att_max(it, u)
                    if u >= 1:
                        att_copy(it, u - 1)
                    if u >= 2:
                        att_out(it, u - 2)
                att_out(it, 6)
                att_copy(it, 7)
                att_out(it, 7)
            own.end(HPG)
            def memory_max(t):
                d = 24 + 12 * (t % 2)
                dve.wait_ge(ma_s, MA + t + 1)
                dve.tensor_reduce(small[:, d:d + 4], acc[3 * (t % 2)][:].rearrange("p a (h t) -> p (a h) t", h=2), AX,
                                  ALU.max, negate=True).then_inc(ma_max, 1)

            memory_max(0)
            for t in range(QT):
                if t < QT - 1:
                    memory_max(t + 1)
                d = 24 + 12 * (t % 2)
                dve.wait_ge(ma_exp, MA + t + 1)
                own(dve.reciprocal(small[:, d + 8:d + 12], small[:, d + 4:d + 8]))
                dve.tensor_tensor(m_probs[t % 2], m_probs[t % 2], bc(small[:, d + 8:d + 12], 2, MEM_T), ALU.mult)\
                   .then_inc(ma_prob, 1)
                dve.wait_ge(ma_turn, MA + t + 1)
                if t >= 1:
                    dve.wait_ge(ma_pv, MA + t)
                dve.tensor_copy(m_probT[:].rearrange("p a c -> p (a c)"), acc[1][:].rearrange("p a c -> p (a c)"))\
                   .then_inc(ma_copied, 1)

            dve.wait_ge(sg_mm, 1)
            dve.tensor_copy(grep[:].rearrange("p a c -> p (a c)"), acc[0][:].rearrange("p a c -> p (a c)")[:, 0:18 * TS])\
               .then_inc(sg_done, 1)
            dve.wait_ge(mem_stored, 16)
            dve.memset(q_half, 0.0)
            own(dve.memset(imp, 0.0))
            with dve.Fori(0, 2) as half:
                own.loop(half, 15)
                dve.wait_ge(ss_b, half * 4)
                for g in range(NG):
                    gs = slice(g * HD, (g + 1) * HD)
                    ins = dve.tensor_copy(q_half[gs, g, :, 0:HPG * NQ].rearrange("p b (r q) -> p b r q", q=NQ),
                                          qT[gs, :, bass.ds(TP + half * 16, 16)].rearrange("p r (b q) -> p b r q", q=NQ))
                ins.then_inc(sq_done, 1)
                for b in range(4):
                    n, rows = half * 4 + b, slice(b * 32, (b + 1) * 32)
                    dve.wait_ge(su_mm, n + 1)
                    dve.tensor_copy(u_s, acc[2][:, :, 0:P].rearrange("p g (k n) -> p g k n", k=2)).then_inc(su_done, 1)
                    dve.wait_ge(sk_mm, n + 1)
                    dve.tensor_copy(kc_s[:, 0:NC_S], acc[3][:, 1, 0:NC_S]).then_inc(sk_done, 1)
                    dve.wait_ge(ss_b, n + 1)
                    dve.tensor_copy(scores[rows, :, W0:WIN], acc[2][rows])
                    dve.tensor_copy(scores[rows, :, WN0:S0], acc[3][rows, :, 0:S0 - WN0]).then_inc(ss_dve, 1)
                dve.wait_ge(ss_dve, half * 4 + 4)
                dve.tensor_reduce(small[:, 0:2], scores[:, :, C0:N0], AX, ALU.max, negate=True).then_inc(sx_max, 1)
                lo = SEG["winnew"][0]
                dve.tensor_tensor(scores[:, :, WN0:C0], scores[:, :, WN0:C0],
                                  bc(cst[:, bass.ds(half * TS + lo, TS)], 1, NG), ALU.add)
                dve.tensor_tensor(scores[:, :, W0:W0 + NQ], scores[:, :, W0:W0 + NQ], bc(const("winfirst"), 1, NG), ALU.add)
                lo = SEG["newmask"][0]
                own(dve.tensor_tensor(scores[:, :, N0:S0], scores[:, :, N0:S0],
                                      bc(cst[:, bass.ds(half * TS + lo, TS)], 1, NG), ALU.add))
                dve.tensor_reduce(small[:, 2:4], scores[:, :, W0:C0], AX, ALU.max, negate=True).then_inc(sx_max, 1)
                dve.wait_ge(sx_exp, half * 3 + 1)
                own(dve.reciprocal(small[:, 16:18], small[:, 8:10]))
                dve.tensor_tensor(imp[:, :, 0:NC_S], scores[:, :, C0:N0], bc(small[:, 16:18], 2, NC_S), ALU.mult)\
                   .then_inc(si_in, 1)
                dve.wait_ge(si_mm, half + 1)
                own(dve.tensor_copy(imp[:, :, 65:65 + NC_S], acc[3][:, 1, 0:NG * NC_S].rearrange("p (g n) -> p g n", g=NG)))
                own(dve.tensor_reduce(small[:, 24:56].rearrange("p (g s) -> p g s", g=NG),
                                      imp[:, :, 64:128].rearrange("p g (s n) -> p g s n", n=4), AX, ALU.add))
                blocks = small[:, 24:56].rearrange("p (g s) -> p g s", g=NG)
                own(dve.tensor_tensor(blocks, blocks, imp[:, :, 68:129:4], ALU.add))
                inner = blocks[:, :, 1:15]
                own(dve.tensor_reduce(small[:, 16:18], inner, AX, ALU.min))
                own(dve.tensor_tensor(inner, inner, bc(small[:, 16:18], 2, 14), ALU.is_equal))
                own(dve.tensor_tensor(inner, inner, bc(const("blockno"), 1, NG), ALU.mult))
                own(dve.tensor_reduce(small[:, 16:18], inner, AX, ALU.max))
                own(dve.tensor_tensor(inner, inner, bc(small[:, 16:18], 2, 14), ALU.is_equal))
                own(dve.tensor_scalar(inner, inner, NEG, None, ALU.mult))
                dve.wait_ge(ss_act, half * 4 + 4)
                part = scores[:, :, S0 + HD:S0 + 15 * HD].rearrange("p g (s c) -> p g s c", c=HD)
                own(dve.tensor_tensor(part, part, bc(inner, 3, HD), ALU.add))
                dve.tensor_reduce(small[:, 4:6], scores[:, :, N0:S0 + PAST], AX, ALU.max, negate=True).then_inc(sx_max, 1)
                for g in range(NG):
                    dve.wait_ge(st_mm, half * 2 + g + 1)
                    dve.wait_ge(so_mm, half * 2 + g)
                    dve.tensor_copy(sprobT[:, 0:NPG, :].rearrange("p a c -> p (a c)"),
                                    acc[0][:].rearrange("p a c -> p (a c)")).then_inc(st_dve, 1)
                dve.wait_ge(sx_exp, half * 3 + 3)
                dve.reciprocal(small[:, 56:58], small[:, 8:10])
                dve.reciprocal(small[:, 58:60], small[:, 12:14])
                own(dve.reciprocal(small[:, 60:62], small[:, 10:12]))
                dve.wait_ge(so_mm, half * 2 + 2)
                dve.tensor_tensor(o_rows, acc[2][:, 0, 0:6 * HD].rearrange("p (s d) -> p s d", d=HD),
                                  bc(small[:, 56:62], 2, HD), ALU.mult).then_inc(so_done, 1)
                dve.wait_ge(sf_mm, half + 1)
                g4 = grep.rearrange("p (r s) t -> p r s t", s=3)
                for s_ in range(3):
                    ins = dve.tensor_tensor(
                        o_gated[:, s_, :].rearrange("p (b r q) -> p b r q", r=HPG, q=NQ),
                        acc[3][:, 0, s_ * P:(s_ + 1) * P].rearrange("p (b c) -> p b c", b=4)[:, :, 0:24]
                        .rearrange("p b (r q) -> p b r q", q=NQ),
                        g4[:, :, s_, bass.ds(half * 16, 16)].rearrange("p r (b q) -> p b r q", q=NQ), ALU.mult)
                own(ins)
                own(dve.tensor_tensor(o_gated[:, 0, :], o_gated[:, 0, :], o_gated[:, 1, :], ALU.add))
                f3 = lambda n: o_gated[:, n, :].rearrange("p (b r q) -> p b r q", r=HPG, q=NQ)
                dve.tensor_tensor(onsaT[:, :, bass.ds(TP + half * 16, 16)].rearrange("p r (b q) -> p b r q", q=NQ),
                                  f3(0), f3(2), ALU.add).then_inc(sf_done, 1)
            own.end(2)
            dve.wait_ge(sf_done, 2)
            own(dve.memset(mem_q, 0.0))
            with dve.Fori(0, 2) as half:
                own.loop(half, 1)
                dve.wait_ge(ms_s, MS + half * 4)
                for h in range(MEM_H):
                    ins = dve.tensor_copy(mem_q[:, :, h, h * NQ:(h + 1) * NQ],
                                          mqT[:, h, bass.ds(TP + half * 16, 16)].rearrange("p (b q) -> p b q", q=NQ))
                ins.then_inc(ms_q, 1)
                dve.wait_ge(ms_s, MS + half * 4 + 4)
                dve.tensor_reduce(small[:, 0:1], acc[0][:, 0, 0:MEM_T], AX, ALU.max, negate=True).then_inc(ms_max, 1)
                dve.wait_ge(ms_exp, MS + half + 1)
                own(dve.reciprocal(small[:, 2:3], small[:, 1:2]))
                dve.wait_ge(ms_pv, MS + half + 1)
                dve.tensor_scalar(mem_o, acc[2][:, 0, :], small[:, 2:3], None, ALU.mult).then_inc(ms_norm, 1)
                dve.wait_ge(ms_ft, half + 1)
                for h in range(MEM_H):
                    ins = dve.tensor_copy(omemT[:, h, bass.ds(TP + half * 16, 16)].rearrange("p (b q) -> p b q", q=NQ),
                                          acc[3][:, 0, h * P:(h + 1) * P].rearrange("p (b c) -> p b c", b=4)[:, :, h * NQ:(h + 1) * NQ])
                ins.then_inc(ms_done, 1)
            own.end(2)

            dve.wait_ge(rw_evicted, N_RW + 2)
            dve.wait_ge(re_back, 16)
            dve.tensor_copy(shift_now[:, :, 0], rwT[:, :, TP - 1])
            own(dve.tensor_copy(shift_now[:, :, 1:], rwT[:, :, TP + NQ - 1:T:NQ]))
            dve.sem_inc(shift_taken, 1)
            dve.wait_ge(rw_in, 48)
            dve.wait_ge(shift_in_sem, 1)
            with dve.Fori(0, N_RW) as n:
                own.loop(n, 4)
                x = rwT[:, bass.ds(n, 1), :].rearrange("p a t -> p (a t)")
                s9 = shift9[:, bass.ds(n, 1), :].rearrange("p a t -> p (a t)")
                own(dve.tensor_tensor(delta[:, 1:T], x[:, 0:T - 1], x[:, 1:T], ALU.subtract))
                own(dve.tensor_tensor(delta[:, 0:1], s9[:, 0:1], x[:, 0:1], ALU.subtract))
                own(dve.tensor_tensor(delta[:, TP:T:NQ], s9[:, 1:], x[:, TP:T:NQ], ALU.subtract))
                own(dve.scalar_tensor_tensor(x, delta, vec[:, bass.ds(n + VEC["mu"], 1)], x, ALU.mult, ALU.add))
            own.end(N_RW)
            dve.sem_inc(xm_done, N_RW)
            h2 = lambda a: a.rearrange("p (b t) -> p b t", b=2)
            for i in range(PAIRS):
                own(dve.tensor_scalar(kkT[:, i, :], kT[:, i, :], v("kk", i), None, ALU.mult))
                if i >= 2:
                    dve.wait_ge(kn_mm, i - 1)
                dve.tensor_tensor(tmp[:, 2 + i % 2, :], kkT[:, i, :], kkT[:, i, :], ALU.mult).then_inc(kn_sq, 1)
                dve.wait_ge(kn_mm, i + 1)
                dve.tensor_scalar(h2(tmp[:, 4 + i % 2, :]), acc[3][:, :, 0:HALF_T], 1e-24, None, ALU.max).then_inc(kn_max, 1)
                dve.wait_ge(kn_root, i + 1)
                own(dve.reciprocal(tmp[:, 4 + i % 2, :], tmp[:, 4 + i % 2, :]))
                own(dve.tensor_tensor(kkT[:, i, :], kkT[:, i, :], tmp[:, 4 + i % 2, :], ALU.mult))
            dve.wait_ge(lo_out, 3 * PAIRS)
            for i in range(PAIRS):
                own(dve.tensor_scalar(zT[:, i, :], zT[:, i, :], -float(np.exp(-0.5)), None, ALU.mult))
                own(dve.tensor_tensor_scan(tmp[:, 1, :], const("reset"), zT[:, i, :], 0.0, ALU.mult, ALU.add))
                dve.tensor_tensor(tmp[:, 5, :], tmp[:, 1, :], zT[:, i, :], ALU.subtract).then_inc(ex_in, 1)
                own(dve.tensor_scalar(delta, bT[:, i, :], -1.0, v("ka", i), ALU.add, ALU.mult))
                own(dve.scalar_tensor_tensor(kT[:, i, :], delta, 1.0, kT[:, i, :], ALU.add, ALU.mult))
                dve.scalar_tensor_tensor(tmp[:, 0, :], rT[:, i, :], v("rk", i), kT[:, i, :], ALU.mult, ALU.mult)\
                   .then_inc(bo_in, 1)
                own(dve.tensor_tensor(bT[:, i, :], bT[:, i, :], kkT[:, i, :], ALU.mult))
                dve.wait_ge(bo_in, i + 1)
                dve.wait_ge(ex_out, i + 1)
                dve.tensor_tensor(bT[:, i, :], bT[:, i, :], tmp[:, 3, :], ALU.mult)
                dve.tensor_tensor(kT[:, i, :], kT[:, i, :], tmp[:, 3, :], ALU.mult)
                dve.tensor_tensor(rT[:, i, :], rT[:, i, :], tmp[:, 2, :], ALU.mult)
                dve.tensor_copy(pend[:, i, 0:NCH], tmp[:, 2, C - 1:TP:C])
                dve.tensor_copy(pend[:, i, NCH:], tmp[:, 2, TP + NQ - 1:T:NQ])
                own(dve.scalar_tensor_tensor(zT[:, i, :], kkT[:, i, :], -1.0, tmp[:, 4, :], ALU.mult, ALU.mult))
                dve.wait_ge(bo_mm, i + 1)
                dve.tensor_tensor(h2(bonusT[:, i, :]), acc[3][:, :, 0:HALF_T], h2(vT[:, i, :]), ALU.mult).then_inc(prep_done, 1)
            both = lambda n: acc[n][:].rearrange("p a c -> p (a c)")
            dve.wait_ge(prep_done, PAIRS)
            dve.memset(S, 0.0).then_inc(s_zero, 1)
            dve.wait_ge(s_zero, 1)

            pairs6 = lambda a: a.rearrange("p (i s) -> p i s", s=C)

            def chunk(c, n, levels, kind, before_w):
                sg, st, sx = (SEG[x + kind][0] for x in ("gram_", "tri_", "x2t_"))
                rows = (slice(0, n), slice(n, 2 * n))
                for e in range(2):
                    r = rows[e]
                    dve.wait_ge(gram_mm, c * 2 + e + 1)
                    own(dve.tensor_tensor(gram[0:2 * n, e, :, 0:2 * n],
                                          both(2 * e)[0:2 * n, 0:PAIRS * P].rearrange("p (i s) -> p i s", i=PAIRS)[:, :, 0:2 * n],
                                          bc(cst[0:2 * n, sg:sg + 2 * n], 1, PAIRS), ALU.mult))
                    own(dve.tensor_tensor(gram[r, e, :, 0:n], gram[r, e, :, 0:n], bc(ident[r, r], 1, PAIRS), ALU.add))
                    dve.tensor_tensor(XX[r, :, 1, :, 0:n], gram[r, e, :, 0:n].rearrange("p (s k) c -> p s k c", k=3),
                                      bc(bc(cst[r, sx:sx + n], 1, 3), 1, 2), ALU.mult)\
                       .then_inc(gram_out, 1)
                for l in range(levels):
                    for s_ in range(2):
                        dve.wait_ge(y_mm, c * 10 + 2 * l + s_ + 1)
                        for e in range(2):
                            r = rows[e]
                            ins = dve.tensor_tensor(Y[r, 3 * s_:3 * s_ + 3, 0:n], pairs6(acc[e][r, s_, 0:3 * C])[:, :, 0:n],
                                                    bc(cst[r, st + l * n:st + (l + 1) * n], 1, 3), ALU.mult)
                        ins.then_inc(y_out, 1)
                before_w()
                dve.wait_ge(w_mm, c + 1)
                dve.tensor_copy(w_tm[rows[1]].rearrange("p a c -> p (a c)"), acc[1][rows[1], 0, 0:PAIRS * C])\
                   .then_inc(w_out_odd, 1)
                dve.wait_ge(u_mm, c + 1)
                dve.tensor_copy(uv[0:n, :, 0, :], pairs6(acc[0][0:n, 1, 0:PAIRS * C])).then_inc(u_out, 1)

            with dve.Fori(0, NCH) as it:
                own.loop(it, 5)
                chunk(it, C, 5, "p", lambda: None)
                dve.wait_ge(s_mm, it + 1)
                dve.wait_ge(o_mm, it + 2)
                own(dve.tensor_tensor(S, pairs6(acc[2][:, 1, 0:PAIRS * C]), S, ALU.add))
                dve.tensor_tensor(S, S, bc(pend[:, :, bass.ds(it, 1)].rearrange("p i a -> p (i a)"), 2, C), ALU.mult)\
                   .then_inc(s_out, 1)
            own.end(NCH)
            turn = [0]

            def masked(x):
                for i in range(PAIRS):
                    turn[0] += 1
                    if turn[0] > 2:
                        y_, i_ = divmod(turn[0] - 3, PAIRS)
                        dve.wait_ge(z_used, y_ * (2 * PAIRS - 1) + 2 * i_ + 1)
                    dve.tensor_tensor(z_b[:, turn[0] % 2, :].rearrange("p (b t) -> p b t", b=NB),
                                      bc(zr_now[:, 0, i, x * TS:(x + 1) * TS], 1, NB),
                                      const("zmask").rearrange("p (b t) -> p b t", b=NB), ALU.mult).then_inc(z_masked, 1)

            dve.wait_ge(staged, NCH + 1)
            chunk(NCH, TS, 1, "s", lambda: masked(0))
            masked(1)
            dve.wait_ge(o_mm, NCH + 2)
            for i in range(PAIRS):
                for e in range(2):
                    j = 2 * i + e
                    if j >= 2:
                        dve.wait_ge(uvb_used, j - 1)
                    dve.wait_ge(u_out, NCH + 1)
                    dve.wait_ge(u_out_odd, NCH + 1)
                    dve.tensor_tensor(uv_b[0:2 * TS, j % 2], bc(uv[0:2 * TS, i, e, :], 1, NB),
                                      bc(const("umask", 2 * TS), 2, C), ALU.mult).then_inc(uvb_done, 1)
                dve.wait_ge(uvb_used, 2 * i + 2)
                for e in range(2):
                    rows = slice(e * HD, (e + 1) * HD)
                    own(dve.tensor_tensor(S_out[rows, i], acc[1][rows, 0, :].rearrange("p (b c) -> p b c", b=NB),
                                          S_s[rows, :, i, :], ALU.add))
                    dve.tensor_tensor(S_out[rows, i], S_out[rows, i], bc(pend[rows, i, NCH:], 2, C), ALU.mult)\
                       .then_inc(wkv_done, 1)
            def gn_difference(i):
                dve.wait_ge(gn_mean, PAIRS + i + 1)
                dve.scalar_tensor_tensor(h2(kkT[:, i % 2, :]), acc[0][:, :, 0:HALF_T], -1.0 / HD, h2(zT[:, i, :]),
                                         ALU.mult, ALU.add).then_inc(gn_diff, 1)

            gn_difference(0)
            for i in range(PAIRS):
                y, d = zT[:, i, :], kkT[:, i % 2, :]
                dve.wait_ge(gn_var, 3 * PAIRS + i + 1)
                dve.tensor_scalar(h2(kkT[:, 4, :]), acc[1][:, :, 0:HALF_T], 1.0 / HD, GN_EPS, ALU.mult, ALU.add).then_inc(gn_max, 1)
                if i < PAIRS - 1:
                    gn_difference(i + 1)
                dve.wait_ge(gn_root, PAIRS + i + 1)
                own(dve.reciprocal(kkT[:, 4, :], kkT[:, 4, :]))
                own(dve.tensor_tensor(y, d, kkT[:, 4, :], ALU.mult))
                own(dve.tensor_scalar(y, y, v("lng", i), v("lnb", i), ALU.mult, ALU.add))
                own(dve.tensor_tensor(y, y, bonusT[:, i, :], ALU.add))
                dve.tensor_tensor(y, y, gT[:, i, :], ALU.mult).then_inc(gn_done, 1)

            dve.wait_ge(wkv_stored, 32)
            own(dve.memset(ones, 1.0))
            for m in range(KT):
                half, n = divmod(m, KT // 2)
                dve.wait_ge(sig_in[half], 16)
                for g in range(3):
                    if g < 2:
                        dve.wait_ge(mg_mm, 2 * m + g + 1)
                    else:
                        dve.wait_ge(slot_used, S_MERGE + 2 * m + 2)
                    dst = prod if g else mT[:, m, :]
                    dve.tensor_tensor(h2(dst), acc[(3 * m + g) % 4][:, :, 0:HALF_T],
                                      h2((sig_b if half else sig_a)[:, n, g, :]), ALU.mult).then_inc(mg_part, 1)
                    if g:
                        dve.wait_ge(mg_part, 3 * m + g + 1)
                        own(dve.tensor_tensor(mT[:, m, :], mT[:, m, :], prod, ALU.add))
            dve.sem_inc(mg_part, 1)

            def norm(done, gain, dst, count):
                for j in range(KT):
                    count(j)
                    dve.tensor_tensor(h2(x1T[:, j, :]), acc[j % 2][:, :, 0:HALF_T], h2(x1T[:, j, :]), ALU.add)\
                       .then_inc(x1_added, 1)
                dve.wait_ge(sqT_summed, done + KT)
                dve.tensor_scalar(h2(rms), acc[3][:, :, 0:HALF_T], 1.0 / D, RMS_EPS, ALU.mult, ALU.add)\
                   .then_inc(rms_in, 1)
                dve.wait_ge(rms_root, done // KT + 1)
                own(dve.reciprocal(rms, rms))
                for j in range(KT):
                    dve.scalar_tensor_tensor(dst[:, j, :], x1T[:, j, :], v(gain, j), rms, ALU.mult, ALU.mult)\
                       .then_inc(hf_done, 1)

            dve.wait_ge(xT_in, 16)
            norm(0, "ffn", hT, lambda j: dve.wait_ge(slot_used, S_OUT + j + 1))
            dve.sem_inc(ff_done, 2)

            def ff_tile(n, it=None):
                dve.wait_ge(slot_used, S_GU + 2 * n + 2 if it is None else it * 20 + S_GU + 2 * n + 2)
                dve.wait_ge(gu_act, n + 3 if it is None else it * 10 + n + 3)
                t = n if it is None else it * 10 + n
                f = ffT[:, bass.ds(t, 1), :].rearrange("p a (b t) -> p (a b) t", b=2)
                dve.tensor_tensor(f, acc[2 + n % 2][:, :, 0:HALF_T], f, ALU.mult).then_inc(ff_done, 1)

            with dve.Fori(0, FFT // 10) as it:
                for n in range(10):
                    ff_tile(n, it)
            for n in range(FFT // 10 * 10, FFT):
                ff_tile(n)

            def down(j):
                if j % 4 == 3:
                    dve.wait_ge(slot_used, S_DOWN + FFT * (j + 1) // KT)
                else:
                    dve.wait_ge(dn_mm, j + 1 - (j + 1) // 4)

            norm(KT, "final", x1T, down)


def kernel(**inputs):
    import concourse.bacc as bacc
    from concourse.bass_utils import run_bass_kernel_spmd as run

    nc = bacc.Bacc("TRN2", target_bir_lowering=False, num_devices=1)
    arrays = {name: np.ascontiguousarray(a) for name, a in layout(inputs).items()}
    aps = {name: nc.dram_tensor(name, a.shape, mybir.dt.from_np(a.dtype), kind="ExternalInput").ap()
           for name, a in arrays.items()}
    for name, shape in OUTS.items():
        aps[name] = nc.dram_tensor(name, shape, F32, kind="ExternalOutput").ap()
    program(nc, aps)
    r = run(nc, [arrays], core_ids=[0])
    return results({name: r.results[0][name] for name in OUTS})
```
